# Optimizing a Trainium2 kernel written in Bass

```python
import math, functools
import jax, jax.numpy as jnp
from jax import lax
import numpy as np

D_MODEL = 1024
BATCH = 1
SEQ = 512
DEPTH = 2
DEC_BATCH = 8
DEC_SEQ = 8
PAST_LEN = 4096
PAGE_SIZE = 128

F32 = jnp.float32
EPS = 1e-6
N_EVEN = (DEPTH + 1) // 2
N_ODD = DEPTH // 2
D_FF = 4 * D_MODEL

POOL_WINDOWS = (2, 4, 8, 16)
POOL_GROUPS = len(POOL_WINDOWS)
POOL_GROUP_DIM = D_MODEL // 16
POOL_DIM = POOL_GROUPS * POOL_GROUP_DIM
POOL_HIST = max(POOL_WINDOWS) - 1

FOX_HEAD_DIM = 64
FOX_HEADS = (D_MODEL - POOL_DIM) // FOX_HEAD_DIM
FOX_DIM = FOX_HEADS * FOX_HEAD_DIM
Q_BLOCK = 128
FORGET_BIAS = 3.0
CACHE_FORGET_BIAS = 9.0

EV_Q = POOL_DIM
EV_K = EV_Q + FOX_DIM
EV_V = EV_K + FOX_DIM
EV_F = EV_V + FOX_DIM
EV_TOTAL = EV_F + FOX_HEADS

GMLP_CHUNK = 128
GMLP_GROUPS = 4
GMLP_DIM = D_MODEL // 2
GMLP_GROUP_DIM = GMLP_DIM // GMLP_GROUPS

RET_HEADS = 4
RET_DIM = D_MODEL - GMLP_DIM
RET_HEAD_DIM = RET_DIM // RET_HEADS
RET_CHUNK = 128
ROPE_BASE = 10000.0

OD_V = GMLP_DIM
OD_Q = 2 * GMLP_DIM
OD_K = OD_Q + RET_DIM
OD_RV = OD_K + RET_DIM
OD_G = OD_RV + RET_DIM
OD_TOTAL = OD_G + RET_DIM

kernel_name = 'hybrid_pool_fox_gmlp_retention_step'

def rmsnorm(x, g):
    xf = x.astype(F32)
    y = xf * lax.rsqrt(jnp.mean(xf * xf, axis=-1, keepdims=True) + EPS)
    return (y * g.astype(F32)).astype(x.dtype)

def squared_relu_mlp(x, w_up, w_down):
    h = jax.nn.relu(x @ w_up)
    return (h * h) @ w_down

def pool_mix(a, hist, start_pos, pool_w, pool_scale):
    b, t, _ = a.shape
    af = a.astype(F32)
    ext = jnp.concatenate([hist.astype(F32), af], axis=1)
    cs = jnp.concatenate([jnp.zeros((b, 1, POOL_DIM), F32), jnp.cumsum(ext, axis=1)], axis=1)
    end = cs[:, POOL_HIST + 1:]
    pos = start_pos + jnp.arange(t)
    parts = []
    for g, w in enumerate(POOL_WINDOWS):
        sl = slice(g * POOL_GROUP_DIM, (g + 1) * POOL_GROUP_DIM)
        win = end[:, :, sl] - cs[:, POOL_HIST + 1 - w:POOL_HIST + 1 - w + t, sl]
        cnt = jnp.minimum(pos + 1, w).astype(F32)
        parts.append(win / cnt[None, :, None])
    d = (jnp.concatenate(parts, axis=-1) - af).reshape(b, t, POOL_GROUPS, POOL_GROUP_DIM)
    y = jnp.einsum('btgc,gcd->btgd', d, pool_w.astype(F32)).reshape(b, t, POOL_DIM) * pool_scale.astype(F32)
    return y.astype(a.dtype), ext[:, -POOL_HIST:].astype(a.dtype)

def fox_prompt(q, k, v, logf):
    b, s, h, d = q.shape
    scale = d ** -0.5
    cum = jnp.cumsum(logf.astype(F32), axis=1).transpose(0, 2, 1)
    kpos = jnp.arange(s)

    def block(n):
        start = n * Q_BLOCK
        qb = lax.dynamic_slice_in_dim(q, start, Q_BLOCK, axis=1)
        cb = lax.dynamic_slice_in_dim(cum, start, Q_BLOCK, axis=2)
        sc = jnp.einsum('bqhd,bkhd->bhqk', qb, k).astype(F32) * scale
        sc = sc + cb[..., :, None] - cum[..., None, :]
        qpos = start + jnp.arange(Q_BLOCK)
        sc = jnp.where(kpos[None, :] <= qpos[:, None], sc, -jnp.inf)
        p = jax.nn.softmax(sc, axis=-1)
        return jnp.einsum('bhqk,bkhd->bqhd', p.astype(v.dtype), v)

    o = lax.map(block, jnp.arange(s // Q_BLOCK))
    return o.transpose(1, 0, 2, 3, 4).reshape(b, s, h, d)

def fox_sample(k_past, v_past, logf_past, q, k, v, logf):
    t, d = q.shape[1], q.shape[-1]
    n_past = k_past.shape[1]
    scale = d ** -0.5
    lp = logf_past.astype(F32)
    suffix = (lax.cumsum(lp, axis=1, reverse=True) - lp).transpose(0, 2, 1)
    g = jnp.cumsum(logf.astype(F32), axis=1).transpose(0, 2, 1)
    s_past = jnp.einsum('bqhd,bkhd->bhqk', q, k_past).astype(F32) * scale + g[..., :, None] + suffix[..., None, :]
    s_new = jnp.einsum('bqhd,bkhd->bhqk', q, k).astype(F32) * scale + g[..., :, None] - g[..., None, :]
    causal = jnp.arange(t)[None, :] <= jnp.arange(t)[:, None]
    s_new = jnp.where(causal, s_new, -jnp.inf)
    p = jax.nn.softmax(jnp.concatenate([s_past, s_new], axis=-1), axis=-1).astype(v.dtype)
    return (jnp.einsum('bhqk,bkhd->bqhd', p[..., :n_past], v_past)
            + jnp.einsum('bhqk,bkhd->bqhd', p[..., n_past:], v))

def gmlp_mix(u, v, ln_g, ln_b, ws, bs):
    b, t, _ = u.shape
    vf = v.astype(F32)
    mu = jnp.mean(vf, axis=-1, keepdims=True)
    var = jnp.mean((vf - mu) ** 2, axis=-1, keepdims=True)
    vn = (vf - mu) * lax.rsqrt(var + EPS) * ln_g.astype(F32) + ln_b.astype(F32)
    tp = -(-t // GMLP_CHUNK) * GMLP_CHUNK
    vp = jnp.pad(vn, ((0, 0), (0, tp - t), (0, 0))).reshape(b, tp // GMLP_CHUNK, GMLP_CHUNK, GMLP_GROUPS, GMLP_GROUP_DIM)
    ws_c = ws.astype(F32) * jnp.tril(jnp.ones((GMLP_CHUNK, GMLP_CHUNK), F32))
    z = jnp.einsum('gts,bnsgc->bntgc', ws_c, vp) + bs.astype(F32).T[None, None, :, :, None]
    z = z.reshape(b, tp, GMLP_DIM)[:, :t]
    return (u.astype(F32) * z).astype(u.dtype), vn.astype(v.dtype)

def rotary(x, pos):
    half = x.shape[-1] // 2
    inv = ROPE_BASE ** (-jnp.arange(half, dtype=F32) / half)
    ang = pos[:, None] * inv[None, :]
    cos, sin = jnp.cos(ang)[None, :, None, :], jnp.sin(ang)[None, :, None, :]
    x1, x2 = x[..., :half], x[..., half:]
    return jnp.concatenate([x1 * cos - x2 * sin, x1 * sin + x2 * cos], axis=-1)

def retention(q, k, v, s0, start_pos):
    b, t, h, dk = q.shape
    pos = (start_pos + jnp.arange(t)).astype(F32)
    qf = rotary(q.astype(F32), pos)
    kf = rotary(k.astype(F32), pos) * dk ** -0.5
    vf = v.astype(F32)
    lc = math.gcd(t, RET_CHUNK) if t >= RET_CHUNK else t
    n = t // lc
    log_g = jnp.log1p(-jnp.exp2(-5.0 - jnp.arange(h, dtype=F32)))
    idx = jnp.arange(lc, dtype=F32)
    diff = idx[:, None] - idx[None, :]
    decay_intra = jnp.where(diff[None] >= 0, jnp.exp(diff[None] * log_g[:, None, None]), 0.0)
    decay_q = jnp.exp((idx[:, None] + 1.0) * log_g[None, :])
    decay_k = jnp.exp((lc - 1.0 - idx)[:, None] * log_g[None, :])
    decay_s = jnp.exp(lc * log_g)

    def chunk(state, inp):
        qc, kc, vc = inp
        sc = jnp.einsum('blhd,bmhd->bhlm', qc, kc) * decay_intra[None]
        o = (jnp.einsum('bhlm,bmhe->blhe', sc, vc)
             + jnp.einsum('blhd,bhde->blhe', qc, state) * decay_q[None, :, :, None])
        state = state * decay_s[None, :, None, None] + jnp.einsum('bmhd,bmhe->bhde', kc * decay_k[None, :, :, None], vc)
        return state, o

    xs = tuple(a.reshape(b, n, lc, h, a.shape[-1]).swapaxes(0, 1) for a in (qf, kf, vf))
    s_final, o = lax.scan(chunk, s0.astype(F32), xs)
    return o.swapaxes(0, 1).reshape(b, t, h, vf.shape[-1]), s_final

def head_norm(o, g):
    mu = jnp.mean(o, axis=-1, keepdims=True)
    var = jnp.mean((o - mu) ** 2, axis=-1, keepdims=True)
    return (o - mu) * lax.rsqrt(var + EPS) * g.astype(F32).reshape(o.shape[2], o.shape[3])

def even_token_mix(xn, w_in, b_f, pool_w, pool_scale, w_out, hist, start_pos, attend):
    b, t, _ = xn.shape
    proj = xn @ w_in
    a = proj[..., :EV_Q]
    q = proj[..., EV_Q:EV_K].reshape(b, t, FOX_HEADS, FOX_HEAD_DIM)
    k = proj[..., EV_K:EV_V].reshape(b, t, FOX_HEADS, FOX_HEAD_DIM)
    v = proj[..., EV_V:EV_F].reshape(b, t, FOX_HEADS, FOX_HEAD_DIM)
    logf = jax.nn.log_sigmoid((proj[..., EV_F:EV_TOTAL] + b_f).astype(F32))
    pool_out, new_hist = pool_mix(a, hist, start_pos, pool_w, pool_scale)
    att = attend(q, k, v, logf).reshape(b, t, FOX_DIM)
    out = jnp.concatenate([pool_out, att.astype(pool_out.dtype)], axis=-1) @ w_out
    return out, new_hist, k, v, logf.astype(xn.dtype)

def odd_token_mix(xn, w_in, ln_g, ln_b, ws, bs, gn_g, w_out, s0, start_pos):
    b, t, _ = xn.shape
    proj = xn @ w_in
    u = proj[..., :OD_V]
    gv = proj[..., OD_V:OD_Q]
    rq = proj[..., OD_Q:OD_K].reshape(b, t, RET_HEADS, RET_HEAD_DIM)
    rk = proj[..., OD_K:OD_RV].reshape(b, t, RET_HEADS, RET_HEAD_DIM)
    rv = proj[..., OD_RV:OD_G].reshape(b, t, RET_HEADS, RET_HEAD_DIM)
    rg = proj[..., OD_G:OD_TOTAL]
    c_out, vn = gmlp_mix(u, gv, ln_g, ln_b, ws, bs)
    r, s_new = retention(rq, rk, rv, s0, start_pos)
    r = head_norm(r, gn_g).reshape(b, t, RET_DIM) * jax.nn.silu(rg.astype(F32))
    out = jnp.concatenate([c_out, r.astype(c_out.dtype)], axis=-1) @ w_out
    return out, vn, s_new

def setup_inputs(seed: int = 0) -> dict:
    key = jax.random.key(seed)
    ks = jax.random.split(key, 32)
    n_pages = PAST_LEN // PAGE_SIZE
    n_used = DEC_BATCH * n_pages
    n_phys = n_used + n_used // 4

    def nrm(i, shape, scale=1.0):
        return jax.random.normal(ks[i], shape, F32) * scale

    x_prompt = nrm(0, (BATCH, SEQ, D_MODEL))
    x_sample = nrm(1, (DEC_BATCH, DEC_SEQ, D_MODEL))
    state_pool = nrm(2, (N_EVEN, DEC_BATCH, POOL_HIST, POOL_DIM))
    cache_k = nrm(3, (N_EVEN, n_phys, PAGE_SIZE, FOX_HEADS, FOX_HEAD_DIM))
    cache_v = nrm(4, (N_EVEN, n_phys, PAGE_SIZE, FOX_HEADS, FOX_HEAD_DIM))
    cache_logf = jax.nn.log_sigmoid(CACHE_FORGET_BIAS + nrm(5, (N_EVEN, n_phys, PAGE_SIZE, FOX_HEADS), 0.5))
    page_table = jax.random.permutation(ks[6], n_phys)[:n_used].reshape(DEC_BATCH, n_pages).astype(jnp.int32)
    state_ret = nrm(7, (N_ODD, DEC_BATCH, RET_HEADS, RET_HEAD_DIM, RET_HEAD_DIM), 0.5)
    norm_mix = 1.0 + nrm(8, (DEPTH, D_MODEL), 0.1)
    w_in_even = nrm(9, (N_EVEN, D_MODEL, EV_TOTAL), D_MODEL ** -0.5)
    b_forget = FORGET_BIAS + nrm(10, (N_EVEN, FOX_HEADS), 0.5)
    pool_w = nrm(11, (N_EVEN, POOL_GROUPS, POOL_GROUP_DIM, POOL_GROUP_DIM), POOL_GROUP_DIM ** -0.5)
    pool_scale = 1.0 + nrm(12, (N_EVEN, POOL_DIM), 0.1)
    w_out_even = nrm(13, (N_EVEN, D_MODEL, D_MODEL), D_MODEL ** -0.5)
    w_in_odd = nrm(14, (N_ODD, D_MODEL, OD_TOTAL), D_MODEL ** -0.5)
    gmlp_ln_g = 1.0 + nrm(15, (N_ODD, GMLP_DIM), 0.1)
    gmlp_ln_b = nrm(16, (N_ODD, GMLP_DIM), 0.1)
    gmlp_ws = nrm(17, (N_ODD, GMLP_GROUPS, GMLP_CHUNK, GMLP_CHUNK), GMLP_CHUNK ** -0.5)
    gmlp_bs = 1.0 + nrm(18, (N_ODD, GMLP_GROUPS, GMLP_CHUNK), 0.1)
    ret_gn_g = 1.0 + nrm(19, (N_ODD, RET_DIM), 0.1)
    w_out_odd = nrm(20, (N_ODD, D_MODEL, D_MODEL), D_MODEL ** -0.5)
    norm_ffn = 1.0 + nrm(21, (DEPTH, D_MODEL), 0.1)
    w_up = nrm(22, (DEPTH, D_MODEL, D_FF), D_MODEL ** -0.5)
    w_down = nrm(23, (DEPTH, D_FF, D_MODEL), D_FF ** -0.5)
    norm_final = 1.0 + nrm(24, (D_MODEL,), 0.1)
    return {'x_prompt': x_prompt, 'x_sample': x_sample, 'state_pool': state_pool,
            'cache_k': cache_k, 'cache_v': cache_v, 'cache_logf': cache_logf,
            'page_table': page_table, 'state_ret': state_ret, 'norm_mix': norm_mix,
            'w_in_even': w_in_even, 'b_forget': b_forget, 'pool_w': pool_w,
            'pool_scale': pool_scale, 'w_out_even': w_out_even, 'w_in_odd': w_in_odd,
            'gmlp_ln_g': gmlp_ln_g, 'gmlp_ln_b': gmlp_ln_b, 'gmlp_ws': gmlp_ws,
            'gmlp_bs': gmlp_bs, 'ret_gn_g': ret_gn_g, 'w_out_odd': w_out_odd,
            'norm_ffn': norm_ffn, 'w_up': w_up, 'w_down': w_down, 'norm_final': norm_final}

def reference(x_prompt, x_sample, state_pool, cache_k, cache_v, cache_logf, page_table, state_ret,
              norm_mix, w_in_even, b_forget, pool_w, pool_scale, w_out_even, w_in_odd,
              gmlp_ln_g, gmlp_ln_b, gmlp_ws, gmlp_bs, ret_gn_g, w_out_odd,
              norm_ffn, w_up, w_down, norm_final):
    dec_b, n_pages = page_table.shape
    past = n_pages * cache_k.shape[2]

    def gather(pool, j):
        rows = pool[j][page_table]
        return rows.reshape((dec_b, past) + rows.shape[3:])

    def run(x, start_pos, get_hist, get_attend, get_state):
        h = x
        hists, ks, vs, lfs, gvs, rs = [], [], [], [], [], []
        for layer in range(DEPTH):
            j = layer // 2
            xn = rmsnorm(h, norm_mix[layer])
            if layer % 2 == 0:
                out, hist, k, v, lf = even_token_mix(xn, w_in_even[j], b_forget[j], pool_w[j], pool_scale[j],
                                                     w_out_even[j], get_hist(j), start_pos, get_attend(j))
                hists.append(hist)
                ks.append(k)
                vs.append(v)
                lfs.append(lf)
            else:
                out, vn, s_new = odd_token_mix(xn, w_in_odd[j], gmlp_ln_g[j], gmlp_ln_b[j], gmlp_ws[j],
                                               gmlp_bs[j], ret_gn_g[j], w_out_odd[j], get_state(j), start_pos)
                gvs.append(vn)
                rs.append(s_new)
            h = h + out
            h = h + squared_relu_mlp(rmsnorm(h, norm_ffn[layer]), w_up[layer], w_down[layer])
        return (rmsnorm(h, norm_final), jnp.stack(hists), jnp.stack(ks), jnp.stack(vs),
                jnp.stack(lfs), jnp.stack(gvs), jnp.stack(rs))

    b = x_prompt.shape[0]
    y_prompt, pool_p, k_p, v_p, lf_p, _, ret_p = run(
        x_prompt, 0,
        lambda j: jnp.zeros((b, POOL_HIST, POOL_DIM), x_prompt.dtype),
        lambda j: fox_prompt,
        lambda j: jnp.zeros((b, RET_HEADS, RET_HEAD_DIM, RET_HEAD_DIM), F32))
    y_sample, pool_s, k_s, v_s, lf_s, gv_s, ret_s = run(
        x_sample, past,
        lambda j: state_pool[j],
        lambda j: functools.partial(fox_sample, gather(cache_k, j), gather(cache_v, j), gather(cache_logf, j)),
        lambda j: state_ret[j])
    return (y_prompt, y_sample, pool_p, k_p, v_p, lf_p, ret_p, pool_s, k_s, v_s, lf_s, gv_s, ret_s)


_drawn_inputs = setup_inputs


def setup_inputs(seed=0):
    import zlib

    import numpy as np

    out = dict(_drawn_inputs(seed))
    spreads = {}
    factors = {'cache_k': 2.894, 'cache_logf': 8.0}
    for name, (base, spread) in spreads.items():
        noise = np.random.default_rng([zlib.crc32(name.encode()), seed]).standard_normal(out[name].shape)
        drawn = base * np.exp(spread * noise) if base else spread * noise
        out[name] = __import__('jax').numpy.asarray(drawn.astype(out[name].dtype))
    for name, factor in factors.items():
        out[name] = (out[name] * factor).astype(out[name].dtype)
    return out
```

```python
import math
from contextlib import ExitStack

import concourse.bass as bass
import numpy as np
from concourse import mybir

F32 = mybir.dt.float32
I32 = mybir.dt.int32
ALU = mybir.AluOpType
ACT = mybir.ActivationFunctionType
AX = mybir.AxisListType

P = 128
DM, SEQ, NB, NS = 1024, 512, 8, 8
TS = NB * NS
T = SEQ + TS
PAGES, PAGE, NPHYS = 32, 128, 320
FF = 4096
EPS = 1e-6
NEG = -1e30
KD = DM // P
NT = SEQ // P
H, D = 12, 64
HQ = H * NS
FOX = H * D
HB = FOX // P
R, DR = 4, 128
HIST = 15
EXT = HIST + SEQ
UNIT = KD * 512
RING = 8
EV = 2572

EV_Q, EV_K, EV_V = 2, 8, 14
OD_U, OD_GV, OD_RQ, OD_RK, OD_RV, OD_RG = 0, 4, 8, 12, 16, 20

PARAMS = [("norm_mix", 16), ("norm_ffn", 16), ("norm_final", 8), ("pool_scale", 2), ("gmlp_ln_g", 4),
          ("gmlp_ln_b", 4), ("ret_gn_g", 4)]
PROW = {}
for _n, _k in PARAMS:
    PROW[_n] = sum(k for _, k in PARAMS[:len(PROW)])
NPARAM = sum(k for _, k in PARAMS)

STAGES = [("x", KD), ("norm0", 1), ("in0", 20), ("logf", 1), ("logfT", 1), ("cum", 1), ("cumT", 1), ("sfxT", 12),
          ("sfx", 6), ("knat", 5), ("vnat", 5), ("gq", 2), ("snew", 1),
          ("hist", 2), ("out0", 8), ("norm1", 1), ("up0", 32), ("down0", 8),
          ("norm2", 1), ("in1", 24), ("wst", 1), ("w8", 1), ("mu", 1), ("var", 1), ("vnat1", 5), ("z", 4),
          ("rot", 8), ("kn", 5), ("vn", 5), ("ret", 16), ("hmu", 4), ("hvar", 4),
          ("out1", 8), ("norm3", 1), ("up1", 32), ("down1", 8), ("norm4", 1), ("y", 5)]
FIRST = {}
_at = 0
for _n, _k in STAGES:
    FIRST[_n] = _at
    _at += _k

BY_SCALAR = {"norm0", "in0", "cum", "cumT", "sfxT", "sfx", "norm1", "up0", "norm2", "in1", "mu", "var", "vn", "hmu",
             "hvar", "norm3", "up1", "norm4"}
OWNER = []
for _n, _k in STAGES:
    OWNER += ["scalar" if _n in BY_SCALAR or (_n == "ret" and _j % 4 == 3) else "vector" for _j in range(_k)]


def emptied_by(owner, n):
    return sum(o == owner for o in OWNER[:n])


WEIGHTS = [("in0", 5, 4), ("out0", 2, 4), ("up0", 8, 4), ("down0", 8, 1),
           ("in1", 6, 4), ("out1", 2, 4), ("up1", 8, 4), ("down1", 8, 1)]
UFIRST = {}
_at = 0
for _n, _k, _b in WEIGHTS:
    UFIRST[_n] = _at
    _at += _k


def tables():
    p, f = np.arange(P)[:, None], np.arange(P)[None, :]
    q, g = np.arange(TS)[:, None], np.arange(TS)[None, :]
    same = q // NS == g // NS
    one = lambda m: m.astype(np.float32)
    w = np.array([[2, 8], [4, 16]])[(np.arange(P) >= 64).astype(int)]
    cnt = np.minimum(np.arange(16)[None, None, :] + 1, w[:, :, None])
    even = {
        "ident": one(p == f),
        "ones": np.ones((P, P), np.float32),
        "upto": np.concatenate([one(p <= f), np.ones((P, SEQ - P), np.float32)], 1),
        "mask": np.where(f <= p, 0.0, NEG).astype(np.float32),
        "later": one(p > f),
        "later_page": one((p // PAGES == f // PAGES) & (p > f)),
        "upto_s": one(same & (q <= g)),
        "mask_s": np.where(same & (q <= g), 0.0, NEG).astype(np.float32),
        "inv_cnt": (1.0 / cnt).astype(np.float32).reshape(P, 32),
        "inv_w": (1.0 / w).astype(np.float32),
    }
    half = DR // 2
    inv = (np.float32(10000.0) ** (-np.arange(half, dtype=np.float32) / np.float32(half))).astype(np.float32)
    pos = np.concatenate([np.arange(SEQ), np.tile(PAGES * PAGE + np.arange(NS), NB)]).astype(np.float32)
    ang = (pos[None, :] * np.concatenate([inv, inv])[:, None]).astype(np.float32)
    lg = np.log1p(-np.exp2(-5.0 - np.arange(R))).astype(np.float32).astype(np.float64)
    dec = lambda n, gap, keep: np.where(keep, np.exp(np.where(keep, gap, 0) * lg[n]), 0.0)
    odd = {
        "cos": np.cos(ang.astype(np.float64)).astype(np.float32),
        "sin": np.sin(ang.astype(np.float64)).astype(np.float32),
        "swap": one(f == p + half) - one(p == f + half),
        "dec": np.concatenate([dec(n, f - p, f >= p) for n in range(R)], 1).astype(np.float32),
        "dec_s": np.concatenate([dec(n, g - q, same & (g >= q)) for n in range(R)], 1).astype(np.float32),
        "dec_q": np.concatenate([np.exp((f + 1) * lg[n]) + 0 * p for n in range(R)], 1).astype(np.float32),
        "dec_k": np.stack([np.exp((P - 1 - np.arange(P)) * lg[n]) for n in range(R)], 1).astype(np.float32),
        "dec_ks": np.stack([np.exp((NS - 1 - np.arange(TS) % NS) * lg[n]) for n in range(R)], 1).astype(np.float32),
        "same_s": one(same),
        "rep": one(np.arange(NS)[:, None] == np.arange(TS)[None, :] % NS),
        "of_seq": one(np.arange(TS)[:, None] // NS == np.arange(NB)[None, :]),
    }
    step = [math.exp(P * float(x)) for x in lg], [math.exp(NS * float(x)) for x in lg]

    def pack(parts):
        width = sum(a.shape[1] for a in parts.values())
        out, at, where = np.zeros((P, width), np.float32), 0, {}
        for name, a in parts.items():
            out[:a.shape[0], at:at + a.shape[1]] = a
            where[name] = (a.shape[0], at, a.shape[1])
            at += a.shape[1]
        return out, where

    return pack(even), pack(odd), step


class Steps:

    def __init__(self, eng, sem):
        self.eng, self.sem, self.n, self.more = eng, sem, 0, 0

    def __call__(self, ins):
        ins.then_inc(self.sem, 1)
        self.n += 1
        self.eng.wait_ge(self.sem, self.n + self.more)

    def loop(self, i, per):
        self.more, self.per, self.start = i * per, per, self.n

    def end(self, times):
        assert self.n - self.start == self.per, (self.n - self.start, self.per)
        self.n, self.more = self.start + self.per * times, 0


def hybrid_step(nc, I, O, where0, where1, decay_step):
    ctx = ExitStack()
    with ctx:
        def sb(name, shape, dt=F32):
            return ctx.enter_context(nc.sbuf_tensor(name, shape, dt))

        sems = {}

        def sem(name):
            if name not in sems:
                sems[name] = ctx.enter_context(nc.semaphore(name))
            return sems[name]

        h = sb("h", [P, KD, T])
        xn = sb("xn", [P, KD, T])
        big = sb("big", [P, 32, T])
        wring = sb("wring", [P, 2, UNIT])
        work = sb("work", [P, RING * FOX + 2 * 33 * HQ])
        c0 = sb("c0", [P, I["tab0"].shape[1]])
        prow = sb("prow", [NPARAM, P])
        pcol = sb("pcol", [P, NPARAM])
        rstd = sb("rstd", [P, T])
        cumT = sb("cumT", [H, T])
        cumn = sb("cumn", [P, (NT + 1) * H])
        lfn = sb("lfn", [P, (NT + 1) * H])
        ptab = sb("ptab", [1, NB * PAGES], I32)
        pidx = sb("pidx", [P, 2], I32)
        wf = sb("wf", [P, KD, H])
        bf = sb("bf", [H, 1])
        pwd = sb("pwd", [P, 2, P])
        small = sb("small", [P, 5 * HQ])
        hstat = sb("hstat", [P, 6 * 4 + 8])
        ps = ctx.enter_context(nc.psum_tensor("ps", [P, 8, 512], F32))

        bigf = big[:, :, :].rearrange("p a t -> p (a t)")
        xnf = xn[:, :, :].rearrange("p a t -> p (a t)")

        def cst(name, lo=0, hi=None, rows=None):
            r, at, w = where0[name]
            return c0[0:rows or r, at + lo:at + (w if hi is None else hi)]

        ident = cst("ident")

        def param(name, j, rows=P):
            return pcol[0:rows, PROW[name] + j:PROW[name] + j + 1]

        def slot(name, j=0):
            return (FIRST[name] + j) % 4

        def bankA(s, n=512, rows=P):
            return ps[0:rows, 2 * s, 0:n]

        def bankB(s, n=TS, rows=P):
            return ps[0:rows, 2 * s + 1, 0:n]

        xstage = bigf[:, 0:NT * DM].rearrange("p (t n) -> p t n", t=NT)
        xstage_s = bigf[0:TS, NT * DM:(NT + 1) * DM]
        at0 = 20 * T
        sfx = bigf[:, at0:at0 + NB * PAGES * H]
        vs = bigf[:, at0 + 3072:at0 + 3840]
        gq = bigf[:, at0 + 3840:at0 + 4608].rearrange("p (h t) -> p h t", h=H)
        qblk = bigf[:, at0 + 4608:at0 + 5376].rearrange("p (b c) -> p b c", b=NB)
        snew = bigf[0:TS, at0 + 5376:at0 + 6144].rearrange("p (h t) -> p h t", h=H)
        kmask = bigf[0:TS, at0 + 6144:at0 + 6912].rearrange("p (h t) -> p h t", h=H)
        at1 = EV_V * T
        kT = bigf[:, at1:at1 + 2 * FOX].rearrange("p (s n) -> p s n", s=2)
        es = [bigf[:, at1 + 1536 + 368 * n:at1 + 1536 + 368 * (n + 1)].rearrange("p (a b t) -> p a b t", a=2, b=NB)
              for n in range(2)]
        hstage = bigf[0:NB * HIST, at1 + 2272:at1 + 2528]
        hcopy = bigf[:, at1 + 2528:at1 + 2768].rearrange("p (a t) -> p a t", a=2)
        hout = bigf[0:NB * HIST, at1 + 2768:at1 + 3024]
        hout_p = bigf[0:HIST, at1 + 3024:at1 + 3280]
        ring = work[:, 0:RING * FOX].rearrange("p (s n) -> p s n", s=RING)
        W1 = RING * FOX
        W2 = W1 + 33 * HQ
        S = work[:, W1:W2].rearrange("p (g c) -> p g c", g=33)
        E = work[:, W2:W2 + 33 * HQ].rearrange("p (g c) -> p g c", g=33)
        lg = work[:, 0:3072].rearrange("p (a s h) -> p a s h", a=2, h=H)
        kstage = work[:, 3072:4608].rearrange("p (s n) -> p s n", s=2)
        lT = xnf[:, 0:3072].rearrange("p (a h g) -> p a h g", a=2, h=H)
        lcT = work[:, W1:W1 + 3072].rearrange("p (a h g) -> p a h g", a=2, h=H)
        z = [work[0:H, W2 + T * n:W2 + T * (n + 1)] for n in range(4)]
        vn0 = work[:, W2:W2 + NT * FOX].rearrange("p (t n) -> p t n", t=NT)
        tb = work[:, W1:W1 + 1024].rearrange("p (s n) -> p s n", s=2)
        ep = [work[:, W1 + 1024:W1 + 1024 + 2 * EXT].rearrange("p (a t) -> p a t", a=2),
              bigf[:, at1:at1 + 2 * EXT].rearrange("p (a t) -> p a t", a=2)]
        eb = work[:, 0:1024].rearrange("p (s n) -> p s n", s=2)
        pT = work[:, 1024:5120].rearrange("p (s j n) -> p s j n", s=2, j=NT)
        ckb = work[:, 5120:6144].rearrange("p (s n) -> p s n", s=2)
        mxr, br, rsum, rden, gcols = (small[:, HQ * n:HQ * (n + 1)] for n in range(5))
        c1 = work[:, 0:I["tab1"].shape[1]]
        O1 = I["tab1"].shape[1]

        def cst1(name, lo=0, hi=None, rows=None):
            r, at, w = where1[name]
            return c1[0:rows or r, at + lo:at + (w if hi is None else hi)]

        def take(n):
            nonlocal O1
            O1 += n
            assert O1 <= RING * FOX + 2 * 33 * HQ
            return work[:, O1 - n:O1]

        wsn = take(512).rearrange("p (g s) -> p g s", g=4)
        vnn = take(2560).rearrange("p (t n) -> p t n", t=NT + 1)
        vmask = vnn.rearrange("p t n -> p (t n)")[0:TS, 0:1024].rearrange("p (b e) -> p b e", b=NB)
        s_out = vnn.rearrange("p t n -> p (t n)")[:, 1024:2048].rearrange("p (b e) -> p b e", b=NB)
        kn = take(2560).rearrange("p (t n) -> p t n", t=NT + 1)
        v2 = take(2560).rearrange("p (t n) -> p t n", t=NT + 1)
        sct = take(T)
        st = bigf[:, 24 * T + 4096:24 * T + 4608].rearrange("p (n e) -> p n e", n=NT)
        s0 = bigf[:, 24 * T:24 * T + 4096].rearrange("p (h b e) -> p h b e", h=R, b=NB)
        wT = take(512).rearrange("p (g t) -> p g t", g=4)
        w8 = take(256)[0:TS, :].rearrange("p (g t) -> p g t", g=4)
        bsr = cumT[0:1, 0:512]
        tmp = sct
        ystage = bigf[:, 0:2 * DM].rearrange("p (s n) -> p s n", s=2)

        block_in = sem("block_filled")
        out_of = {"scalar": sem("emptied_by_scalar"), "vector": sem("emptied_by_vector")}

        def wait_emptied(eng, n):
            eng.wait_ge(out_of[OWNER[n - 1]], emptied_by(OWNER[n - 1], n))

        w_in = [sem("weights_in_0"), sem("weights_in_1")]
        page_in = [sem(f"page_in_{n}") for n in range(RING)]

        blk = ctx.enter_context(nc.Block())

        @blk.sync
        def _(sp):
            sp.dma_start(xstage, I["x_prompt"][0].rearrange("(t p) n -> p t n", p=P)).then_inc(sem("x_in"), 16)
            sp.dma_start(xstage_s, I["x_sample"].rearrange("b s n -> (b s) n")).then_inc(sem("x_in"), 16)
            sp.dma_start(ptab[:, :], I["page_table"].rearrange("b g -> (b g)").rearrange("(o n) -> o n", o=1))\
                .then_inc(sem("ptab_in"), 16)

            def unit(stage, j):
                u = UFIRST[stage] + j
                if u >= 2:
                    for name, n, per in WEIGHTS:
                        if UFIRST[name] <= u - 2 < UFIRST[name] + n:
                            sp.wait_ge(block_in, FIRST[name] + (u - 2 - UFIRST[name] + 1) * per)
                layer = int(stage[-1])
                if stage[:-1] == "down":
                    src = I["w_down"][layer, :, j * P:(j + 1) * P].rearrange("(k p) n -> p k n", p=P)
                    dst = wring[:, u % 2, :].rearrange("p (k n) -> p k n", n=P)
                else:
                    w = {"in0": I["w_in_even"][0], "out0": I["w_out_even"][0], "in1": I["w_in_odd"][0],
                         "out1": I["w_out_odd"][0], "up0": I["w_up"][0], "up1": I["w_up"][1]}[stage]
                    src = w[:, j * 512:(j + 1) * 512].rearrange("(k p) n -> p k n", p=P)
                    dst = wring[:, u % 2, :].rearrange("p (k n) -> p k n", n=512)
                sp.dma_start(dst, src).then_inc(w_in[u % 2], 16)

            for j in range(5):
                unit("in0", j)
            unit("out0", 0)
            unit("out0", 1)

            sp.wait_ge(sem("ptab_in"), 16)
            sp.wait_ge(sem("fox_prompt_done"), H)

            def page(cache, b, p, used, count):
                if used is not None:
                    sp.wait_ge(used, count)
                v = sp.value_load(ptab[0:1, bass.ds(b * PAGES + p, 1)], min_val=0, max_val=NPHYS - 1)
                sp.dma_start(ring[:, p % RING, :], I[cache][0, bass.ds(v, 1)].rearrange("o p h d -> (o p) (h d)"))\
                    .then_inc(page_in[p % RING], 16)

            k_used, v_used = sem("k_page_used"), sem("v_page_used")
            for p in range(PAGES):
                page("cache_k", 0, p, k_used if p >= RING else None, p - RING + 1)
            for p in range(PAGES):
                page("cache_k", 1, p, k_used, PAGES + p - RING + 1)
            for p in range(PAGES):
                if p < RING:
                    page("cache_v", 0, p, k_used, 2 * PAGES + p - RING + 1)
                else:
                    page("cache_v", 0, p, v_used, p - RING + 1)
            with sp.Fori(1, NB - 1) as b:
                for p in range(PAGES):
                    if p < RING:
                        page("cache_k", b + 1, p, v_used, b * PAGES + p - RING + 1)
                    else:
                        page("cache_k", b + 1, p, k_used, (b + 1) * PAGES + p - RING + 1)
                for p in range(PAGES):
                    if p < RING:
                        page("cache_v", b, p, k_used, (b + 2) * PAGES + p - RING + 1)
                    else:
                        page("cache_v", b, p, v_used, b * PAGES + p - RING + 1)
            for p in range(PAGES):
                page("cache_v", NB - 1, p, v_used, (NB - 1) * PAGES + p - RING + 1)

            for name, n, _ in WEIGHTS[2:]:
                for j in range(n):
                    unit(name, j)

        @blk.gpsimd
        def _(pool):
            own = Steps(pool, sem("pool_steps"))
            pool.dma_start(c0[:, :], I["tab0"]).then_inc(sem("tab0_in"), 16)
            for name, n in PARAMS:
                src = I[name]
                while len(src.shape) > 1:
                    src = src.rearrange("a b -> (a b)")
                pool.dma_start(prow[PROW[name]:PROW[name] + n, :], src.rearrange("(r c) -> r c", c=P))\
                    .then_inc(sem("params_in"), 16)
            pool.dma_start(wf[:, :, :], I["w_in_even"][0, :, EV - H:EV].rearrange("(k p) n -> p k n", p=P))\
                .then_inc(sem("wf_in"), 16)
            pool.dma_start(bf[:, :], I["b_forget"].rearrange("o h -> h o")).then_inc(sem("wf_in"), 16)
            for a in range(2):
                rows = I["page_table"][4 * a:4 * a + 4, :].rearrange("b g -> (b g)").rearrange("(n o) -> n o", o=1)
                pool.dma_start(pidx[:, a:a + 1], rows).then_inc(sem("pidx_in"), 16)
            own(pool.memset(pwd[:, :, :], 0.0))
            for g in range(4):
                r = slice(64 * (g % 2), 64 * (g % 2) + 64)
                pool.dma_start(pwd[r, g // 2, r], I["pool_w"][0, g]).then_inc(sem("pwd_in"), 16)
            pool.wait_ge(sem("pidx_in"), 32)
            flat = I["cache_logf"][0].rearrange("n s h -> n (s h)")
            for a in range(2):
                pool.indirect_dma_start(lg[:, a].rearrange("p s h -> p (s h)"), None, flat,
                                        bass.IndirectOffsetOnAxis(ap=pidx[:, a:a + 1], axis=0))\
                    .then_inc(sem("lg_in"), 16)

            pool.wait_ge(sem("lfn_ready"), 1)
            pool.dma_start(O["logf_prompt"][0, 0].rearrange("(t p) h -> p t h", p=P),
                           lfn[:, 0:NT * H].rearrange("p (t h) -> p t h", h=H)).then_inc(sem("stored"), 16)
            pool.dma_start(O["logf_sample"][0].rearrange("b s h -> (b s) h"), lfn[0:TS, NT * H:(NT + 1) * H])\
                .then_inc(sem("stored"), 16)
            kp = O["k_prompt"][0, 0].rearrange("(t p) h d -> t p (h d)", p=P)
            for t in range(NT + 1):
                wait_emptied(pool, FIRST["knat"] + t + 1)
                dst = kp[t] if t < NT else O["k_sample"][0].rearrange("b s h d -> (b s) (h d)")
                pool.dma_start(dst, kstage[0:P if t < NT else TS, t % 2, :]).then_inc(sem(f"k_stored_{t % 2}"), 16)
            wait_emptied(pool, FIRST["vnat"] + NT)
            pool.dma_start(O["v_prompt"][0, 0].rearrange("(t p) h d -> p t (h d)", p=P), vn0)\
                .then_inc(sem("v_stored"), 16)
            wait_emptied(pool, FIRST["vnat"] + NT + 1)
            pool.dma_start(O["v_sample"][0].rearrange("b s h d -> (b s) (h d)"), vs[0:TS, :])\
                .then_inc(sem("v_stored"), 16)
            pool.dma_start(hstage, I["state_pool"][0].rearrange("b t c -> (b t) c")).then_inc(sem("hist_in"), 16)

            own(pool.memset(ep[0][:, :, 0:HIST], 0.0))
            own(pool.tensor_copy(ep[0][:, :, HIST:EXT], big[:, 0:2, 0:SEQ]))
            add = lambda o, a, b: own(pool.tensor_tensor(o, a, b, ALU.add))

            def group(src, rows, a):
                inv = cst("inv_w", a, a + 1)[rows, :]
                dst = xn[rows, a, 0:SEQ]
                own(pool.tensor_scalar(dst, src[rows, a, HIST:EXT], inv, None, ALU.mult))
                own(pool.tensor_tensor(xn[rows, a, 0:16], src[rows, a, HIST:HIST + 16],
                                       cst("inv_cnt", 16 * a, 16 * a + 16)[rows, :], ALU.mult))
                own(pool.tensor_tensor(dst, dst, big[rows, a, 0:SEQ], ALU.subtract))

            def group_s(src, rows, a):
                inv = cst("inv_w", a, a + 1)[rows, :]
                dst = xn[rows, a, SEQ:T].rearrange("p (b s) -> p b s", b=NB)
                own(pool.tensor_scalar(dst, src[rows, a, :, HIST:HIST + NS], inv, None, ALU.mult))
                own(pool.tensor_tensor(dst, dst, big[rows, a, SEQ:T].rearrange("p (b s) -> p b s", b=NB),
                                       ALU.subtract))

            lo, hi = slice(0, 64), slice(64, 128)
            e, f = ep
            add(f[:, :, 1:EXT], e[:, :, 1:EXT], e[:, :, 0:EXT - 1])
            group(f, lo, 0)
            add(e[:, :, 3:EXT], f[:, :, 3:EXT], f[:, :, 1:EXT - 2])
            group(e, hi, 0)
            add(f[:, 1, 7:EXT], e[:, 1, 7:EXT], e[:, 1, 3:EXT - 4])
            group(f, lo, 1)
            add(e[:, 1, 15:EXT], f[:, 1, 15:EXT], f[:, 1, 7:EXT - 8])
            group(e, hi, 1)
            pool.wait_ge(sem("ext_s_ready"), 2)
            e, f = es
            N = HIST + NS
            add(f[:, :, :, 1:N], e[:, :, :, 1:N], e[:, :, :, 0:N - 1])
            group_s(f, lo, 0)
            add(e[:, :, :, 3:N], f[:, :, :, 3:N], f[:, :, :, 1:N - 2])
            group_s(e, hi, 0)
            add(f[:, 1, :, 7:N], e[:, 1, :, 7:N], e[:, 1, :, 3:N - 4])
            group_s(f, lo, 1)
            add(e[:, 1, :, 15:N], f[:, 1, :, 15:N], f[:, 1, :, 7:N - 8])
            group_s(e, hi, 1)
            own(pool.memset(hstat[0:1, 24:25], 0.0))
            pool.memset(hstat[0:1, 25:26], 0.0).then_inc(sem("pool_d_ready"), 1)
            pool.wait_ge(sem("hist_out_ready"), 1)
            pool.dma_start(O["pool_sample"][0].rearrange("b t c -> (b t) c"), hout).then_inc(sem("stored"), 16)
            pool.dma_start(O["pool_prompt"][0, 0], hout_p).then_inc(sem("stored"), 16)

            pool.wait_ge(sem("fox_sample_done"), NB)
            pool.wait_ge(sem("v_stored"), 32)
            pool.dma_start(c1, I["tab1"]).then_inc(sem("tab1_in"), 16)
            pool.dma_start(bsr, I["gmlp_bs"].rearrange("o g t -> o (g t)")).then_inc(sem("bs_in"), 16)
            pool.dma_start(wsn, I["gmlp_ws"][0].rearrange("g t s -> t g s")).then_inc(sem("ws_in"), 16)
            pool.wait_ge(block_in, FIRST["down0"] + 8)
            for n in range(R):
                pool.dma_start(s0[:, n], I["state_ret"][0, :, n].rearrange("b d e -> d b e")).then_inc(sem("s0_in"), 16)
            wait_emptied(pool, FIRST["vnat1"] + NT + 1)
            pool.dma_start(O["gmlp_v_sample"][0].rearrange("b s c -> (b s) c"), vnn[0:TS, NT, :])\
                .then_inc(sem("gv_stored"), 16)
            for n in range(R):
                pool.wait_ge(sem("ret_state_ready"), n + 1)
                pool.dma_start(O["ret_prompt"][0, 0, n], st[:, NT - 1, :]).then_inc(sem("ret_stored"), 16)
                pool.dma_start(O["ret_sample"][0, :, n].rearrange("b d e -> d b e"), s_out)\
                    .then_inc(sem("ret_stored"), 16)
            yp = O["y_prompt"][0].rearrange("(t p) n -> t p n", p=P)
            for t in range(NT + 1):
                wait_emptied(pool, FIRST["y"] + t + 1)
                dst = yp[t] if t < NT else O["y_sample"].rearrange("b s n -> (b s) n")
                pool.dma_start(dst, ystage[0:P if t < NT else TS, t % 2, :]).then_inc(sem(f"y_stored_{t % 2}"), 16)
            pool.wait_ge(sem("stored"), 64)
            pool.wait_ge(sem("k_stored_0"), 48)
            pool.wait_ge(sem("k_stored_1"), 32)
            pool.wait_ge(sem("gv_stored"), 16)
            pool.wait_ge(sem("ret_stored"), 32 * R)
            pool.wait_ge(sem("y_stored_0"), 48)
            pool.wait_ge(sem("y_stored_1"), 32)

        @blk.tensor
        def _(pe):
            mm = nc.tensor.matmul
            tr = nc.tensor.transpose

            def open_block(n):
                if n >= 4:
                    wait_emptied(pe, n - 3)

            def gemm(stage, rhs, ready=None):
                _, units, per = next(w for w in WEIGHTS if w[0] == stage)
                ks = UNIT // (512 if per == 4 else P)
                body = 2 if per == 4 else 4

                def unit(j, i, first=False):
                    u = UFIRST[stage] + j
                    pe.wait_ge(w_in[u % 2], 16 * (u // 2 + 1) + i * (16 * body // 2))
                    for m in range(per):
                        n = j * per + m
                        s = slot(stage, n)
                        if isinstance(i, int):
                            open_block(FIRST[stage] + n)
                        else:
                            who = OWNER[FIRST[stage]]
                            pe.wait_ge(out_of[who], i * (body * per) + emptied_by(who, FIRST[stage]) + n - 3)
                        for k in range(ks):
                            if first and m == 0 and ready:
                                pe.wait_ge(sem(ready[0]), ready[1] + k + 1)
                            at = k * (512 if per == 4 else P) + m * P
                            w = wring[:, u % 2, at:at + P]
                            mm(bankA(s), w, rhs[:, k, 0:SEQ], start=(k == 0), stop=(k == ks - 1))
                            last = mm(bankB(s), w, rhs[:, k, SEQ:T], start=(k == 0), stop=(k == ks - 1))
                        last.then_inc(block_in, 1)

                j = 0
                if ready:
                    for j in range(body):
                        unit(j, 0, first=(j == 0))
                    j = body
                loops = (units - j) // body
                if loops > 1:
                    for n in range(4 if j == 0 else 0):
                        open_block(FIRST[stage] + n)
                    with pe.Fori(0, loops) as i:
                        for m in range(body):
                            unit(j + m, i)
                elif loops == 1:
                    for m in range(body):
                        unit(j + m, 0)
                for m in range(j + loops * body, units):
                    unit(m, 0)

            def ones_sum(stage, j, ready, base, src, ks, rows_of=None):
                s = slot(stage, j)
                open_block(FIRST[stage] + j)
                for k in range(ks):
                    pe.wait_ge(sem(ready), base + k + 1)
                    mm(bankA(s), cst("ones"), src[:, k, 0:SEQ], start=(k == 0), stop=(k == ks - 1))
                    last = mm(bankB(s), cst("ones"), src[:, k, SEQ:T], start=(k == 0), stop=(k == ks - 1))
                last.then_inc(block_in, 1)

            pe.wait_ge(sem("tab0_in"), 16)
            pe.wait_ge(sem("x_in"), 32)
            for f in range(KD):
                s = slot("x", f)
                open_block(f)
                for t in range(NT):
                    tr(ps[:, 2 * s, t * P:(t + 1) * P], xstage[:, t, f * P:(f + 1) * P], ident)
                tr(bankB(s), xstage_s[:, f * P:(f + 1) * P], ident[0:TS, 0:TS]).then_inc(block_in, 1)
            pe.wait_ge(sem("params_in"), 16 * len(PARAMS))
            wait_emptied(pe, KD)
            tr(ps[:, 7, 0:NPARAM], prow[:, :], ident[0:NPARAM, 0:NPARAM]).then_inc(sem("params_turned"), 1)
            ones_sum("norm0", 0, "sq_ready", 0, xn, KD)
            pe.wait_ge(sem("params_ready"), 1)
            gemm("in0", xn, ("xn_ready", 0))

            s = slot("logf")
            open_block(FIRST["logf"])
            pe.wait_ge(sem("wf_in"), 32)
            for k in range(KD):
                mm(bankA(s, rows=H), wf[:, k, :], xn[:, k, 0:SEQ], start=(k == 0), stop=(k == KD - 1))
                last = mm(bankB(s, rows=H), wf[:, k, :], xn[:, k, SEQ:T], start=(k == 0), stop=(k == KD - 1))
            last.then_inc(block_in, 1)

            def heads_to_tokens(stage, src):
                s = slot(stage)
                open_block(FIRST[stage])
                for t in range(NT):
                    tr(ps[:, 2 * s, t * H:(t + 1) * H], src[0:H, t * P:(t + 1) * P], ident[0:H, 0:H])
                tr(bankB(s, H, TS), src[0:H, SEQ:T], ident[0:H, 0:H]).then_inc(block_in, 1)

            pe.wait_ge(sem("logf_ready"), 1)
            heads_to_tokens("logfT", z[3])
            pe.wait_ge(sem("lfn_ready"), 1)
            s = slot("cum")
            open_block(FIRST["cum"])
            for t in range(NT):
                mm(ps[0:H, 2 * s, t * P:SEQ], lfn[:, t * H:(t + 1) * H], cst("upto", 0, SEQ - t * P),
                   start=(t == 0), stop=(t == NT - 1))
            mm(bankB(s, rows=H), lfn[0:TS, NT * H:(NT + 1) * H], cst("upto_s"), start=True, stop=True)\
                .then_inc(block_in, 1)
            wait_emptied(pe, FIRST["cum"] + 1)
            heads_to_tokens("cumT", cumT)

            pe.wait_ge(sem("lg_in"), 32)
            for n in range(H):
                s = slot("sfxT", n)
                open_block(FIRST["sfxT"] + n)
                for a in range(2):
                    page = lg[:, a, :, n]
                    mm(ps[:, 2 * s, a * P:(a + 1) * P], page, ident, start=True, stop=True)
                    last = mm(ps[:, 2 * s + 1, a * P:(a + 1) * P], page, cst("later_page"), start=True, stop=True)
                last.then_inc(block_in, 1)
            lf = lT.rearrange("p a h g -> p (a h g)")
            lcf = lcT.rearrange("p a h g -> p (a h g)")
            wait_emptied(pe, FIRST["sfxT"] + H)
            for n in range(6):
                s = slot("sfx", n)
                open_block(FIRST["sfx"] + n)
                mm(bankA(s), cst("later"), lf[:, n * 512:(n + 1) * 512], start=True, stop=False)
                mm(bankA(s), cst("ones"), lcf[:, n * 512:(n + 1) * 512], start=False, stop=True).then_inc(block_in, 1)

            for stage, first in (("knat", EV_K), ("vnat", EV_V)):
                for t in range(NT + 1):
                    s = slot(stage, t)
                    open_block(FIRST[stage] + t)
                    rows, cols = (P, slice(t * P, (t + 1) * P)) if t < NT else (TS, slice(SEQ, T))
                    for f in range(HB):
                        at = f * P
                        last = tr(ps[0:rows, 2 * s + at // 512, at % 512:at % 512 + P], big[:, first + f, cols], ident)
                    last.then_inc(block_in, 1)

            for n in range(H):
                s = slot("gq", n // 8)
                if n % 8 == 0:
                    open_block(FIRST["gq"] + n // 8)
                last = mm(ps[:, 2 * s, n % 8 * TS:(n % 8 + 1) * TS], ident[0:H, n:n + 1].broadcast_to([H, P]),
                          cumT[0:H, SEQ:T], start=True, stop=True)
                if n in (7, H - 1):
                    last.then_inc(block_in, 1)
            s = slot("snew")
            open_block(FIRST["snew"])
            for n in range(H):
                r = slice(64 * (n % 2), 64 * (n % 2) + 64)
                last = mm(ps[0:TS, 2 * s + n % 2, n // 2 * TS:(n // 2 + 1) * TS], big[r, EV_K + n // 2, SEQ:T],
                          big[r, EV_Q + n // 2, SEQ:T], start=True, stop=True)
            last.then_inc(block_in, 1)

            wait_emptied(pe, FIRST["snew"] + 1)
            NSTEP = H * NT

            def key_gates(hd):
                if hd >= 1:
                    pe.wait_ge(sem("gates_copied"), hd)
                mm(ps[:, 7, :], ident[0:H, hd:hd + 1].broadcast_to([H, P]), cumT[0:H, 0:SEQ], start=True, stop=True)\
                    .then_inc(sem("gates_spread"), 1)

            def turn(n):
                hd, i = n // NT, n % NT
                pe.wait_ge(sem("probs_scaled"), n + 1)
                if n >= 3:
                    pe.wait_ge(sem("probs_turned_copied"), n - 2)
                for j in range(i + 1):
                    last = tr(ps[:, 3 + n % 3, j * P:(j + 1) * P], eb[:, n % 2, j * P:(j + 1) * P], ident)
                last.then_inc(sem("probs_turned"), 1)

            def weigh(hd):
                pe.wait_ge(sem("probs_turned_copied"), NT * (hd + 1))
                if hd >= 1:
                    pe.wait_ge(sem("fox_prompt_done"), hd)
                r = slice(64 * (hd % 2), 64 * (hd % 2) + 64)
                for j in range(NT):
                    last = mm(ps[r, 6, j * P:SEQ], vn0[:, j, hd * D:(hd + 1) * D], pT[:, hd % 2, j, j * P:SEQ],
                              start=(j == 0), stop=(j == NT - 1))
                last.then_inc(sem("fox_prompt_out"), 1)

            key_gates(0)
            for n in range(NSTEP + 4):
                if n < NSTEP:
                    hd, i = n // NT, n % NT
                    r = slice(64 * (hd % 2), 64 * (hd % 2) + 64)
                    if i == 1 and hd + 1 < H:
                        key_gates(hd + 1)
                    if n >= 3:
                        pe.wait_ge(sem("scores_read"), n - 2)
                    mm(ps[:, n % 3, 0:(i + 1) * P], big[r, EV_Q + hd // 2, i * P:(i + 1) * P],
                       big[r, EV_K + hd // 2, 0:(i + 1) * P], start=True, stop=True).then_inc(sem("scores_made"), 1)
                if 2 <= n < NSTEP + 2:
                    turn(n - 2)
                if n >= 3 and (n - 3) % NT == NT - 1:
                    weigh((n - 3) // NT)

            pe.wait_ge(sem("fox_prompt_done"), H)
            pe.wait_ge(sem("hist_in"), 16)
            for a in range(2):
                s = slot("hist", a)
                last = tr(ps[:, 2 * s, 0:NB * HIST], hstage[:, a * P:(a + 1) * P], ident[0:NB * HIST, 0:NB * HIST])
                last.then_inc(block_in, 1)
            pe.wait_ge(sem("pwd_in"), 64)
            pe.wait_ge(sem("pool_d_ready"), 1)
            s = 3
            for a in range(2):
                wait_emptied(pe, FIRST["hist"] + 2) if a == 0 else None
                mm(ps[:, 4 + a, :], pwd[:, a, :], xn[:, a, 0:SEQ], start=True, stop=True)
                last = mm(ps[:, 6 + a, 0:TS], pwd[:, a, :], xn[:, a, SEQ:T], start=True, stop=True)
            last.then_inc(sem("pooled"), 1)
            pe.wait_ge(sem("hist_copied"), 1)
            for a in range(2):
                tr(ps[0:NB * HIST, a, 0:P], hcopy[:, a, :], ident)
                last = tr(ps[0:HIST, a, P:2 * P], big[:, a, SEQ - HIST:SEQ], ident)
            last.then_inc(sem("hist_turned"), 1)

            pe.wait_ge(sem("hist_out_ready"), 1)
            pe.wait_ge(sem("pool_mixed"), 1)
            pe.wait_ge(sem("qblk_ready"), 2)

            def turn_page(b, p):
                k = b * PAGES + p
                arrived(b, p, True)
                static = isinstance(b, int)
                if not static or k >= 2:
                    pe.wait_ge(sem("kT_low"), k - 1)
                    pe.wait_ge(sem("kT_high"), k - 1)
                for f in range(HB):
                    at = f * P
                    last = tr(ps[:, 2 * (p % 2) + at // 512, at % 512:at % 512 + P],
                              ring[:, p % RING, at:at + P], ident)
                last.then_inc(sem("k_page_used"), 1)

            def arrived(b, p, is_k):
                if is_k:
                    at = b * (2 * PAGES) - PAGES + p if not (isinstance(b, int) and b == 0) else p
                else:
                    at = b * (2 * PAGES) + 2 * PAGES + p if not (isinstance(b, int) and b == NB - 1) else \
                        b * 2 * PAGES + PAGES + p
                off = (p - p % RING) // RING
                if is_k and isinstance(b, int) and b == 0:
                    cnt = off + 1
                elif is_k:
                    cnt = b * (2 * PAGES // RING) - PAGES // RING + off + 1
                elif isinstance(b, int) and b == NB - 1:
                    cnt = (b * 2 * PAGES + PAGES) // RING + off + 1
                else:
                    cnt = b * (2 * PAGES // RING) + 2 * PAGES // RING + off + 1
                pe.wait_ge(page_in[p % RING], cnt * 16)

            def score_page(b, p):
                k = b * PAGES + p
                pe.wait_ge(sem("kT_low"), k + 1)
                pe.wait_ge(sem("kT_high"), k + 1)
                if p % 4 == 0:
                    quad = b * (PAGES // 4) + p // 4
                    if not isinstance(b, int) or quad >= 2:
                        pe.wait_ge(sem("quads_read"), quad - 1)
                for f in range(HB):
                    at = p % 4 * HQ + f * 16
                    q = qblk[:, b, f * 16:(f + 1) * 16] if isinstance(b, int) else \
                        qblk[:, bass.ds(b, 1), f * 16:(f + 1) * 16]
                    last = mm(ps[:, 4 + p // 4 % 2, at:at + 16], kT[:, p % 2, f * P:(f + 1) * P], q,
                              start=True, stop=True)
                last.then_inc(sem("pages_scored"), 1)

            def turn_max(b):
                pe.wait_ge(sem("max_ready"), b + 1)
                tr(ps[0:HQ, 6, 0:P], mxr, ident).then_inc(sem("max_turned"), 1)

            def spread_max(b):
                pe.wait_ge(sem("gmax_ready"), b + 1)
                mm(ps[:, 6, 128:128 + HQ], gcols[0:HQ, 0:1].broadcast_to([HQ, P]), ident[0:HQ, 0:HQ],
                   start=True, stop=True).then_inc(sem("max_spread"), 1)

            def spread_sum(b):
                pe.wait_ge(sem("sum_ready"), b + 1)
                mm(ps[:, 6, 256:256 + HQ], cst("ones"), rsum, start=True, stop=True).then_inc(sem("sum_spread"), 1)

            def weigh_page(b, p):
                for f in range(HB):
                    v = ring[:, p % RING, f * P:(f + 1) * P] if p < PAGES else vs[:, f * P:(f + 1) * P]
                    last = mm(ps[:, 7, f * 16:(f + 1) * 16], v, E[:, p, f * 16:(f + 1) * 16],
                              start=(p == 0 and f == 0), stop=(p == PAGES), skip_group_check=True)
                last.then_inc(sem("v_page_used") if p < PAGES else sem("fox_sample_out"), 1)

            def k_pages(b, soft):
                if soft is not None:
                    turn_max(soft)
                for p in range(PAGES + 1):
                    if p < PAGES:
                        turn_page(b, p)
                    if p >= 1:
                        score_page(b, p - 1)
                    if soft is not None and p == 2:
                        spread_max(soft)
                    if soft is not None and p == 20:
                        spread_sum(soft)

            def v_pages(b):
                if not isinstance(b, int) or b >= 1:
                    pe.wait_ge(sem("fox_sample_done"), b)
                for p in range(PAGES):
                    arrived(b, p, False)
                    weigh_page(b, p)
                weigh_page(b, PAGES)

            k_pages(0, None)
            k_pages(1, 0)
            v_pages(0)
            with pe.Fori(1, NB - 1) as b:
                k_pages(b + 1, b)
                v_pages(b)
            turn_max(NB - 1)
            spread_max(NB - 1)
            spread_sum(NB - 1)
            v_pages(NB - 1)

            pe.wait_ge(sem("fox_sample_done"), NB)
            gemm("out0", xn)
            ones_sum("norm1", 0, "sq_ready", KD, big, KD)
            gemm("up0", xn, ("xn_ready", KD))
            gemm("down0", big, ("u_ready", 0))

            ones_sum("norm2", 0, "sq_ready", 2 * KD, xn, KD)
            gemm("in1", xn, ("xn_ready", 2 * KD))
            s = slot("wst")
            open_block(FIRST["wst"])
            pe.wait_ge(sem("ws_in"), 16)
            for g in range(4):
                last = tr(ps[:, 2 * s, g * P:(g + 1) * P], wsn[:, g, :], ident)
            last.then_inc(block_in, 1)
            s = slot("w8")
            open_block(FIRST["w8"])
            wait_emptied(pe, FIRST["wst"] + 1)
            pe.wait_ge(sem("tab1_in"), 16)
            mm(ps[0:TS, 2 * s, 0:4 * NS], cst1("rep"), wT[0:NS, :, 0:NS], start=True, stop=True).then_inc(block_in, 1)
            ones_sum("mu", 0, "emptied_by_scalar", emptied_by("scalar", FIRST["in1"] + OD_GV), big[:, OD_GV:OD_GV + 4, :], 4)
            ones_sum("var", 0, "lnsq_ready", 0, xn[:, 4:8, :], 4)
            pe.wait_ge(sem("ln_ready"), 4)
            for t in range(NT + 1):
                s = slot("vnat1", t)
                open_block(FIRST["vnat1"] + t)
                rows, cols = (P, slice(t * P, (t + 1) * P)) if t < NT else (TS, slice(SEQ, T))
                for f in range(4):
                    last = tr(ps[0:rows, 2 * s, f * P:(f + 1) * P], big[:, OD_GV + f, cols], ident)
                last.then_inc(block_in, 1)
            pe.wait_ge(sem("bs_in"), 16)
            wait_emptied(pe, FIRST["vnat1"] + NT + 1)
            for g in range(4):
                s = slot("z", g)
                open_block(FIRST["z"] + g)
                bias = bsr[0:1, g * P:(g + 1) * P].rearrange("p (o t) -> p o t", o=1)
                mm(bankA(s), cst("ones", rows=1), bias.broadcast_to([1, NT, P]), start=True, stop=False)
                for t in range(NT):
                    mm(ps[:, 2 * s, t * P:(t + 1) * P], vnn[:, t, g * P:(g + 1) * P], wT[:, g, :],
                       start=False, stop=(t == NT - 1))
                mm(bankB(s), cst("ones", rows=1), bias[:, :, 0:NS].broadcast_to([1, NB, NS]), start=True, stop=False)
                mm(bankB(s), vnn[0:TS, NT, g * P:(g + 1) * P], w8[:, g, :], start=False, stop=True)\
                    .then_inc(block_in, 1)
            for n in range(2 * R):
                s = slot("rot", n)
                open_block(FIRST["rot"] + n)
                mm(bankA(s), cst1("swap"), big[:, OD_RQ + n, 0:SEQ], start=True, stop=True)
                mm(bankB(s), cst1("swap"), big[:, OD_RQ + n, SEQ:T], start=True, stop=True).then_inc(block_in, 1)
            pe.wait_ge(sem("rotated"), 2 * R)
            for stage, first in (("kn", OD_RK), ("vn", OD_RV)):
                for t in range(NT + 1):
                    s = slot(stage, t)
                    open_block(FIRST[stage] + t)
                    rows, cols = (P, slice(t * P, (t + 1) * P)) if t < NT else (TS, slice(SEQ, T))
                    for f in range(R):
                        last = tr(ps[0:rows, 2 * s, f * P:(f + 1) * P], big[:, first + f, cols], ident)
                    last.then_inc(block_in, 1)
            wait_emptied(pe, FIRST["vn"] + NT + 1)
            pe.wait_ge(sem("s0_in"), 16 * R)
            for n in range(R):
                base = FIRST["ret"] + 4 * n
                q, k = big[:, OD_RQ + n, :], big[:, OD_RK + n, :]
                cols = slice(n * P, (n + 1) * P)
                s = base % 4
                open_block(base)
                for t in range(NT):
                    mm(ps[:, 2 * s, t * P:(t + 1) * P], k[:, t * P:(t + 1) * P], q[:, t * P:(t + 1) * P],
                       start=True, stop=True)
                mm(bankB(s, rows=TS), k[:, SEQ:T], q[:, SEQ:T], start=True, stop=True).then_inc(block_in, 1)
                s = (base + 1) % 4
                open_block(base + 1)
                for t in range(NT):
                    last = mm(ps[:, 2 * s, t * P:(t + 1) * P], kn[:, t, cols], v2[:, t, cols], start=True, stop=True)
                last.then_inc(block_in, 1)
                s = (base + 2) % 4
                open_block(base + 2)
                pe.wait_ge(sem("v_spread"), n + 1)
                for a in range(2):
                    last = mm(ps[:, 2 * s + a, :], kn[0:TS, NT, cols], vmask[:, 4 * a:4 * a + 4, :],
                              start=True, stop=True)
                last.then_inc(block_in, 1)
                s = (base + 3) % 4
                open_block(base + 3)
                pe.wait_ge(sem("q_decayed"), n + 1)
                pe.wait_ge(sem("states_ready"), n + 1)
                for t in range(NT):
                    o = ps[:, 2 * s, t * P:(t + 1) * P]
                    mm(o, v2[:, t, cols], sct[:, t * P:(t + 1) * P], start=True, stop=(t == 0))
                    if t:
                        mm(o, st[:, t - 1, :], q[:, t * P:(t + 1) * P], start=False, stop=True)
                mm(bankB(s), v2[0:TS, NT, cols], sct[0:TS, SEQ:T], start=True, stop=False)
                for b in range(NB):
                    last = mm(ps[:, 2 * s + 1, b * NS:(b + 1) * NS], s0[:, n, b, :],
                              q[:, SEQ + b * NS:SEQ + (b + 1) * NS], start=False, stop=(b == NB - 1))
                last.then_inc(block_in, 1)
            for n in range(R):
                ones_sum("hmu", n, "emptied_by_scalar", emptied_by("scalar", FIRST["ret"] + 16) - 1, big[:, OD_RQ + n:OD_RQ + n + 1, :], 1)
            for n in range(R):
                ones_sum("hvar", n, "hsq_ready", n, xn[:, 4 + n:5 + n, :], 1)
            pe.wait_ge(sem("mixed1"), 1)
            gemm("out1", xn)
            ones_sum("norm3", 0, "sq_ready", 3 * KD, big, KD)
            gemm("up1", xn, ("xn_ready", 3 * KD))
            gemm("down1", big, ("u_ready", 32))

            ones_sum("norm4", 0, "sq_ready", 4 * KD, xn, KD)
            pe.wait_ge(sem("xn_ready"), 5 * KD)
            for t in range(NT + 1):
                s = slot("y", t)
                open_block(FIRST["y"] + t)
                rows, cols = (P, slice(t * P, (t + 1) * P)) if t < NT else (TS, slice(SEQ, T))
                for f in range(KD):
                    last = tr(ps[0:rows, 2 * s + f // 4, f % 4 * P:(f % 4 + 1) * P], xn[:, f, cols], ident)
                last.then_inc(block_in, 1)

        @blk.scalar
        def _(act):
            own = Steps(act, sem("act_steps"))
            act_f = nc.scalar.activation

            def evacuate(stage, count, dst, func=ACT.Copy, dyn=4):
                def one(n, i, m):
                    s = slot(stage, n)
                    act.wait_ge(block_in, FIRST[stage] + n + 1 + m)
                    d = dst(n, i)
                    act_f(d[:, 0:SEQ] if len(d.shape) == 2 else d[:, :, 0:SEQ], bankA(s), func)
                    act_f(d[:, SEQ:T] if len(d.shape) == 2 else d[:, :, SEQ:T], bankB(s), func)\
                        .then_inc(out_of["scalar"], 1)
                loops = count // 4
                if loops > 1:
                    with act.Fori(0, loops) as i:
                        for n in range(4):
                            one(n, i, i * 4)
                else:
                    for n in range(count):
                        one(n, None, 0)

            def norm(k):
                if k == 0:
                    wait_emptied(act, KD)
                for f in range(KD):
                    if k:
                        wait_emptied(act, FIRST[("", "out0", "down0", "out1", "down1")[k]] + f + 1)
                    act_f((big if k in (1, 3) else xn)[:, f, :], h[:, f, :], ACT.Square).then_inc(sem("sq_ready"), 1)
                root(f"norm{k}", 0, DM, rstd[:, :], "rms_ready")

            def root(stage, j, width, dst, signal):
                s = slot(stage, j)
                act.wait_ge(block_in, FIRST[stage] + j + 1)
                act_f(dst[:, 0:SEQ], bankA(s), ACT.Sqrt, bias=EPS, scale=1.0 / width).then_inc(sem(signal), 1)
                act_f(dst[:, SEQ:T], bankB(s), ACT.Sqrt, bias=EPS, scale=1.0 / width).then_inc(out_of["scalar"], 1)

            wait_emptied(act, KD)
            norm(0)
            evacuate("in0", 20, lambda n, i: big[:, n, :] if i is None else big[:, bass.ds(i * 4 + n, 1), :])

            act.wait_ge(sem("negabs_ready"), 1)
            own(act_f(z[2], z[1], ACT.Exp))
            act_f(z[1], z[2], ACT.Ln, bias=1.0).then_inc(sem("log1p_ready"), 1)
            s = slot("cum")
            act.wait_ge(block_in, FIRST["cum"] + 1)
            act_f(cumT[:, 0:SEQ], bankA(s, rows=H), ACT.Copy)
            act_f(cumT[:, SEQ:T], bankB(s, rows=H), ACT.Copy).then_inc(out_of["scalar"], 1)
            s = slot("cumT")
            act.wait_ge(block_in, FIRST["cumT"] + 1)
            act_f(cumn[:, 0:NT * H], bankA(s, NT * H), ACT.Copy)
            act_f(cumn[0:TS, NT * H:(NT + 1) * H], bankB(s, H, TS), ACT.Copy).then_inc(out_of["scalar"], 1)
            for n in range(H):
                s = slot("sfxT", n)
                act.wait_ge(block_in, FIRST["sfxT"] + n + 1)
                act_f(lT[:, :, n, :], bankA(s, 2 * P).rearrange("p (a g) -> p a g", a=2), ACT.Copy)
                act_f(lcT[:, :, n, :], bankB(s, 2 * P).rearrange("p (a g) -> p a g", a=2), ACT.Copy)\
                    .then_inc(out_of["scalar"], 1)
            to = sfx.rearrange("p (a g h) -> p a h g", a=2, h=H)
            for n in range(6):
                s = slot("sfx", n)
                act.wait_ge(block_in, FIRST["sfx"] + n + 1)
                act_f(to[:, n // 3, n % 3 * 4:n % 3 * 4 + 4, :], bankA(s).rearrange("p (h g) -> p h g", h=4), ACT.Copy)\
                    .then_inc(out_of["scalar"], 1)

            def copy_gates(hd):
                act.wait_ge(sem("gates_spread"), hd + 1)
                if hd >= 2:
                    act.wait_ge(sem("scores_read"), NT * (hd - 1))
                act_f(ckb[:, hd % 2, :], ps[:, 7, :], ACT.Copy, scale=-1.0).then_inc(sem("gates_copied"), 1)

            NSTEP = H * NT
            wait_emptied(act, FIRST["snew"] + 1)
            act.wait_ge(sem("k_stored_0"), 48)
            act.wait_ge(sem("k_stored_1"), 32)
            copy_gates(0)
            for n in range(NSTEP + 2):
                if n < NSTEP:
                    hd, i = n // NT, n % NT
                    if i == 1 and hd + 1 < H:
                        copy_gates(hd + 1)
                    act.wait_ge(sem("shift_ready"), n + 1)
                    if n >= 2:
                        act.wait_ge(sem("probs_turned"), n - 1)
                    w = (i + 1) * P
                    act_f(eb[:, n % 2, 0:w], tb[:, n % 2, 0:w], ACT.Exp, bias=hstat[:, 8 + n % 4:9 + n % 4],
                          accum_out=hstat[:, 12 + n % 4:13 + n % 4]).then_inc(sem("probs_made"), 1)
                if n >= 2:
                    m = n - 2
                    hd, i = m // NT, m % NT
                    act.wait_ge(sem("probs_turned"), m + 1)
                    if hd >= 2:
                        act.wait_ge(sem("fox_prompt_out"), hd - 1)
                    act_f(pT[:, hd % 2, 0:i + 1, i * P:(i + 1) * P],
                          ps[:, 3 + m % 3, 0:(i + 1) * P].rearrange("p (j q) -> p j q", j=i + 1), ACT.Copy)\
                        .then_inc(sem("probs_turned_copied"), 1)

            def copy_page(b, p):
                k = b * PAGES + p
                act.wait_ge(sem("k_page_used"), k + 1)
                if not isinstance(b, int) or k >= 2:
                    act.wait_ge(sem("pages_scored"), k - 1)
                act_f(kT[:, p % 2, 0:512], ps[:, 2 * (p % 2), :], ACT.Copy).then_inc(sem("kT_low"), 1)

            def exps(b):
                act.wait_ge(sem("shifted"), b + 1)
                act_f(E, E, ACT.Exp).then_inc(sem("exp_done"), 1)

            def k_pages(b, soft):
                for p in range(PAGES):
                    copy_page(b, p)
                    if soft is not None and p == 7:
                        exps(soft)

            act.wait_ge(sem("qblk_ready"), 2)
            k_pages(0, None)
            k_pages(1, 0)
            with act.Fori(1, NB - 1) as b:
                k_pages(b + 1, b)
            exps(NB - 1)

            norm(1)
            def mlp(stage):
                with act.Fori(0, 8) as i:
                    for n in range(4):
                        s = slot(stage, n)
                        act.wait_ge(block_in, FIRST[stage] + n + 1 + i * 4)
                        act_f(big[:, bass.ds(i * 4 + n, 1), 0:SEQ], bankA(s), ACT.Relu)
                        act_f(big[:, bass.ds(i * 4 + n, 1), SEQ:T], bankB(s), ACT.Relu).then_inc(out_of["scalar"], 1)
            act.wait_ge(sem("stored"), 64)
            mlp("up0")
            norm(2)
            evacuate("in1", 24, lambda n, i: big[:, n, :] if i is None else big[:, bass.ds(i * 4 + n, 1), :])
            s = slot("mu")
            act.wait_ge(block_in, FIRST["mu"] + 1)
            act_f(rstd[:, 0:SEQ], bankA(s), ACT.Copy, scale=1.0 / 512)
            act_f(rstd[:, SEQ:T], bankB(s), ACT.Copy, scale=1.0 / 512).then_inc(out_of["scalar"], 1)
            for f in range(4):
                act.wait_ge(sem("centred"), f + 1)
                act_f(xn[:, 4 + f, :], big[:, OD_GV + f, :], ACT.Square).then_inc(sem("lnsq_ready"), 1)
            root("var", 0, 512, rstd[:, :], "ln_root")
            for n in range(R):
                act_f(big[:, OD_U + n, :], big[:, OD_RG + n, :], ACT.Exp, scale=-1.0) if False else None
            for stage, dst in (("kn", None), ("vn", v2)):
                if dst is None:
                    continue
                for t in range(NT + 1):
                    s = slot(stage, t)
                    rows = P if t < NT else TS
                    act.wait_ge(block_in, FIRST[stage] + t + 1)
                    act_f(dst[0:rows, t, :], bankA(s, rows=rows), ACT.Copy).then_inc(out_of["scalar"], 1)
            for n in range(R):
                s = slot("ret", 4 * n + 3)
                act.wait_ge(block_in, FIRST["ret"] + 4 * n + 4)
                act_f(big[:, OD_RQ + n, 0:SEQ], bankA(s), ACT.Copy)
                act_f(big[:, OD_RQ + n, SEQ:T], bankB(s), ACT.Copy).then_inc(out_of["scalar"], 1)
            for n in range(R):
                own(act_f(big[:, OD_RK + n, :], big[:, OD_RG + n, :], ACT.Exp, scale=-1.0))
            act.sem_inc(sem("gate_exp"), 1)
            for n in range(R):
                s = slot("hmu", n)
                act.wait_ge(block_in, FIRST["hmu"] + n + 1)
                act_f(big[:, OD_RV + n, 0:SEQ], bankA(s), ACT.Copy, scale=1.0 / DR)
                act_f(big[:, OD_RV + n, SEQ:T], bankB(s), ACT.Copy, scale=1.0 / DR).then_inc(out_of["scalar"], 1)
            for n in range(R):
                act.wait_ge(sem("hcentred"), n + 1)
                act_f(xn[:, 4 + n, :], big[:, OD_RQ + n, :], ACT.Square).then_inc(sem("hsq_ready"), 1)
            for n in range(R):
                root("hvar", n, DR, big[:, OD_RV + n, :], "hroot_a")
            norm(3)
            act.wait_ge(sem("ret_stored"), 32 * R)
            mlp("up1")
            norm(4)

        @blk.vector
        def _(dve):
            own = Steps(dve, sem("dve_steps"))
            tt, stt, ts = nc.vector.tensor_tensor, nc.vector.scalar_tensor_tensor, nc.vector.tensor_scalar
            cp = nc.vector.tensor_copy

            def drained(stage, n):
                dve.wait_ge(block_in, FIRST[stage] + n + 1)
                return slot(stage, n)

            def norm(k, row):
                wait_emptied(dve, FIRST[f"norm{k}"] + 1)
                own(nc.vector.reciprocal(rstd[:, :], rstd[:, :]))
                for f in range(KD):
                    stt(xn[:, f, :], h[:, f, :], pcol[:, row + f:row + f + 1], rstd[:, :], ALU.mult, ALU.mult)\
                        .then_inc(sem("xn_ready"), 1)

            def residual(stage):
                for n in range(KD):
                    s = drained(stage, n)
                    tt(h[:, n, 0:SEQ], bankA(s), h[:, n, 0:SEQ], ALU.add)
                    tt(h[:, n, SEQ:T], bankB(s), h[:, n, SEQ:T], ALU.add).then_inc(out_of["vector"], 1)

            def squares(stage, base):
                with dve.Fori(0, 8) as i:
                    for n in range(4):
                        dve.wait_ge(out_of["scalar"], emptied_by("scalar", FIRST[stage]) + n + 1 + i * 4)
                        u = big[:, bass.ds(i * 4 + n, 1), :]
                        tt(u, u, u, ALU.mult).then_inc(sem("u_ready"), 1)

            for f in range(KD):
                s = drained("x", f)
                cp(h[:, f, 0:SEQ], bankA(s))
                cp(h[:, f, SEQ:T], bankB(s)).then_inc(out_of["vector"], 1)
            dve.wait_ge(sem("params_turned"), 1)
            cp(pcol[:, :], ps[:, 7, 0:NPARAM]).then_inc(sem("params_ready"), 1)
            dve.wait_ge(sem("params_ready"), 1)
            norm(0, PROW["norm_mix"])

            s = drained("logf", 0)
            dve.wait_ge(sem("wf_in"), 32)
            ts(z[0][:, 0:SEQ], bankA(s, rows=H), bf[:, 0:1], None, ALU.add)
            ts(z[0][:, SEQ:T], bankB(s, rows=H), bf[:, 0:1], None, ALU.add).then_inc(out_of["vector"], 1)
            wait_emptied(dve, FIRST["logf"] + 1)
            own(ts(z[2], z[0], -1.0, None, ALU.mult))
            tt(z[1], z[2], z[0], ALU.min).then_inc(sem("negabs_ready"), 1)
            own(ts(z[0], z[0], 0.0, None, ALU.min))
            dve.wait_ge(sem("log1p_ready"), 1)
            tt(z[3], z[0], z[1], ALU.subtract).then_inc(sem("logf_ready"), 1)
            s = drained("logfT", 0)
            cp(lfn[:, 0:NT * H], bankA(s, NT * H))
            cp(lfn[0:TS, NT * H:(NT + 1) * H], bankB(s, H, TS)).then_inc(out_of["vector"], 1)
            wait_emptied(dve, FIRST["logfT"] + 1)
            dve.sem_inc(sem("lfn_ready"), 1)

            def rows(stage, dst, before=None):
                for t in range(NT + 1):
                    if before:
                        before(t)
                    s = drained(stage, t)
                    r = P if t < NT else TS
                    d = dst(t)
                    cp(d[0:r, 0:512], bankA(s, rows=r))
                    cp(d[0:r, 512:FOX], bankB(s, FOX - 512, r)).then_inc(out_of["vector"], 1)

            def stage_free(t):
                if t == 0:
                    wait_emptied(dve, FIRST["sfx"] + 6)
                if t >= 2:
                    dve.wait_ge(sem(f"k_stored_{t % 2}"), 16 * (t // 2))

            rows("knat", lambda t: kstage[:, t % 2, :], stage_free)
            own(nc.vector.memset(vs, 0.0))
            rows("vnat", lambda t: vn0[:, t, :] if t < NT else vs)
            s = drained("gq", 0)
            cp(gq[:, 0:8, :], bankA(s).rearrange("p (h t) -> p h t", h=8)).then_inc(out_of["vector"], 1)
            s = drained("gq", 1)
            cp(gq[:, 8:H, :], bankA(s, 256).rearrange("p (h t) -> p h t", h=4)).then_inc(out_of["vector"], 1)
            gk = cumn[0:TS, NT * H:(NT + 1) * H].rearrange("p (h o) -> p h o", o=1).broadcast_to([TS, H, TS])
            mk = cst("mask_s").rearrange("p (o t) -> p o t", o=1).broadcast_to([TS, H, TS])
            own(tt(kmask, mk, gk, ALU.subtract))
            s = drained("snew", 0)
            for a in range(2):
                of = lambda x: x.rearrange("p (f a) t -> p a f t", a=2)[:, a]
                ins = stt(of(snew), ps[0:TS, 2 * s + a, 0:HB * TS].rearrange("p (f t) -> p f t", f=HB), D ** -0.5,
                          of(kmask), ALU.mult, ALU.add)
            ins.then_inc(out_of["vector"], 1)
            own(nc.vector.memset(qblk, 0.0))
            for a in range(2):
                r = slice(64 * a, 64 * a + 64)
                dst = qblk[r, :, :].rearrange("p b (f c) -> p b f c", f=HB)[:, :, :, 8 * a:8 * a + 8]
                src = big[r, EV_Q:EV_Q + HB, SEQ:T].rearrange("p f (b s) -> p b f s", b=NB)
                cp(dst, src).then_inc(sem("qblk_ready"), 1)

            mx, mf, shift, den, rec = (hstat[:, 4 * n:4 * n + 4] for n in range(5))

            def scale_probs(n):
                hd, i = n // NT, n % NT
                c = n % 4
                dve.wait_ge(sem("probs_made"), n + 1)
                own(nc.vector.reciprocal(rec[:, c:c + 1], den[:, c:c + 1]))
                w = (i + 1) * P
                ts(eb[:, n % 2, 0:w], eb[:, n % 2, 0:w], rec[:, c:c + 1], None, ALU.mult)\
                    .then_inc(sem("probs_scaled"), 1)

            def head_out(hd):
                r = slice(64 * (hd % 2), 64 * (hd % 2) + 64)
                dve.wait_ge(sem("fox_prompt_out"), hd + 1)
                cp(xn[r, 2 + hd // 2, 0:SEQ], ps[r, 6, :]).then_inc(sem("fox_prompt_done"), 1)

            NSTEP = H * NT
            for n in range(NSTEP + 5):
                if n < NSTEP:
                    hd, i = n // NT, n % NT
                    c, w = n % 4, (i + 1) * P
                    dve.wait_ge(sem("scores_made"), n + 1)
                    dve.wait_ge(sem("gates_copied"), hd + 1)
                    if n >= 2:
                        dve.wait_ge(sem("probs_made"), n - 1)
                    stt(tb[:, n % 2, 0:w], ps[:, n % 3, 0:w], D ** -0.5, ckb[:, hd % 2, 0:w], ALU.mult, ALU.add)\
                        .then_inc(sem("scores_read"), 1)
                    dve.wait_ge(sem("scores_read"), n + 1)
                    own(tt(tb[:, n % 2, w - P:w], tb[:, n % 2, w - P:w], cst("mask"), ALU.add))
                    own(nc.vector.reduce_max(mx[:, c:c + 1], tb[:, n % 2, 0:w], AX.X))
                    g = cumn[:, i * H + hd:i * H + hd + 1]
                    own(tt(mf[:, c:c + 1], mx[:, c:c + 1], g, ALU.add))
                    tt(shift[:, c:c + 1], g, mf[:, c:c + 1], ALU.subtract).then_inc(sem("shift_ready"), 1)
                if 1 <= n < NSTEP + 1:
                    scale_probs(n - 1)
                if n >= 4 and (n - 4) % NT == NT - 1:
                    head_out((n - 4) // NT)

            for a in range(2):
                s = drained("hist", a)
                cp(es[0][:, a, :, 0:HIST], ps[:, 2 * s, 0:NB * HIST].rearrange("p (b t) -> p b t", b=NB))\
                    .then_inc(out_of["vector"], 1)
            wait_emptied(dve, FIRST["hist"] + 2)
            for a in range(2):
                own(cp(es[0][:, a, :, HIST:HIST + NS], big[:, a, SEQ:T].rearrange("p (b s) -> p b s", b=NB)))
                cp(hcopy[:, a, :].rearrange("p (b t) -> p b t", b=NB), es[0][:, a, :, NS:NS + HIST])\
                    .then_inc(sem("ext_s_ready"), 1)
            dve.wait_ge(sem("ext_s_ready"), 2)
            dve.sem_inc(sem("hist_copied"), 1)
            dve.wait_ge(sem("pooled"), 1)
            for a in range(2):
                ts(xn[:, a, 0:SEQ], ps[:, 4 + a, :], param("pool_scale", a), None, ALU.mult)
                own(ts(xn[:, a, SEQ:T], ps[:, 6 + a, 0:TS], param("pool_scale", a), None, ALU.mult))
            dve.sem_inc(sem("pool_mixed"), 1)
            dve.wait_ge(sem("hist_turned"), 1)
            for a in range(2):
                cp(hout[:, a * P:(a + 1) * P], ps[0:NB * HIST, a, 0:P])
                own(cp(hout_p[:, a * P:(a + 1) * P], ps[0:HIST, a, P:2 * P]))
            dve.sem_inc(sem("hist_out_ready"), 1)

            def at(x, b, n=1):
                return x[:, b:b + n] if isinstance(b, int) else x[:, bass.ds(b, n)]

            def copy_page(b, p):
                k = b * PAGES + p
                dve.wait_ge(sem("k_page_used"), k + 1)
                if not isinstance(b, int) or k >= 2:
                    dve.wait_ge(sem("pages_scored"), k - 1)
                cp(kT[:, p % 2, 512:FOX], ps[:, 2 * (p % 2) + 1, 0:FOX - 512]).then_inc(sem("kT_high"), 1)

            def add_suffix(b, quad):
                dve.wait_ge(sem("pages_scored"), b * PAGES + 4 * quad + 4)
                n = 4 * H
                lo = b * (PAGES * H) + quad * n
                g = sfx[:, lo:lo + n] if isinstance(b, int) else sfx[:, bass.ds(lo, n)]
                g = g.rearrange("p (n o) -> p n o", o=1).broadcast_to([P, n, NS])
                src = ps[:, 4 + quad % 2, 0:4 * HQ].rearrange("p (n s) -> p n s", s=NS)
                stt(S[:, 4 * quad:4 * quad + 4, :].rearrange("p g (h s) -> p (g h) s", s=NS), src, D ** -0.5, g,
                    ALU.mult, ALU.add).then_inc(sem("quads_read"), 1)

            def new_keys(b):
                src = snew[:, :, b * NS:(b + 1) * NS] if isinstance(b, int) else snew[:, :, bass.ds(b * NS, NS)]
                own(cp(S[0:TS, PAGES, :].rearrange("p (h s) -> p h s", s=NS), src))

            def maxima(b):
                dve.wait_ge(sem("quads_read"), (b + 1) * (PAGES // 4))
                nc.vector.reduce_max(mxr, S.rearrange("p g c -> p c g"), AX.X).then_inc(sem("max_ready"), 1)

            def column_max(b):
                dve.wait_ge(sem("max_turned"), b + 1)
                nc.vector.reduce_max(gcols[0:HQ, 0:1], ps[0:HQ, 6, 0:P], AX.X).then_inc(sem("gmax_ready"), 1)

            def shift_all(b):
                dve.wait_ge(sem("max_spread"), b + 1)
                if not isinstance(b, int) or b >= 1:
                    dve.wait_ge(sem("fox_sample_out"), b)
                g = gq[:, :, b * NS:(b + 1) * NS] if isinstance(b, int) else gq[:, :, bass.ds(b * NS, NS)]
                hq = lambda x: x.rearrange("p (h s) -> p h s", s=NS)
                own(tt(hq(br), hq(ps[:, 6, 128:128 + HQ]), g, ALU.add))
                own(tt(hq(br), g, hq(br), ALU.subtract))
                tt(E, S, br.rearrange("p (o c) -> p o c", o=1).broadcast_to([P, 33, HQ]), ALU.add)\
                    .then_inc(sem("shifted"), 1)
                dve.wait_ge(sem("shifted"), b + 1)

            def sums(b):
                dve.wait_ge(sem("exp_done"), b + 1)
                nc.vector.reduce_sum(rsum, E.rearrange("p g c -> p c g"), AX.X).then_inc(sem("sum_ready"), 1)

            def out(b):
                dve.wait_ge(sem("sum_spread"), b + 1)
                own(nc.vector.reciprocal(rden, ps[:, 6, 256:256 + HQ]))
                dve.wait_ge(sem("fox_sample_out"), b + 1)
                for a in range(2):
                    r = slice(64 * a, 64 * a + 64)
                    pick = lambda x: x.rearrange("p (f a s) -> p f a s", a=2, s=NS)[:, :, a, :]
                    dst = xn[r, 2:KD, SEQ + b * NS:SEQ + (b + 1) * NS] if isinstance(b, int) else \
                        xn[r, 2:KD, bass.ds(b * NS + SEQ, NS)]
                    own(tt(dst, pick(ps[r, 7, 0:HQ]), pick(rden[r, :]), ALU.mult))
                dve.sem_inc(sem("fox_sample_done"), 1)

            def k_pages(b, soft):
                if soft is not None:
                    maxima(soft)
                for p in range(PAGES):
                    copy_page(b, p)
                    if soft is not None:
                        if p == 1:
                            column_max(soft)
                        if p == 4:
                            shift_all(soft)
                        if p == 14:
                            sums(soft)
                    if p % 4 == 1 and p > 4:
                        add_suffix(b, p // 4 - 1)
                add_suffix(b, PAGES // 4 - 1)
                new_keys(b)

            own(nc.vector.memset(S[TS:P, PAGES, :], NEG))
            k_pages(0, None)
            k_pages(1, 0)
            out(0)
            with dve.Fori(1, NB - 1) as b:
                own.loop(b - 1, 6)
                k_pages(b + 1, b)
                out(b)
            own.end(NB - 2)
            maxima(NB - 1)
            column_max(NB - 1)
            shift_all(NB - 1)
            sums(NB - 1)
            out(NB - 1)

            residual("out0")
            norm(1, PROW["norm_ffn"])
            squares("up0", 0)
            residual("down0")

            norm(2, PROW["norm_mix"] + KD)
            s = drained("wst", 0)
            low = cst("upto", 0, P).rearrange("p (o t) -> p o t", o=1).broadcast_to([P, 4, P])
            tt(wT, bankA(s).rearrange("p (g t) -> p g t", g=4), low, ALU.mult).then_inc(out_of["vector"], 1)
            s = drained("w8", 0)
            corner = ps[0:TS, 2 * s, 0:4 * NS].rearrange("p (g t) -> p g t", g=4)
            for g in range(4):
                last = tt(w8[:, g, :].rearrange("p (b t) -> p b t", b=NB),
                          corner[:, g:g + 1, :].broadcast_to([TS, NB, NS]),
                          cst1("same_s").rearrange("p (b t) -> p b t", b=NB), ALU.mult)
            last.then_inc(out_of["vector"], 1)
            wait_emptied(dve, FIRST["mu"] + 1)
            for f in range(4):
                g = big[:, OD_GV + f, :]
                tt(g, g, rstd[:, :], ALU.subtract).then_inc(sem("centred"), 1)
            wait_emptied(dve, FIRST["var"] + 1)
            own(nc.vector.reciprocal(rstd[:, :], rstd[:, :]))
            for f in range(4):
                g = big[:, OD_GV + f, :]
                own(stt(g, g, param("gmlp_ln_g", f), rstd[:, :], ALU.mult, ALU.mult))
                ts(g, g, param("gmlp_ln_b", f), None, ALU.add).then_inc(sem("ln_ready"), 1)
            for t in range(NT + 1):
                s = drained("vnat1", t)
                r = P if t < NT else TS
                cp(vnn[0:r, t, :], bankA(s, rows=r)).then_inc(out_of["vector"], 1)
            for g in range(4):
                s = drained("z", g)
                tt(xn[:, g, 0:SEQ], bankA(s), big[:, OD_U + g, 0:SEQ], ALU.mult)
                tt(xn[:, g, SEQ:T], bankB(s), big[:, OD_U + g, SEQ:T], ALU.mult).then_inc(out_of["vector"], 1)
            for n in range(2 * R):
                sc = 1.0 if n < R else DR ** -0.5
                x = big[:, OD_RQ + n, :]
                s = drained("rot", n)
                if n:
                    dve.wait_ge(sem("rotated"), n)
                stt(tmp[:, 0:SEQ], bankA(s), sc, cst1("sin", 0, SEQ), ALU.mult, ALU.mult)
                stt(tmp[:, SEQ:T], bankB(s), sc, cst1("sin", SEQ, T), ALU.mult, ALU.mult).then_inc(out_of["vector"], 1)
                own(stt(x, x, sc, cst1("cos"), ALU.mult, ALU.mult))
                tt(x, x, tmp, ALU.add).then_inc(sem("rotated"), 1)
            for t in range(NT + 1):
                s = drained("kn", t)
                r = P if t < NT else TS
                dk = cst1("dec_k" if t < NT else "dec_ks").rearrange("p (h o) -> p h o", o=1).broadcast_to([r, R, P])
                tt(kn[0:r, t, :].rearrange("p (h d) -> p h d", h=R),
                   bankA(s, rows=r).rearrange("p (h d) -> p h d", h=R), dk, ALU.mult).then_inc(out_of["vector"], 1)
            wait_emptied(dve, FIRST["vn"] + NT + 1)
            dve.wait_ge(sem("gv_stored"), 16)
            for n in range(R):
                base = 4 * n
                cols = slice(n * P, (n + 1) * P)
                if n:
                    dve.wait_ge(block_in, FIRST["ret"] + base - 1)
                vv = v2[0:TS, NT, cols].rearrange("p (o e) -> p o e", o=1).broadcast_to([TS, NB, P])
                mb = cst1("of_seq").rearrange("p (b o) -> p b o", o=1).broadcast_to([TS, NB, P])
                tt(vmask, vv, mb, ALU.mult).then_inc(sem("v_spread"), 1)
                s = drained("ret", base)
                if n:
                    wait_emptied(dve, FIRST["ret"] + base)
                dd = cst1("dec", n * P, (n + 1) * P).rearrange("p (o l) -> p o l", o=1).broadcast_to([P, NT, P])
                tt(sct[:, 0:SEQ].rearrange("p (t l) -> p t l", t=NT), bankA(s).rearrange("p (t l) -> p t l", t=NT),
                   dd, ALU.mult)
                tt(sct[0:TS, SEQ:T], bankB(s, rows=TS), cst1("dec_s", n * TS, (n + 1) * TS), ALU.mult)\
                    .then_inc(out_of["vector"], 1)
                q = big[:, OD_RQ + n, :]
                dq = cst1("dec_q", n * P, (n + 1) * P).rearrange("p (o l) -> p o l", o=1)
                qp = q[:, 0:SEQ].rearrange("p (t l) -> p t l", t=NT)
                tt(qp, qp, dq.broadcast_to([P, NT, P]), ALU.mult)
                qs = q[:, SEQ:T].rearrange("p (b l) -> p b l", b=NB)
                tt(qs, qs, dq[:, :, 0:NS].broadcast_to([P, NB, NS]), ALU.mult).then_inc(sem("q_decayed"), 1)
                s = drained("ret", base + 1)
                if n:
                    dve.wait_ge(sem("ret_stored"), 32 * n)
                own(cp(st[:, 0, :], ps[:, 2 * s, 0:P]))
                for t in range(1, NT):
                    ins = stt(st[:, t, :], st[:, t - 1, :], decay_step[0][n], ps[:, 2 * s, t * P:(t + 1) * P],
                              ALU.mult, ALU.add)
                    if t < NT - 1:
                        own(ins)
                ins.then_inc(out_of["vector"], 1)
                wait_emptied(dve, FIRST["ret"] + base + 2)
                dve.sem_inc(sem("states_ready"), 1)
                s = drained("ret", base + 2)
                for a in range(2):
                    ins = stt(s_out[:, 4 * a:4 * a + 4, :].rearrange("p b e -> p (b e)"),
                              s0[:, n, 4 * a:4 * a + 4, :].rearrange("p b e -> p (b e)"), decay_step[1][n],
                              ps[:, 2 * s + a, :], ALU.mult, ALU.add)
                ins.then_inc(out_of["vector"], 1)
                wait_emptied(dve, FIRST["ret"] + base + 3)
                dve.sem_inc(sem("ret_state_ready"), 1)
            for n in range(R):
                o, mu = big[:, OD_RQ + n, :], big[:, OD_RV + n, :]
                wait_emptied(dve, FIRST["hmu"] + n + 1)
                tt(o, o, mu, ALU.subtract).then_inc(sem("hcentred"), 1)
            dve.wait_ge(sem("gate_exp"), 1)
            ex = big[:, OD_RK:OD_RK + R, :]
            own(ts(ex, ex, 1.0, None, ALU.add))
            own(nc.vector.reciprocal(ex, ex))
            own(tt(ex, ex, big[:, OD_RG:OD_RG + R, :], ALU.mult))
            dve.wait_ge(sem("hcentred"), R)
            for n in range(R):
                o, rs = big[:, OD_RQ + n, :], big[:, OD_RV + n, :]
                wait_emptied(dve, FIRST["hvar"] + n + 1)
                own(nc.vector.reciprocal(rs, rs))
                own(stt(rs, rs, param("ret_gn_g", n), o, ALU.mult, ALU.mult))
                own(tt(xn[:, 4 + n, :], rs, big[:, OD_RK + n, :], ALU.mult))
            dve.sem_inc(sem("mixed1"), 1)
            residual("out1")
            norm(3, PROW["norm_ffn"] + KD)
            squares("up1", 32)
            residual("down1")
            norm(4, PROW["norm_final"])
            for t in range(NT + 1):
                s = drained("y", t)
                r = P if t < NT else TS
                if t >= 2:
                    dve.wait_ge(sem(f"y_stored_{t % 2}"), 16 * (t // 2))
                cp(ystage[0:r, t % 2, 0:512], bankA(s, rows=r))
                cp(ystage[0:r, t % 2, 512:DM], bankB(s, 512, r)).then_inc(out_of["vector"], 1)


_INS = ['x_prompt', 'x_sample', 'state_pool', 'cache_k', 'cache_v', 'cache_logf', 'page_table', 'state_ret', 'norm_mix',
        'w_in_even', 'b_forget', 'pool_w', 'pool_scale', 'w_out_even', 'w_in_odd', 'gmlp_ln_g', 'gmlp_ln_b', 'gmlp_ws',
        'gmlp_bs', 'ret_gn_g', 'w_out_odd', 'norm_ffn', 'w_up', 'w_down', 'norm_final']
_OUTS = [("y_prompt", (1, 512, 1024)), ("y_sample", (8, 8, 1024)), ("pool_prompt", (1, 1, 15, 256)),
         ("k_prompt", (1, 1, 512, 12, 64)), ("v_prompt", (1, 1, 512, 12, 64)), ("logf_prompt", (1, 1, 512, 12)),
         ("ret_prompt", (1, 1, 4, 128, 128)), ("pool_sample", (1, 8, 15, 256)), ("k_sample", (1, 8, 8, 12, 64)),
         ("v_sample", (1, 8, 8, 12, 64)), ("logf_sample", (1, 8, 8, 12)), ("gmlp_v_sample", (1, 8, 8, 512)),
         ("ret_sample", (1, 8, 4, 128, 128))]


def kernel(**inputs):
    import numpy as _np
    import concourse.bacc as _bacc
    from concourse import mybir as _mybir
    from concourse.bass_utils import run_bass_kernel_spmd as _run

    nc = _bacc.Bacc("TRN2", target_bir_lowering=False, num_devices=1)
    (tab0, where0), (tab1, where1), step = tables()
    arrays, ins, outs = {}, {}, {}
    for name in _INS:
        arrays[f"in_{name}"] = _np.ascontiguousarray(inputs[name])
    arrays["in_tab0"], arrays["in_tab1"] = tab0, tab1
    for name, a in arrays.items():
        ins[name[3:]] = nc.dram_tensor(name, a.shape, _mybir.dt.from_np(a.dtype), kind="ExternalInput").ap()
    for name, shape in _OUTS:
        outs[name] = nc.dram_tensor(f"out_{name}", shape, _mybir.dt.float32, kind="ExternalOutput").ap()
    hybrid_step(nc, ins, outs, where0, where1, step)
    r = _run(nc, [arrays], core_ids=[0])
    return tuple(r.results[0][f"out_{name}"] for name, _ in _OUTS)
```

```python
import math
from contextlib import ExitStack

import concourse.bass as bass
import numpy as np
from concourse import mybir

F32 = mybir.dt.float32
I32 = mybir.dt.int32
ALU = mybir.AluOpType
ACT = mybir.ActivationFunctionType
AX = mybir.AxisListType

P = 128
DM, SEQ, NB, NS = 1024, 512, 8, 8
TS = NB * NS
T = SEQ + TS
TH = T // 2
PAGES, PAGE, NPHYS = 32, 128, 320
FF = 4096
EPS = 1e-6
NEG = -1e30
KD = DM // P
NT = SEQ // P
H, D = 12, 64
HQ = H * NS
FOX = H * D
HB = FOX // P
R, DR = 4, 128
HIST = 15
EXT = HIST + SEQ
UNIT = KD * 512
RING = 4
GROUP = 4
GROUPS = PAGES // GROUP
LAG = 8
EXPS = GROUPS // 2
JT = HQ // 32
EV = 2572

EV_Q, EV_K, EV_V = 2, 8, 14
OD_U, OD_GV, OD_RQ, OD_RK, OD_RV, OD_RG = 0, 4, 8, 12, 16, 20

PARAMS = [("norm_mix", 16), ("norm_ffn", 16), ("norm_final", 8), ("pool_scale", 2), ("gmlp_ln_g", 4),
          ("gmlp_ln_b", 4), ("ret_gn_g", 4)]
PROW = {}
for _n, _k in PARAMS:
    PROW[_n] = sum(k for _, k in PARAMS[:len(PROW)])
NPARAM = sum(k for _, k in PARAMS)

STAGES = [("x", KD), ("norm0", 1), ("in0", 20), ("logf", 1), ("logfT", 1), ("cum", 1), ("cumT", 1), ("sfxT", 12),
          ("sfx", 6), ("knat", 5), ("vnat", 5), ("g96", 1),
          ("hist", 2), ("out0", 8), ("norm1", 1), ("up0", 32), ("down0", 8),
          ("norm2", 1), ("in1", 24), ("wst", 1), ("w8", 1), ("mu", 1), ("var", 1), ("vnat1", 5), ("z", 4),
          ("rot", 8), ("kn", 5), ("vn", 5), ("ret", 16), ("hmu", 4), ("hvar", 4),
          ("out1", 8), ("norm3", 1), ("up1", 32), ("down1", 8), ("norm4", 1), ("y", 5)]
FIRST = {}
_at = 0
for _n, _k in STAGES:
    FIRST[_n] = _at
    _at += _k

BY_SCALAR = {"norm0", "in0", "cum", "cumT", "sfxT", "sfx", "norm1", "up0", "norm2", "in1", "mu", "var", "vn", "hmu",
             "hvar", "norm3", "up1", "norm4"}
OWNER = []
for _n, _k in STAGES:
    OWNER += ["scalar" if _n in BY_SCALAR or (_n == "ret" and _j % 4 == 3) else "vector" for _j in range(_k)]


def emptied_by(owner, n):
    return sum(o == owner for o in OWNER[:n])


WEIGHTS = [("in0", 5, 4), ("out0", 2, 4), ("up0", 8, 4), ("down0", 8, 1),
           ("in1", 6, 4), ("out1", 2, 4), ("up1", 8, 4), ("down1", 8, 1)]
UFIRST = {}
_at = 0
for _n, _k, _b in WEIGHTS:
    UFIRST[_n] = _at
    _at += _k


def tables():
    p, f = np.arange(P)[:, None], np.arange(P)[None, :]
    q, g = np.arange(TS)[:, None], np.arange(TS)[None, :]
    same = q // NS == g // NS
    one = lambda m: m.astype(np.float32)
    w = np.array([[2, 8], [4, 16]])[(np.arange(P) >= 64).astype(int)]
    cnt = np.minimum(np.arange(16)[None, None, :] + 1, w[:, :, None])
    even = {
        "ident": one(p == f),
        "ones": np.ones((P, P), np.float32),
        "upto": np.concatenate([one(p <= f), np.ones((P, SEQ - P), np.float32)], 1),
        "mask": np.where(f <= p, 0.0, NEG).astype(np.float32),
        "later": one(p > f),
        "later_page": one((p // PAGES == f // PAGES) & (p > f)),
        "upto_s": one(same & (q <= g)),
        "head_of": one(np.arange(H)[:, None] == np.arange(HQ)[None, :] // NS),
        "mask_new": np.where(g % NS <= np.arange(HQ)[:, None] % NS, 0.0, NEG).astype(np.float32),
        "own_query": one(g % NS == np.arange(HQ)[:, None] % NS),
        "mask_seq": np.where(np.arange(2 * TS - NS)[None, :] // NS == NB - 1, 0.0, NEG).repeat(HQ, 0)
        .astype(np.float32),
        "inv_cnt": (1.0 / cnt).astype(np.float32).reshape(P, 32),
        "inv_w": (1.0 / w).astype(np.float32),
    }
    half = DR // 2
    inv = (np.float32(10000.0) ** (-np.arange(half, dtype=np.float32) / np.float32(half))).astype(np.float32)
    pos = np.concatenate([np.arange(SEQ), np.tile(PAGES * PAGE + np.arange(NS), NB)]).astype(np.float32)
    ang = (pos[None, :] * np.concatenate([inv, inv])[:, None]).astype(np.float32)
    lg = np.log1p(-np.exp2(-5.0 - np.arange(R))).astype(np.float32).astype(np.float64)
    dec = lambda n, gap, keep: np.where(keep, np.exp(np.where(keep, gap, 0) * lg[n]), 0.0)
    odd = {
        "cos": np.cos(ang.astype(np.float64)).astype(np.float32),
        "sin": np.sin(ang.astype(np.float64)).astype(np.float32),
        "swap": one(f == p + half) - one(p == f + half),
        "dec": np.concatenate([dec(n, f - p, f >= p) for n in range(R)], 1).astype(np.float32),
        "dec_s": np.concatenate([dec(n, g - q, same & (g >= q)) for n in range(R)], 1).astype(np.float32),
        "dec_q": np.concatenate([np.exp((f + 1) * lg[n]) + 0 * p for n in range(R)], 1).astype(np.float32),
        "dec_k": np.stack([np.exp((P - 1 - np.arange(P)) * lg[n]) for n in range(R)], 1).astype(np.float32),
        "dec_ks": np.stack([np.exp((NS - 1 - np.arange(TS) % NS) * lg[n]) for n in range(R)], 1).astype(np.float32),
        "same_s": one(same),
        "rep": one(np.arange(NS)[:, None] == np.arange(TS)[None, :] % NS),
        "of_seq": one(np.arange(TS)[:, None] // NS == np.arange(NB)[None, :]),
    }
    step = [math.exp(P * float(x)) for x in lg], [math.exp(NS * float(x)) for x in lg]

    def pack(parts):
        width = sum(a.shape[1] for a in parts.values())
        out, at, where = np.zeros((P, width), np.float32), 0, {}
        for name, a in parts.items():
            out[:a.shape[0], at:at + a.shape[1]] = a
            where[name] = (a.shape[0], at, a.shape[1])
            at += a.shape[1]
        return out, where

    return pack(even), pack(odd), step


class Steps:

    def __init__(self, eng, sem):
        self.eng, self.sem, self.n, self.more = eng, sem, 0, 0

    def __call__(self, ins):
        ins.then_inc(self.sem, 1)
        self.n += 1
        self.eng.wait_ge(self.sem, self.n + self.more)

    def loop(self, i, per):
        self.more, self.per, self.start = i * per, per, self.n

    def end(self, times):
        assert self.n - self.start == self.per, (self.n - self.start, self.per)
        self.n, self.more = self.start + self.per * times, 0


def hybrid_step(nc, I, O, where0, where1, decay_step):
    ctx = ExitStack()
    with ctx:
        def sb(name, shape, dt=F32):
            return ctx.enter_context(nc.sbuf_tensor(name, shape, dt))

        sems = {}

        def sem(name):
            if name not in sems:
                sems[name] = ctx.enter_context(nc.semaphore(name))
            return sems[name]

        h = sb("h", [P, KD, T])
        xn = sb("xn", [P, KD, T])
        big = sb("big", [P, 32, T])
        wring = sb("wring", [P, 2, UNIT])
        work = sb("work", [P, 2 * RING * FOX + 2 * 33 * HQ])
        c0 = sb("c0", [P, I["tab0"].shape[1]])
        prow = sb("prow", [NPARAM, P])
        pcol = sb("pcol", [P, NPARAM])
        rstd = sb("rstd", [P, T])
        cumT = sb("cumT", [H, T])
        cumn = sb("cumn", [P, (NT + 1) * H])
        lfn = sb("lfn", [P, (NT + 1) * H])
        ptab = sb("ptab", [1, NB * PAGES], I32)
        pidx = sb("pidx", [P, 2], I32)
        wf = sb("wf", [P, KD, H])
        bf = sb("bf", [H, 1])
        pwd = sb("pwd", [P, 2, P])
        stats = sb("stats", [HQ, 24])
        hstat = sb("hstat", [P, 6 * 4 + 8])
        ps = ctx.enter_context(nc.psum_tensor("ps", [P, 8, 512], F32))

        bigf = big[:, :, :].rearrange("p a t -> p (a t)")
        xnf = xn[:, :, :].rearrange("p a t -> p (a t)")

        def cst(name, lo=0, hi=None, rows=None):
            r, at, w = where0[name]
            return c0[0:rows or r, at + lo:at + (w if hi is None else hi)]

        ident = cst("ident")

        def param(name, j, rows=P):
            return pcol[0:rows, PROW[name] + j:PROW[name] + j + 1]

        def slot(name, j=0):
            return (FIRST[name] + j) % 4

        def bankA(s, n=512, rows=P):
            return ps[0:rows, 2 * s, 0:n]

        def bankB(s, n=TS, rows=P):
            return ps[0:rows, 2 * s + 1, 0:n]

        xstage = bigf[:, 0:NT * DM].rearrange("p (t n) -> p t n", t=NT)
        xstage_s = bigf[0:TS, NT * DM:(NT + 1) * DM]
        at0 = 20 * T
        sfx = bigf[:, at0:at0 + NB * PAGES * H]
        vs = bigf[:, at0 + 3072:at0 + 3840]
        qall = bigf[:, at0 + 3840:at0 + 5376].rearrange("p (b f c) -> p b f c", b=NB, f=HB)
        knew = bigf[:, at0 + 5376:at0 + 5760].rearrange("p (f t) -> p f t", f=HB)
        qcur = bigf[:, at0 + 5760:at0 + 5952].rearrange("p (f c) -> p f c", f=HB)
        key_bias = bigf[0:HQ, at0 + 6336:at0 + 6400]
        qgate = bigf[0:HQ, at0 + 6400:at0 + 6408]
        ostage = bigf[0:HQ, at0 + 6408:at0 + 6664]
        kT = bigf[:, 2 * T:2 * T + 2 * HB * GROUP * PAGE]\
            .rearrange("p (s f n) -> p s f n", s=2, f=HB)
        ptf = 2 * T + 2 * HB * GROUP * PAGE
        pTs = bigf[:, ptf:ptf + (PAGES + 1) * HQ].rearrange("p (g c) -> p g c", c=HQ)
        at1 = EV_V * T
        es = [bigf[:, at1 + 1536 + 368 * n:at1 + 1536 + 368 * (n + 1)].rearrange("p (a b t) -> p a b t", a=2, b=NB)
              for n in range(2)]
        hstage = bigf[0:NB * HIST, at1 + 2272:at1 + 2528]
        hcopy = bigf[:, at1 + 2528:at1 + 2768].rearrange("p (a t) -> p a t", a=2)
        hout = bigf[0:NB * HIST, at1 + 2768:at1 + 3024]
        hout_p = bigf[0:HIST, at1 + 3024:at1 + 3280]
        W1 = 2 * RING * FOX
        k_ring = work[:, 0:RING * FOX].rearrange("p (s n) -> p s n", s=RING)
        v_ring = work[:, RING * FOX:W1].rearrange("p (s n) -> p s n", s=RING)
        W2 = W1 + 33 * HQ
        S = work[0:HQ, W1:W1 + PAGES * PAGE + TS]
        SG = W1 + PAGES * PAGE + TS
        sgate = work[:, SG:SG + 2 * GROUP * HQ].rearrange("p (s c) -> p s c", s=2)
        lg = work[:, 0:3072].rearrange("p (a s h) -> p a s h", a=2, h=H)
        kstage = work[:, 3072:4608].rearrange("p (s n) -> p s n", s=2)
        lT = xnf[:, 0:3072].rearrange("p (a h g) -> p a h g", a=2, h=H)
        lcT = work[:, W1:W1 + 3072].rearrange("p (a h g) -> p a h g", a=2, h=H)
        z = [work[0:H, W2 + T * n:W2 + T * (n + 1)] for n in range(4)]
        vn0 = work[:, W2:W2 + NT * FOX].rearrange("p (t n) -> p t n", t=NT)
        tb = work[:, W1:W1 + 1024].rearrange("p (s n) -> p s n", s=2)
        ep = [work[:, W1 + 1024:W1 + 1024 + 2 * EXT].rearrange("p (a t) -> p a t", a=2),
              bigf[:, at1:at1 + 2 * EXT].rearrange("p (a t) -> p a t", a=2)]
        eb = work[:, 0:1024].rearrange("p (s n) -> p s n", s=2)
        pT = work[:, 1024:5120].rearrange("p (s j n) -> p s j n", s=2, j=NT)
        ckb = work[:, 5120:6144].rearrange("p (s n) -> p s n", s=2)
        col = lambda n, w=1: stats[:, n:n + w]
        smax, gmax, gfull, sshift, ssum, sden, srec = col(0, 9), col(9), col(10), col(11), col(12, 5), col(17), col(18)
        c1 = work[:, 0:I["tab1"].shape[1]]
        O1 = I["tab1"].shape[1]

        def cst1(name, lo=0, hi=None, rows=None):
            r, at, w = where1[name]
            return c1[0:rows or r, at + lo:at + (w if hi is None else hi)]

        def take(n):
            nonlocal O1
            O1 += n
            assert O1 <= 2 * RING * FOX + 2 * 33 * HQ
            return work[:, O1 - n:O1]

        wsn = take(512).rearrange("p (g s) -> p g s", g=4)
        vnn = take(2560).rearrange("p (t n) -> p t n", t=NT + 1)
        vmask = vnn.rearrange("p t n -> p (t n)")[0:TS, 0:1024].rearrange("p (b e) -> p b e", b=NB)
        s_out = vnn.rearrange("p t n -> p (t n)")[:, 1024:2048].rearrange("p (b e) -> p b e", b=NB)
        kn = take(2560).rearrange("p (t n) -> p t n", t=NT + 1)
        v2 = take(2560).rearrange("p (t n) -> p t n", t=NT + 1)
        sct = take(T)
        st = bigf[:, 24 * T + 4096:24 * T + 4608].rearrange("p (n e) -> p n e", n=NT)
        s0 = bigf[:, 24 * T:24 * T + 4096].rearrange("p (h b e) -> p h b e", h=R, b=NB)
        wT = take(512).rearrange("p (g t) -> p g t", g=4)
        w8 = take(256)[0:TS, :].rearrange("p (g t) -> p g t", g=4)
        bsr = cumT[0:1, 0:512]
        tmp = sct
        ystage = bigf[:, 0:2 * DM].rearrange("p (s n) -> p s n", s=2)

        block_in = sem("block_filled")
        out_of = {"scalar": sem("emptied_by_scalar"), "vector": sem("emptied_by_vector")}

        def wait_emptied(eng, n):
            eng.wait_ge(out_of[OWNER[n - 1]], emptied_by(OWNER[n - 1], n))

        w_in = [sem("weights_in_0"), sem("weights_in_1")]
        k_in = [sem(f"k_page_in_{n}") for n in range(RING)]
        v_in = [sem(f"v_page_in_{n}") for n in range(RING)]

        blk = ctx.enter_context(nc.Block())

        @blk.sync
        def _(sp):
            sp.dma_start(xstage, I["x_prompt"][0].rearrange("(t p) n -> p t n", p=P)).then_inc(sem("x_in"), 16)
            sp.dma_start(xstage_s, I["x_sample"].rearrange("b s n -> (b s) n")).then_inc(sem("x_in"), 16)
            sp.dma_start(ptab[:, :], I["page_table"].rearrange("b g -> (b g)").rearrange("(o n) -> o n", o=1))\
                .then_inc(sem("ptab_in"), 16)

            def unit(stage, j):
                u = UFIRST[stage] + j
                if u >= 2:
                    for name, n, per in WEIGHTS:
                        if UFIRST[name] <= u - 2 < UFIRST[name] + n:
                            sp.wait_ge(block_in, FIRST[name] + (u - 2 - UFIRST[name] + 1) * per)
                layer = int(stage[-1])
                if stage[:-1] == "down":
                    src = I["w_down"][layer, :, j * P:(j + 1) * P].rearrange("(k p) n -> p k n", p=P)
                    dst = wring[:, u % 2, :].rearrange("p (k n) -> p k n", n=P)
                else:
                    w = {"in0": I["w_in_even"][0], "out0": I["w_out_even"][0], "in1": I["w_in_odd"][0],
                         "out1": I["w_out_odd"][0], "up0": I["w_up"][0], "up1": I["w_up"][1]}[stage]
                    src = w[:, j * 512:(j + 1) * 512].rearrange("(k p) n -> p k n", p=P)
                    dst = wring[:, u % 2, :].rearrange("p (k n) -> p k n", n=512)
                sp.dma_start(dst, src).then_inc(w_in[u % 2], 16)

            for j in range(5):
                unit("in0", j)
            unit("out0", 0)
            unit("out0", 1)

            sp.wait_ge(sem("ptab_in"), 16)
            sp.wait_ge(sem("fox_prompt_done"), H)

            def page_ids(b, p):
                _, ids = nc.values_load_multi_w_load_instructions(
                    ptab[0:1, bass.ds(b * PAGES + p, RING)], engines=[mybir.EngineType.SP], min_val=0,
                    max_val=NPHYS - 1)
                return ids

            def page(cache, b, p, ids):
                ring, arrived, used = (k_ring, k_in, sem("k_page_used")) if cache == "cache_k" else \
                    (v_ring, v_in, sem("v_page_used"))
                if not isinstance(b, int) or b * PAGES + p >= RING:
                    sp.wait_ge(used, b * PAGES + p - RING + 1)
                sp.dma_start(ring[:, p % RING, :],
                             I[cache][0, bass.ds(ids[p % RING], 1)].rearrange("o p h d -> (o p) (h d)"))\
                    .then_inc(arrived[p % RING], 16)

            def phase(c, k=True, ending=True, starting=True):
                for p in range(0, PAGES, RING):
                    if k:
                        k_ids = page_ids(c, p)
                    v, q = (c - 2, PAGES - LAG + p) if p < LAG else (c - 1, p - LAG)
                    with_v = ending if p < LAG else starting
                    if with_v:
                        v_ids = page_ids(v, q)
                    for m in range(RING):
                        if k:
                            page("cache_k", c, p + m, k_ids)
                        if with_v:
                            page("cache_v", v, q + m, v_ids)

            phase(0, ending=False, starting=False)
            phase(1, ending=False)
            with sp.Fori(2, NB) as c:
                phase(c)
            phase(NB, k=False)
            for q in range(PAGES - LAG, PAGES, RING):
                ids = page_ids(NB - 1, q)
                for m in range(RING):
                    page("cache_v", NB - 1, q + m, ids)

            for name, n, _ in WEIGHTS[2:]:
                for j in range(n):
                    unit(name, j)

        @blk.gpsimd
        def _(pool):
            own = Steps(pool, sem("pool_steps"))
            pool.dma_start(c0[:, :], I["tab0"]).then_inc(sem("tab0_in"), 16)
            for name, n in PARAMS:
                src = I[name]
                while len(src.shape) > 1:
                    src = src.rearrange("a b -> (a b)")
                pool.dma_start(prow[PROW[name]:PROW[name] + n, :], src.rearrange("(r c) -> r c", c=P))\
                    .then_inc(sem("params_in"), 16)
            pool.dma_start(wf[:, :, :], I["w_in_even"][0, :, EV - H:EV].rearrange("(k p) n -> p k n", p=P))\
                .then_inc(sem("wf_in"), 16)
            pool.dma_start(bf[:, :], I["b_forget"].rearrange("o h -> h o")).then_inc(sem("wf_in"), 16)
            for a in range(2):
                rows = I["page_table"][4 * a:4 * a + 4, :].rearrange("b g -> (b g)").rearrange("(n o) -> n o", o=1)
                pool.dma_start(pidx[:, a:a + 1], rows).then_inc(sem("pidx_in"), 16)
            own(pool.memset(pwd[:, :, :], 0.0))
            for g in range(4):
                r = slice(64 * (g % 2), 64 * (g % 2) + 64)
                pool.dma_start(pwd[r, g // 2, r], I["pool_w"][0, g]).then_inc(sem("pwd_in"), 16)
            pool.wait_ge(sem("pidx_in"), 32)
            flat = I["cache_logf"][0].rearrange("n s h -> n (s h)")
            for a in range(2):
                pool.indirect_dma_start(lg[:, a].rearrange("p s h -> p (s h)"), None, flat,
                                        bass.IndirectOffsetOnAxis(ap=pidx[:, a:a + 1], axis=0))\
                    .then_inc(sem("lg_in"), 16)

            pool.wait_ge(sem("lfn_ready"), 1)
            pool.dma_start(O["logf_prompt"][0, 0].rearrange("(t p) h -> p t h", p=P),
                           lfn[:, 0:NT * H].rearrange("p (t h) -> p t h", h=H)).then_inc(sem("stored"), 16)
            pool.dma_start(O["logf_sample"][0].rearrange("b s h -> (b s) h"), lfn[0:TS, NT * H:(NT + 1) * H])\
                .then_inc(sem("stored"), 16)
            kp = O["k_prompt"][0, 0].rearrange("(t p) h d -> t p (h d)", p=P)
            for t in range(NT + 1):
                wait_emptied(pool, FIRST["knat"] + t + 1)
                dst = kp[t] if t < NT else O["k_sample"][0].rearrange("b s h d -> (b s) (h d)")
                pool.dma_start(dst, kstage[0:P if t < NT else TS, t % 2, :]).then_inc(sem(f"k_stored_{t % 2}"), 16)
            wait_emptied(pool, FIRST["vnat"] + NT)
            pool.dma_start(O["v_prompt"][0, 0].rearrange("(t p) h d -> p t (h d)", p=P), vn0)\
                .then_inc(sem("v_stored"), 16)
            wait_emptied(pool, FIRST["vnat"] + NT + 1)
            pool.dma_start(O["v_sample"][0].rearrange("b s h d -> (b s) (h d)"), vs[0:TS, :])\
                .then_inc(sem("v_stored"), 16)
            pool.dma_start(hstage, I["state_pool"][0].rearrange("b t c -> (b t) c")).then_inc(sem("hist_in"), 16)

            own(pool.memset(ep[0][:, :, 0:HIST], 0.0))
            own(pool.tensor_copy(ep[0][:, :, HIST:EXT], big[:, 0:2, 0:SEQ]))
            add = lambda o, a, b: own(pool.tensor_tensor(o, a, b, ALU.add))

            def group(src, rows, a):
                inv = cst("inv_w", a, a + 1)[rows, :]
                dst = xn[rows, a, 0:SEQ]
                own(pool.tensor_scalar(dst, src[rows, a, HIST:EXT], inv, None, ALU.mult))
                own(pool.tensor_tensor(xn[rows, a, 0:16], src[rows, a, HIST:HIST + 16],
                                       cst("inv_cnt", 16 * a, 16 * a + 16)[rows, :], ALU.mult))
                own(pool.tensor_tensor(dst, dst, big[rows, a, 0:SEQ], ALU.subtract))

            def group_s(src, rows, a):
                inv = cst("inv_w", a, a + 1)[rows, :]
                dst = xn[rows, a, SEQ:T].rearrange("p (b s) -> p b s", b=NB)
                own(pool.tensor_scalar(dst, src[rows, a, :, HIST:HIST + NS], inv, None, ALU.mult))
                own(pool.tensor_tensor(dst, dst, big[rows, a, SEQ:T].rearrange("p (b s) -> p b s", b=NB),
                                       ALU.subtract))

            lo, hi = slice(0, 64), slice(64, 128)
            e, f = ep
            add(f[:, :, 1:EXT], e[:, :, 1:EXT], e[:, :, 0:EXT - 1])
            group(f, lo, 0)
            add(e[:, :, 3:EXT], f[:, :, 3:EXT], f[:, :, 1:EXT - 2])
            group(e, hi, 0)
            add(f[:, 1, 7:EXT], e[:, 1, 7:EXT], e[:, 1, 3:EXT - 4])
            group(f, lo, 1)
            add(e[:, 1, 15:EXT], f[:, 1, 15:EXT], f[:, 1, 7:EXT - 8])
            group(e, hi, 1)
            pool.wait_ge(sem("ext_s_ready"), 2)
            e, f = es
            N = HIST + NS
            add(f[:, :, :, 1:N], e[:, :, :, 1:N], e[:, :, :, 0:N - 1])
            group_s(f, lo, 0)
            add(e[:, :, :, 3:N], f[:, :, :, 3:N], f[:, :, :, 1:N - 2])
            group_s(e, hi, 0)
            add(f[:, 1, :, 7:N], e[:, 1, :, 7:N], e[:, 1, :, 3:N - 4])
            group_s(f, lo, 1)
            add(e[:, 1, :, 15:N], f[:, 1, :, 15:N], f[:, 1, :, 7:N - 8])
            group_s(e, hi, 1)
            own(pool.memset(hstat[0:1, 24:25], 0.0))
            pool.memset(hstat[0:1, 25:26], 0.0).then_inc(sem("pool_d_ready"), 1)
            pool.wait_ge(sem("hist_out_ready"), 1)
            pool.dma_start(O["pool_sample"][0].rearrange("b t c -> (b t) c"), hout).then_inc(sem("stored"), 16)
            pool.dma_start(O["pool_prompt"][0, 0], hout_p).then_inc(sem("stored"), 16)

            pool.wait_ge(sem("outputs_placed"), NB + 1)
            pool.wait_ge(sem("v_stored"), 32)
            pool.dma_start(c1, I["tab1"]).then_inc(sem("tab1_in"), 16)
            pool.dma_start(bsr, I["gmlp_bs"].rearrange("o g t -> o (g t)")).then_inc(sem("bs_in"), 16)
            pool.dma_start(wsn, I["gmlp_ws"][0].rearrange("g t s -> t g s")).then_inc(sem("ws_in"), 16)
            pool.wait_ge(block_in, FIRST["down0"] + 8)
            for n in range(R):
                pool.dma_start(s0[:, n], I["state_ret"][0, :, n].rearrange("b d e -> d b e")).then_inc(sem("s0_in"), 16)
            wait_emptied(pool, FIRST["vnat1"] + NT + 1)
            pool.dma_start(O["gmlp_v_sample"][0].rearrange("b s c -> (b s) c"), vnn[0:TS, NT, :])\
                .then_inc(sem("gv_stored"), 16)
            for n in range(R):
                pool.wait_ge(sem("ret_state_ready"), n + 1)
                pool.dma_start(O["ret_prompt"][0, 0, n], st[:, NT - 1, :]).then_inc(sem("ret_stored"), 16)
                pool.dma_start(O["ret_sample"][0, :, n].rearrange("b d e -> d b e"), s_out)\
                    .then_inc(sem("ret_stored"), 16)
            yp = O["y_prompt"][0].rearrange("(t p) n -> t p n", p=P)
            for t in range(NT + 1):
                wait_emptied(pool, FIRST["y"] + t + 1)
                dst = yp[t] if t < NT else O["y_sample"].rearrange("b s n -> (b s) n")
                pool.dma_start(dst, ystage[0:P if t < NT else TS, t % 2, :]).then_inc(sem(f"y_stored_{t % 2}"), 16)
            pool.wait_ge(sem("stored"), 64)
            pool.wait_ge(sem("k_stored_0"), 48)
            pool.wait_ge(sem("k_stored_1"), 32)
            pool.wait_ge(sem("gv_stored"), 16)
            pool.wait_ge(sem("ret_stored"), 32 * R)
            pool.wait_ge(sem("y_stored_0"), 48)
            pool.wait_ge(sem("y_stored_1"), 32)

        @blk.tensor
        def _(pe):
            mm = nc.tensor.matmul
            tr = nc.tensor.transpose

            def open_block(n):
                if n >= 4:
                    wait_emptied(pe, n - 3)

            def gemm(stage, rhs, ready=None):
                _, units, per = next(w for w in WEIGHTS if w[0] == stage)
                ks = UNIT // (512 if per == 4 else P)
                body = 2 if per == 4 else 4

                def unit(j, i, first=False):
                    u = UFIRST[stage] + j
                    pe.wait_ge(w_in[u % 2], 16 * (u // 2 + 1) + i * (16 * body // 2))
                    for m in range(per):
                        n = j * per + m
                        s = slot(stage, n)
                        if isinstance(i, int):
                            open_block(FIRST[stage] + n)
                        else:
                            who = OWNER[FIRST[stage]]
                            pe.wait_ge(out_of[who], i * (body * per) + emptied_by(who, FIRST[stage]) + n - 3)
                        for k in range(ks):
                            if first and m == 0 and ready:
                                pe.wait_ge(sem(ready[0]), ready[1] + k + 1)
                            at = k * (512 if per == 4 else P) + m * P
                            w = wring[:, u % 2, at:at + P]
                            mm(bankA(s, TH), w, rhs[:, k, 0:TH], start=(k == 0), stop=(k == ks - 1))
                            last = mm(bankB(s, TH), w, rhs[:, k, TH:T], start=(k == 0), stop=(k == ks - 1))
                        last.then_inc(block_in, 1)

                j = 0
                if ready:
                    for j in range(body):
                        unit(j, 0, first=(j == 0))
                    j = body
                loops = (units - j) // body
                if loops > 1:
                    for n in range(4 if j == 0 else 0):
                        open_block(FIRST[stage] + n)
                    with pe.Fori(0, loops) as i:
                        for m in range(body):
                            unit(j + m, i)
                elif loops == 1:
                    for m in range(body):
                        unit(j + m, 0)
                for m in range(j + loops * body, units):
                    unit(m, 0)

            def ones_sum(stage, j, ready, base, src, ks, rows_of=None):
                s = slot(stage, j)
                open_block(FIRST[stage] + j)
                for k in range(ks):
                    pe.wait_ge(sem(ready), base + k + 1)
                    mm(bankA(s, TH), cst("ones"), src[:, k, 0:TH], start=(k == 0), stop=(k == ks - 1))
                    last = mm(bankB(s, TH), cst("ones"), src[:, k, TH:T], start=(k == 0), stop=(k == ks - 1))
                last.then_inc(block_in, 1)

            pe.wait_ge(sem("tab0_in"), 16)
            pe.wait_ge(sem("x_in"), 32)
            for f in range(KD):
                s = slot("x", f)
                open_block(f)
                for t in range(NT):
                    tr(ps[:, 2 * s, t * P:(t + 1) * P], xstage[:, t, f * P:(f + 1) * P], ident)
                tr(bankB(s), xstage_s[:, f * P:(f + 1) * P], ident[0:TS, 0:TS]).then_inc(block_in, 1)
            pe.wait_ge(sem("params_in"), 16 * len(PARAMS))
            wait_emptied(pe, KD)
            tr(ps[:, 7, 0:NPARAM], prow[:, :], ident[0:NPARAM, 0:NPARAM]).then_inc(sem("params_turned"), 1)
            ones_sum("norm0", 0, "sq_ready", 0, xn, KD)
            pe.wait_ge(sem("params_ready"), 1)
            gemm("in0", xn, ("xn_ready", 0))

            s = slot("logf")
            open_block(FIRST["logf"])
            pe.wait_ge(sem("wf_in"), 32)
            for k in range(KD):
                mm(bankA(s, TH, H), wf[:, k, :], xn[:, k, 0:TH], start=(k == 0), stop=(k == KD - 1))
                last = mm(bankB(s, TH, H), wf[:, k, :], xn[:, k, TH:T], start=(k == 0), stop=(k == KD - 1))
            last.then_inc(block_in, 1)

            def heads_to_tokens(stage, src):
                s = slot(stage)
                open_block(FIRST[stage])
                for t in range(NT):
                    tr(ps[:, 2 * s, t * H:(t + 1) * H], src[0:H, t * P:(t + 1) * P], ident[0:H, 0:H])
                tr(bankB(s, H, TS), src[0:H, SEQ:T], ident[0:H, 0:H]).then_inc(block_in, 1)

            pe.wait_ge(sem("logf_ready"), 1)
            heads_to_tokens("logfT", z[3])
            pe.wait_ge(sem("lfn_ready"), 1)
            s = slot("cum")
            open_block(FIRST["cum"])
            for t in range(NT):
                mm(ps[0:H, 2 * s, t * P:SEQ], lfn[:, t * H:(t + 1) * H], cst("upto", 0, SEQ - t * P),
                   start=(t == 0), stop=(t == NT - 1))
            mm(bankB(s, rows=H), lfn[0:TS, NT * H:(NT + 1) * H], cst("upto_s"), start=True, stop=True)\
                .then_inc(block_in, 1)
            wait_emptied(pe, FIRST["cum"] + 1)
            heads_to_tokens("cumT", cumT)

            pe.wait_ge(sem("lg_in"), 32)
            for n in range(H):
                s = slot("sfxT", n)
                open_block(FIRST["sfxT"] + n)
                for a in range(2):
                    page = lg[:, a, :, n]
                    mm(ps[:, 2 * s, a * P:(a + 1) * P], page, ident, start=True, stop=True)
                    last = mm(ps[:, 2 * s + 1, a * P:(a + 1) * P], page, cst("later_page"), start=True, stop=True)
                last.then_inc(block_in, 1)
            lf = lT.rearrange("p a h g -> p (a h g)")
            lcf = lcT.rearrange("p a h g -> p (a h g)")
            wait_emptied(pe, FIRST["sfxT"] + H)
            for n in range(6):
                s = slot("sfx", n)
                open_block(FIRST["sfx"] + n)
                mm(bankA(s), cst("later"), lf[:, n * 512:(n + 1) * 512], start=True, stop=False)
                mm(bankA(s), cst("ones"), lcf[:, n * 512:(n + 1) * 512], start=False, stop=True).then_inc(block_in, 1)

            for stage, first in (("knat", EV_K), ("vnat", EV_V)):
                for t in range(NT + 1):
                    s = slot(stage, t)
                    open_block(FIRST[stage] + t)
                    rows, cols = (P, slice(t * P, (t + 1) * P)) if t < NT else (TS, slice(SEQ, T))
                    for f in range(HB):
                        at = f * P
                        last = tr(ps[0:rows, 2 * s + at // 512, at % 512:at % 512 + P], big[:, first + f, cols], ident)
                    last.then_inc(block_in, 1)

            s = slot("g96")
            open_block(FIRST["g96"])
            mm(ps[0:HQ, 2 * s, 0:TS], cst("head_of"), cumT[0:H, SEQ:T], start=True, stop=True).then_inc(block_in, 1)

            wait_emptied(pe, FIRST["g96"] + 1)
            NSTEP = H * NT

            def key_gates(hd):
                if hd >= 1:
                    pe.wait_ge(sem("gates_copied"), hd)
                mm(ps[:, 7, :], ident[0:H, hd:hd + 1].broadcast_to([H, P]), cumT[0:H, 0:SEQ], start=True, stop=True)\
                    .then_inc(sem("gates_spread"), 1)

            def turn(n):
                hd, i = n // NT, n % NT
                pe.wait_ge(sem("probs_scaled"), n + 1)
                if n >= 3:
                    pe.wait_ge(sem("probs_turned_copied"), n - 2)
                for j in range(i + 1):
                    last = tr(ps[:, 3 + n % 3, j * P:(j + 1) * P], eb[:, n % 2, j * P:(j + 1) * P], ident)
                last.then_inc(sem("probs_turned"), 1)

            def weigh(hd):
                pe.wait_ge(sem("probs_turned_copied"), NT * (hd + 1))
                if hd >= 1:
                    pe.wait_ge(sem("fox_prompt_done"), hd)
                r = slice(64 * (hd % 2), 64 * (hd % 2) + 64)
                for j in range(NT):
                    last = mm(ps[r, 6, j * P:SEQ], vn0[:, j, hd * D:(hd + 1) * D], pT[:, hd % 2, j, j * P:SEQ],
                              start=(j == 0), stop=(j == NT - 1))
                last.then_inc(sem("fox_prompt_out"), 1)

            key_gates(0)
            for n in range(NSTEP + 4):
                if n < NSTEP:
                    hd, i = n // NT, n % NT
                    r = slice(64 * (hd % 2), 64 * (hd % 2) + 64)
                    if i == 1 and hd + 1 < H:
                        key_gates(hd + 1)
                    if n >= 3:
                        pe.wait_ge(sem("scores_read"), n - 2)
                    mm(ps[:, n % 3, 0:(i + 1) * P], big[r, EV_Q + hd // 2, i * P:(i + 1) * P],
                       big[r, EV_K + hd // 2, 0:(i + 1) * P], start=True, stop=True).then_inc(sem("scores_made"), 1)
                if 2 <= n < NSTEP + 2:
                    turn(n - 2)
                if n >= 3 and (n - 3) % NT == NT - 1:
                    weigh((n - 3) // NT)

            pe.wait_ge(sem("fox_prompt_done"), H)
            pe.wait_ge(sem("hist_in"), 16)
            for a in range(2):
                s = slot("hist", a)
                last = tr(ps[:, 2 * s, 0:NB * HIST], hstage[:, a * P:(a + 1) * P], ident[0:NB * HIST, 0:NB * HIST])
                last.then_inc(block_in, 1)
            pe.wait_ge(sem("pwd_in"), 64)
            pe.wait_ge(sem("pool_d_ready"), 1)
            s = 3
            for a in range(2):
                wait_emptied(pe, FIRST["hist"] + 2) if a == 0 else None
                mm(ps[:, 4 + a, :], pwd[:, a, :], xn[:, a, 0:SEQ], start=True, stop=True)
                last = mm(ps[:, 6 + a, 0:TS], pwd[:, a, :], xn[:, a, SEQ:T], start=True, stop=True)
            last.then_inc(sem("pooled"), 1)
            pe.wait_ge(sem("hist_copied"), 1)
            for a in range(2):
                tr(ps[0:NB * HIST, a, 0:P], hcopy[:, a, :], ident)
                last = tr(ps[0:HIST, a, P:2 * P], big[:, a, SEQ - HIST:SEQ], ident)
            last.then_inc(sem("hist_turned"), 1)

            pe.wait_ge(sem("hist_out_ready"), 1)
            pe.wait_ge(sem("pool_mixed"), 1)
            pe.wait_ge(sem("queries_placed"), 2)
            pe.wait_ge(sem("v_stored"), 32)

            def turn_page(b, p):
                k = b * PAGES + p
                pe.wait_ge(k_in[p % RING], 16 * (b * (PAGES // RING) + p // RING + 1))
                static = isinstance(b, int)
                if not static or k >= 2:
                    pe.wait_ge(sem("kT_low"), k - 1)
                    pe.wait_ge(sem("kT_high"), k - 1)
                for f in range(HB):
                    at = f * P
                    last = tr(ps[:, 2 * (p % 2) + at // 512, at % 512:at % 512 + P],
                              k_ring[:, p % RING, at:at + P], ident)
                last.then_inc(sem("k_page_used"), 1)

            def score_group(b, g):
                first = isinstance(b, int) and b == 0
                pe.wait_ge(sem("kT_low"), b * PAGES + (g + 1) * GROUP)
                pe.wait_ge(sem("kT_high"), b * PAGES + (g + 1) * GROUP)
                if g == 0:
                    pe.wait_ge(sem("queries_staged"), b + 1)
                pe.wait_ge(sem("suffix_staged"), b * GROUPS + g + 1)
                if g >= 2:
                    pe.wait_ge(sem("scores_in"), b * (GROUPS + 1) + g - 1)
                elif not first:
                    pe.wait_ge(sem("scores_in"), b * (GROUPS + 1))
                bank = 4 + g % 2
                for half in range(2):
                    for j in range(JT):
                        mm(ps[32 * j:32 * j + 32, bank, :], qcur[:, 2 * j + half, :], kT[:, g % 2, 2 * j + half, :],
                           start=(half == 0), stop=False)
                for m in range(GROUP):
                    for j in range(JT):
                        at = m * HQ + 32 * j
                        last = mm(ps[32 * j:32 * j + 32, bank, m * PAGE:(m + 1) * PAGE],
                                  sgate[:, g % 2, at:at + 32], ident, start=False, stop=(m == GROUP - 1))
                last.then_inc(sem("groups_scored"), 1)

            def score_new(b):
                pe.wait_ge(sem("scores_in"), b * (GROUPS + 1) + GROUPS - 1)
                for half in range(2):
                    for j in range(JT):
                        last = mm(ps[32 * j:32 * j + 32, 4, 0:TS], qcur[:, 2 * j + half, :], knew[:, 2 * j + half, :],
                                  start=(half == 0), stop=(half == 1))
                last.then_inc(sem("new_scored"), 1)

            def turn_probs(b, g):
                pe.wait_ge(sem("exp_done"), b * (EXPS + 1) + g // 2 + 1)
                if g:
                    pe.wait_ge(sem("probs_in"), b * (GROUPS + 1) + g)
                elif not (isinstance(b, int) and b == 0):
                    pe.wait_ge(sem("outputs_placed"), b)
                if g == GROUPS:
                    last = mm(ps[0:TS, 6, 0:HQ], S[:, PAGES * PAGE:PAGES * PAGE + TS], ident[0:HQ, 0:HQ],
                              start=True, stop=True)
                else:
                    for m in range(GROUP):
                        at = (g * GROUP + m) * PAGE
                        last = tr(ps[:, 6, m * HQ:(m + 1) * HQ], S[:, at:at + PAGE], ident[0:HQ, 0:HQ])
                last.then_inc(sem("probs_turned_s"), 1)

            def turn_out(b):
                pe.wait_ge(sem("out_scaled"), b + 1)
                if not isinstance(b, int) or b < NB - 1:
                    pe.wait_ge(sem("probs_in"), (b + 2) * (GROUPS + 1))
                else:
                    pe.wait_ge(sem("outputs_placed"), NB)
                for c in range(2):
                    last = tr(ps[:, 6, c * HQ:(c + 1) * HQ], ostage[:, c * P:(c + 1) * P], ident[0:HQ, 0:HQ])
                last.then_inc(sem("out_turned"), 1)

            def weigh_page(b, p):
                if p == 0 and not (isinstance(b, int) and b == 0):
                    pe.wait_ge(sem("out_scaled"), b)
                if p < PAGES:
                    pe.wait_ge(v_in[p % RING], 16 * (b * (PAGES // RING) + p // RING + 1))
                if p % GROUP == 0:
                    pe.wait_ge(sem("probs_in"), b * (GROUPS + 1) + p // GROUP + 1)
                for j in range(JT):
                    v = v_ring[:, p % RING, 256 * j:256 * j + 256] if p < PAGES else vs[:, 256 * j:256 * j + 256]
                    last = mm(ps[32 * j:32 * j + 32, 7, 0:256], pTs[:, p, 32 * j:32 * j + 32], v,
                              start=(p == 0), stop=(p == PAGES))
                last.then_inc(sem("v_page_used") if p < PAGES else sem("fox_sample_out"), 1)

            def phase(c, k=True, ending=True, starting=True):
                for p in range(PAGES):
                    if k:
                        turn_page(c, p)
                        if p >= GROUP and p % GROUP == 0:
                            score_group(c, p // GROUP - 1)
                    if p < LAG and ending:
                        weigh_page(c - 2, PAGES - LAG + p)
                        if p == LAG - 1:
                            weigh_page(c - 2, PAGES)
                    if p >= LAG and starting:
                        weigh_page(c - 1, p - LAG)
                    if starting and 3 <= p < 3 + GROUPS + 1:
                        turn_probs(c - 1, p - 3)
                    if ending and p == 14:
                        turn_out(c - 2)
                if k:
                    score_group(c, GROUPS - 1)
                    score_new(c)

            phase(0, ending=False, starting=False)
            phase(1, ending=False)
            with pe.Fori(2, NB) as c:
                phase(c)
            phase(NB, k=False)
            for q in range(PAGES - LAG, PAGES + 1):
                weigh_page(NB - 1, q)
            turn_out(NB - 1)

            pe.wait_ge(sem("outputs_placed"), NB + 1)
            gemm("out0", xn)
            ones_sum("norm1", 0, "sq_ready", KD, big, KD)
            gemm("up0", xn, ("xn_ready", KD))
            gemm("down0", big, ("u_ready", 0))

            ones_sum("norm2", 0, "sq_ready", 2 * KD, xn, KD)
            gemm("in1", xn, ("xn_ready", 2 * KD))
            s = slot("wst")
            open_block(FIRST["wst"])
            pe.wait_ge(sem("ws_in"), 16)
            for g in range(4):
                last = tr(ps[:, 2 * s, g * P:(g + 1) * P], wsn[:, g, :], ident)
            last.then_inc(block_in, 1)
            s = slot("w8")
            open_block(FIRST["w8"])
            wait_emptied(pe, FIRST["wst"] + 1)
            pe.wait_ge(sem("tab1_in"), 16)
            mm(ps[0:TS, 2 * s, 0:4 * NS], cst1("rep"), wT[0:NS, :, 0:NS], start=True, stop=True).then_inc(block_in, 1)
            ones_sum("mu", 0, "emptied_by_scalar", emptied_by("scalar", FIRST["in1"] + OD_GV), big[:, OD_GV:OD_GV + 4, :], 4)
            ones_sum("var", 0, "lnsq_ready", 0, xn[:, 4:8, :], 4)
            pe.wait_ge(sem("ln_ready"), 4)
            for t in range(NT + 1):
                s = slot("vnat1", t)
                open_block(FIRST["vnat1"] + t)
                rows, cols = (P, slice(t * P, (t + 1) * P)) if t < NT else (TS, slice(SEQ, T))
                for f in range(4):
                    last = tr(ps[0:rows, 2 * s, f * P:(f + 1) * P], big[:, OD_GV + f, cols], ident)
                last.then_inc(block_in, 1)
            pe.wait_ge(sem("bs_in"), 16)
            wait_emptied(pe, FIRST["vnat1"] + NT + 1)
            for g in range(4):
                s = slot("z", g)
                open_block(FIRST["z"] + g)
                bias = bsr[0:1, g * P:(g + 1) * P].rearrange("p (o t) -> p o t", o=1)
                mm(bankA(s), cst("ones", rows=1), bias.broadcast_to([1, NT, P]), start=True, stop=False)
                for t in range(NT):
                    mm(ps[:, 2 * s, t * P:(t + 1) * P], vnn[:, t, g * P:(g + 1) * P], wT[:, g, :],
                       start=False, stop=(t == NT - 1))
                mm(bankB(s), cst("ones", rows=1), bias[:, :, 0:NS].broadcast_to([1, NB, NS]), start=True, stop=False)
                mm(bankB(s), vnn[0:TS, NT, g * P:(g + 1) * P], w8[:, g, :], start=False, stop=True)\
                    .then_inc(block_in, 1)
            for n in range(2 * R):
                s = slot("rot", n)
                open_block(FIRST["rot"] + n)
                mm(bankA(s, TH), cst1("swap"), big[:, OD_RQ + n, 0:TH], start=True, stop=True)
                mm(bankB(s, TH), cst1("swap"), big[:, OD_RQ + n, TH:T], start=True, stop=True).then_inc(block_in, 1)
            pe.wait_ge(sem("rotated"), 2 * R)
            for stage, first in (("kn", OD_RK), ("vn", OD_RV)):
                for t in range(NT + 1):
                    s = slot(stage, t)
                    open_block(FIRST[stage] + t)
                    rows, cols = (P, slice(t * P, (t + 1) * P)) if t < NT else (TS, slice(SEQ, T))
                    for f in range(R):
                        last = tr(ps[0:rows, 2 * s, f * P:(f + 1) * P], big[:, first + f, cols], ident)
                    last.then_inc(block_in, 1)
            wait_emptied(pe, FIRST["vn"] + NT + 1)
            pe.wait_ge(sem("s0_in"), 16 * R)
            for n in range(R):
                base = FIRST["ret"] + 4 * n
                q, k = big[:, OD_RQ + n, :], big[:, OD_RK + n, :]
                cols = slice(n * P, (n + 1) * P)
                s = base % 4
                open_block(base)
                for t in range(NT):
                    mm(ps[:, 2 * s, t * P:(t + 1) * P], k[:, t * P:(t + 1) * P], q[:, t * P:(t + 1) * P],
                       start=True, stop=True)
                mm(bankB(s, rows=TS), k[:, SEQ:T], q[:, SEQ:T], start=True, stop=True).then_inc(block_in, 1)
                s = (base + 1) % 4
                open_block(base + 1)
                for t in range(NT):
                    last = mm(ps[:, 2 * s, t * P:(t + 1) * P], kn[:, t, cols], v2[:, t, cols], start=True, stop=True)
                last.then_inc(block_in, 1)
                s = (base + 2) % 4
                open_block(base + 2)
                pe.wait_ge(sem("v_spread"), n + 1)
                for a in range(2):
                    last = mm(ps[:, 2 * s + a, :], kn[0:TS, NT, cols], vmask[:, 4 * a:4 * a + 4, :],
                              start=True, stop=True)
                last.then_inc(block_in, 1)
                s = (base + 3) % 4
                open_block(base + 3)
                pe.wait_ge(sem("q_decayed"), n + 1)
                pe.wait_ge(sem("states_ready"), n + 1)
                for t in range(NT):
                    o = ps[:, 2 * s, t * P:(t + 1) * P]
                    mm(o, v2[:, t, cols], sct[:, t * P:(t + 1) * P], start=True, stop=(t == 0))
                    if t:
                        mm(o, st[:, t - 1, :], q[:, t * P:(t + 1) * P], start=False, stop=True)
                mm(bankB(s), v2[0:TS, NT, cols], sct[0:TS, SEQ:T], start=True, stop=False)
                for b in range(NB):
                    last = mm(ps[:, 2 * s + 1, b * NS:(b + 1) * NS], s0[:, n, b, :],
                              q[:, SEQ + b * NS:SEQ + (b + 1) * NS], start=False, stop=(b == NB - 1))
                last.then_inc(block_in, 1)
            for n in range(R):
                ones_sum("hmu", n, "emptied_by_scalar", emptied_by("scalar", FIRST["ret"] + 16) - 1, big[:, OD_RQ + n:OD_RQ + n + 1, :], 1)
            for n in range(R):
                ones_sum("hvar", n, "hsq_ready", n, xn[:, 4 + n:5 + n, :], 1)
            pe.wait_ge(sem("mixed1"), 1)
            gemm("out1", xn)
            ones_sum("norm3", 0, "sq_ready", 3 * KD, big, KD)
            gemm("up1", xn, ("xn_ready", 3 * KD))
            gemm("down1", big, ("u_ready", 32))

            ones_sum("norm4", 0, "sq_ready", 4 * KD, xn, KD)
            pe.wait_ge(sem("xn_ready"), 5 * KD)
            for t in range(NT + 1):
                s = slot("y", t)
                open_block(FIRST["y"] + t)
                rows, cols = (P, slice(t * P, (t + 1) * P)) if t < NT else (TS, slice(SEQ, T))
                for f in range(KD):
                    last = tr(ps[0:rows, 2 * s + f // 4, f % 4 * P:(f % 4 + 1) * P], xn[:, f, cols], ident)
                last.then_inc(block_in, 1)

        @blk.scalar
        def _(act):
            own = Steps(act, sem("act_steps"))
            act_f = nc.scalar.activation

            def evacuate(stage, count, dst, func=ACT.Copy, dyn=4):
                def one(n, i, m):
                    s = slot(stage, n)
                    act.wait_ge(block_in, FIRST[stage] + n + 1 + m)
                    d = dst(n, i)
                    act_f(d[:, 0:TH] if len(d.shape) == 2 else d[:, :, 0:TH], bankA(s, TH), func)
                    act_f(d[:, TH:T] if len(d.shape) == 2 else d[:, :, TH:T], bankB(s, TH), func)\
                        .then_inc(out_of["scalar"], 1)
                loops = count // 4
                if loops > 1:
                    with act.Fori(0, loops) as i:
                        for n in range(4):
                            one(n, i, i * 4)
                else:
                    for n in range(count):
                        one(n, None, 0)

            def norm(k):
                if k == 0:
                    wait_emptied(act, KD)
                for f in range(KD):
                    if k:
                        wait_emptied(act, FIRST[("", "out0", "down0", "out1", "down1")[k]] + f + 1)
                    act_f((big if k in (1, 3) else xn)[:, f, :], h[:, f, :], ACT.Square).then_inc(sem("sq_ready"), 1)
                root(f"norm{k}", 0, DM, rstd[:, :], "rms_ready")

            def root(stage, j, width, dst, signal):
                s = slot(stage, j)
                act.wait_ge(block_in, FIRST[stage] + j + 1)
                act_f(dst[:, 0:TH], bankA(s, TH), ACT.Sqrt, bias=EPS, scale=1.0 / width).then_inc(sem(signal), 1)
                act_f(dst[:, TH:T], bankB(s, TH), ACT.Sqrt, bias=EPS, scale=1.0 / width).then_inc(out_of["scalar"], 1)

            wait_emptied(act, KD)
            norm(0)
            evacuate("in0", 20, lambda n, i: big[:, n, :] if i is None else big[:, bass.ds(i * 4 + n, 1), :])

            act.wait_ge(sem("negabs_ready"), 1)
            own(act_f(z[2], z[1], ACT.Exp))
            act_f(z[1], z[2], ACT.Ln, bias=1.0).then_inc(sem("log1p_ready"), 1)
            s = slot("cum")
            act.wait_ge(block_in, FIRST["cum"] + 1)
            act_f(cumT[:, 0:SEQ], bankA(s, rows=H), ACT.Copy)
            act_f(cumT[:, SEQ:T], bankB(s, rows=H), ACT.Copy).then_inc(out_of["scalar"], 1)
            s = slot("cumT")
            act.wait_ge(block_in, FIRST["cumT"] + 1)
            act_f(cumn[:, 0:NT * H], bankA(s, NT * H), ACT.Copy)
            act_f(cumn[0:TS, NT * H:(NT + 1) * H], bankB(s, H, TS), ACT.Copy).then_inc(out_of["scalar"], 1)
            for n in range(H):
                s = slot("sfxT", n)
                act.wait_ge(block_in, FIRST["sfxT"] + n + 1)
                act_f(lT[:, :, n, :], bankA(s, 2 * P).rearrange("p (a g) -> p a g", a=2), ACT.Copy)
                act_f(lcT[:, :, n, :], bankB(s, 2 * P).rearrange("p (a g) -> p a g", a=2), ACT.Copy)\
                    .then_inc(out_of["scalar"], 1)
            to = sfx.rearrange("p (a g h) -> p a h g", a=2, h=H)
            for n in range(6):
                s = slot("sfx", n)
                act.wait_ge(block_in, FIRST["sfx"] + n + 1)
                act_f(to[:, n // 3, n % 3 * 4:n % 3 * 4 + 4, :], bankA(s).rearrange("p (h g) -> p h g", h=4), ACT.Copy)\
                    .then_inc(out_of["scalar"], 1)

            def copy_gates(hd):
                act.wait_ge(sem("gates_spread"), hd + 1)
                if hd >= 2:
                    act.wait_ge(sem("scores_read"), NT * (hd - 1))
                act_f(ckb[:, hd % 2, :], ps[:, 7, :], ACT.Copy, scale=-1.0).then_inc(sem("gates_copied"), 1)

            NSTEP = H * NT
            wait_emptied(act, FIRST["g96"] + 1)
            act.wait_ge(sem("k_stored_0"), 48)
            act.wait_ge(sem("k_stored_1"), 32)
            copy_gates(0)
            for n in range(NSTEP + 2):
                if n < NSTEP:
                    hd, i = n // NT, n % NT
                    if i == 1 and hd + 1 < H:
                        copy_gates(hd + 1)
                    act.wait_ge(sem("shift_ready"), n + 1)
                    if n >= 2:
                        act.wait_ge(sem("probs_turned"), n - 1)
                    w = (i + 1) * P
                    act_f(eb[:, n % 2, 0:w], tb[:, n % 2, 0:w], ACT.Exp, bias=hstat[:, 8 + n % 4:9 + n % 4],
                          accum_out=hstat[:, 12 + n % 4:13 + n % 4]).then_inc(sem("probs_made"), 1)
                if n >= 2:
                    m = n - 2
                    hd, i = m // NT, m % NT
                    act.wait_ge(sem("probs_turned"), m + 1)
                    if hd >= 2:
                        act.wait_ge(sem("fox_prompt_out"), hd - 1)
                    act_f(pT[:, hd % 2, 0:i + 1, i * P:(i + 1) * P],
                          ps[:, 3 + m % 3, 0:(i + 1) * P].rearrange("p (j q) -> p j q", j=i + 1), ACT.Copy)\
                        .then_inc(sem("probs_turned_copied"), 1)

            def copy_page(b, p):
                k = b * PAGES + p
                act.wait_ge(sem("k_page_used"), k + 1)
                quad = b * GROUPS + p // GROUP
                if p % GROUP == 0 and (not isinstance(b, int) or quad >= 2):
                    act.wait_ge(sem("groups_scored"), quad - 1)
                at = p % GROUP * PAGE
                act_f(kT[:, p // GROUP % 2, 0:4, at:at + PAGE],
                      ps[:, 2 * (p % 2), :].rearrange("p (f n) -> p f n", f=4), ACT.Copy).then_inc(sem("kT_low"), 1)

            def exps(b, c):
                act.wait_ge(sem("softmax_shift"), b + 1)
                n = 2 * GROUP * PAGE
                part = S[:, c * n:(c + 1) * n] if c < EXPS else S[:, c * n:c * n + TS]
                act_f(part, part, ACT.Exp, bias=sshift, accum_out=ssum[:, c:c + 1]).then_inc(sem("exp_done"), 1)

            def k_pages(b, soft):
                for p in range(PAGES):
                    copy_page(b, p)
                    if soft is not None and 1 <= p <= EXPS:
                        exps(soft, p - 1)
                        if p == EXPS:
                            exps(soft, EXPS)

            k_pages(0, None)
            k_pages(1, 0)
            with act.Fori(2, NB) as c:
                k_pages(c, c - 1)
            for c in range(EXPS + 1):
                exps(NB - 1, c)

            norm(1)
            def mlp(stage):
                with act.Fori(0, 8) as i:
                    for n in range(4):
                        s = slot(stage, n)
                        act.wait_ge(block_in, FIRST[stage] + n + 1 + i * 4)
                        act_f(big[:, bass.ds(i * 4 + n, 1), 0:TH], bankA(s, TH), ACT.Relu)
                        act_f(big[:, bass.ds(i * 4 + n, 1), TH:T], bankB(s, TH), ACT.Relu).then_inc(out_of["scalar"], 1)
            act.wait_ge(sem("stored"), 64)
            mlp("up0")
            norm(2)
            evacuate("in1", 24, lambda n, i: big[:, n, :] if i is None else big[:, bass.ds(i * 4 + n, 1), :])
            s = slot("mu")
            act.wait_ge(block_in, FIRST["mu"] + 1)
            act_f(rstd[:, 0:TH], bankA(s, TH), ACT.Copy, scale=1.0 / 512)
            act_f(rstd[:, TH:T], bankB(s, TH), ACT.Copy, scale=1.0 / 512).then_inc(out_of["scalar"], 1)
            for f in range(4):
                act.wait_ge(sem("centred"), f + 1)
                act_f(xn[:, 4 + f, :], big[:, OD_GV + f, :], ACT.Square).then_inc(sem("lnsq_ready"), 1)
            root("var", 0, 512, rstd[:, :], "ln_root")
            for n in range(R):
                act_f(big[:, OD_U + n, :], big[:, OD_RG + n, :], ACT.Exp, scale=-1.0) if False else None
            for stage, dst in (("kn", None), ("vn", v2)):
                if dst is None:
                    continue
                for t in range(NT + 1):
                    s = slot(stage, t)
                    rows = P if t < NT else TS
                    act.wait_ge(block_in, FIRST[stage] + t + 1)
                    act_f(dst[0:rows, t, :], bankA(s, rows=rows), ACT.Copy).then_inc(out_of["scalar"], 1)
            for n in range(R):
                s = slot("ret", 4 * n + 3)
                act.wait_ge(block_in, FIRST["ret"] + 4 * n + 4)
                act_f(big[:, OD_RQ + n, 0:SEQ], bankA(s), ACT.Copy)
                act_f(big[:, OD_RQ + n, SEQ:T], bankB(s), ACT.Copy).then_inc(out_of["scalar"], 1)
            for n in range(R):
                own(act_f(big[:, OD_RK + n, :], big[:, OD_RG + n, :], ACT.Exp, scale=-1.0))
            act.sem_inc(sem("gate_exp"), 1)
            for n in range(R):
                s = slot("hmu", n)
                act.wait_ge(block_in, FIRST["hmu"] + n + 1)
                act_f(big[:, OD_RV + n, 0:TH], bankA(s, TH), ACT.Copy, scale=1.0 / DR)
                act_f(big[:, OD_RV + n, TH:T], bankB(s, TH), ACT.Copy, scale=1.0 / DR).then_inc(out_of["scalar"], 1)
            for n in range(R):
                act.wait_ge(sem("hcentred"), n + 1)
                act_f(xn[:, 4 + n, :], big[:, OD_RQ + n, :], ACT.Square).then_inc(sem("hsq_ready"), 1)
            for n in range(R):
                root("hvar", n, DR, big[:, OD_RV + n, :], "hroot_a")
            norm(3)
            act.wait_ge(sem("ret_stored"), 32 * R)
            mlp("up1")
            norm(4)

        @blk.vector
        def _(dve):
            own = Steps(dve, sem("dve_steps"))
            tt, stt, ts = nc.vector.tensor_tensor, nc.vector.scalar_tensor_tensor, nc.vector.tensor_scalar
            cp = nc.vector.tensor_copy

            def drained(stage, n):
                dve.wait_ge(block_in, FIRST[stage] + n + 1)
                return slot(stage, n)

            def norm(k, row):
                wait_emptied(dve, FIRST[f"norm{k}"] + 1)
                own(nc.vector.reciprocal(rstd[:, :], rstd[:, :]))
                for f in range(KD):
                    stt(xn[:, f, :], h[:, f, :], pcol[:, row + f:row + f + 1], rstd[:, :], ALU.mult, ALU.mult)\
                        .then_inc(sem("xn_ready"), 1)

            def residual(stage):
                for n in range(KD):
                    s = drained(stage, n)
                    tt(h[:, n, 0:TH], bankA(s, TH), h[:, n, 0:TH], ALU.add)
                    tt(h[:, n, TH:T], bankB(s, TH), h[:, n, TH:T], ALU.add).then_inc(out_of["vector"], 1)

            def squares(stage, base):
                with dve.Fori(0, 8) as i:
                    for n in range(4):
                        dve.wait_ge(out_of["scalar"], emptied_by("scalar", FIRST[stage]) + n + 1 + i * 4)
                        u = big[:, bass.ds(i * 4 + n, 1), :]
                        tt(u, u, u, ALU.mult).then_inc(sem("u_ready"), 1)

            for f in range(KD):
                s = drained("x", f)
                cp(h[:, f, 0:SEQ], bankA(s))
                cp(h[:, f, SEQ:T], bankB(s)).then_inc(out_of["vector"], 1)
            dve.wait_ge(sem("params_turned"), 1)
            cp(pcol[:, :], ps[:, 7, 0:NPARAM]).then_inc(sem("params_ready"), 1)
            dve.wait_ge(sem("params_ready"), 1)
            norm(0, PROW["norm_mix"])

            s = drained("logf", 0)
            dve.wait_ge(sem("wf_in"), 32)
            ts(z[0][:, 0:TH], bankA(s, TH, H), bf[:, 0:1], None, ALU.add)
            ts(z[0][:, TH:T], bankB(s, TH, H), bf[:, 0:1], None, ALU.add).then_inc(out_of["vector"], 1)
            wait_emptied(dve, FIRST["logf"] + 1)
            own(ts(z[2], z[0], -1.0, None, ALU.mult))
            tt(z[1], z[2], z[0], ALU.min).then_inc(sem("negabs_ready"), 1)
            own(ts(z[0], z[0], 0.0, None, ALU.min))
            dve.wait_ge(sem("log1p_ready"), 1)
            tt(z[3], z[0], z[1], ALU.subtract).then_inc(sem("logf_ready"), 1)
            s = drained("logfT", 0)
            cp(lfn[:, 0:NT * H], bankA(s, NT * H))
            cp(lfn[0:TS, NT * H:(NT + 1) * H], bankB(s, H, TS)).then_inc(out_of["vector"], 1)
            wait_emptied(dve, FIRST["logfT"] + 1)
            dve.sem_inc(sem("lfn_ready"), 1)

            def rows(stage, dst, before=None):
                for t in range(NT + 1):
                    if before:
                        before(t)
                    s = drained(stage, t)
                    r = P if t < NT else TS
                    d = dst(t)
                    cp(d[0:r, 0:512], bankA(s, rows=r))
                    cp(d[0:r, 512:FOX], bankB(s, FOX - 512, r)).then_inc(out_of["vector"], 1)

            def stage_free(t):
                if t == 0:
                    wait_emptied(dve, FIRST["sfx"] + 6)
                if t >= 2:
                    dve.wait_ge(sem(f"k_stored_{t % 2}"), 16 * (t // 2))

            rows("knat", lambda t: kstage[:, t % 2, :], stage_free)
            own(nc.vector.memset(vs, 0.0))
            rows("vnat", lambda t: vn0[:, t, :] if t < NT else vs)
            s = drained("g96", 0)
            gates = ps[0:HQ, 2 * s, 0:TS]
            tt(key_bias, cst("mask_new"), gates, ALU.subtract)
            tt(ostage[:, 0:TS], gates, cst("own_query"), ALU.mult).then_inc(out_of["vector"], 1)
            wait_emptied(dve, FIRST["g96"] + 1)
            nc.vector.reduce_sum(qgate, ostage[:, 0:TS].rearrange("p (b s) -> p b s", b=NB), AX.X)
            own(nc.vector.memset(bigf[:, at0 + 3840:at0 + 5376], 0.0))
            cp(knew, big[:, EV_K:EV_K + HB, SEQ:T])
            for a in range(2):
                r = slice(64 * a, 64 * a + 64)
                for c in range(2):
                    at = 16 * c + 8 * a
                    dst = qall[r, :, :, at:at + NS].rearrange("p b (j c) s -> p c j b s", c=2)[:, c]
                    src = big[r, EV_Q:EV_Q + HB, SEQ:T].rearrange("p (j c) (b s) -> p c j b s", c=2, b=NB)[:, c]
                    ins = ts(dst, src, D ** -0.5, None, ALU.mult)
                ins.then_inc(sem("queries_placed"), 1)

            mx, mf, shift, den, rec = (hstat[:, 4 * n:4 * n + 4] for n in range(5))

            def scale_probs(n):
                hd, i = n // NT, n % NT
                c = n % 4
                dve.wait_ge(sem("probs_made"), n + 1)
                own(nc.vector.reciprocal(rec[:, c:c + 1], den[:, c:c + 1]))
                w = (i + 1) * P
                ts(eb[:, n % 2, 0:w], eb[:, n % 2, 0:w], rec[:, c:c + 1], None, ALU.mult)\
                    .then_inc(sem("probs_scaled"), 1)

            def head_out(hd):
                r = slice(64 * (hd % 2), 64 * (hd % 2) + 64)
                dve.wait_ge(sem("fox_prompt_out"), hd + 1)
                cp(xn[r, 2 + hd // 2, 0:SEQ], ps[r, 6, :]).then_inc(sem("fox_prompt_done"), 1)

            NSTEP = H * NT
            for n in range(NSTEP + 5):
                if n < NSTEP:
                    hd, i = n // NT, n % NT
                    c, w = n % 4, (i + 1) * P
                    dve.wait_ge(sem("scores_made"), n + 1)
                    dve.wait_ge(sem("gates_copied"), hd + 1)
                    if n >= 2:
                        dve.wait_ge(sem("probs_made"), n - 1)
                    stt(tb[:, n % 2, 0:w], ps[:, n % 3, 0:w], D ** -0.5, ckb[:, hd % 2, 0:w], ALU.mult, ALU.add)\
                        .then_inc(sem("scores_read"), 1)
                    dve.wait_ge(sem("scores_read"), n + 1)
                    own(tt(tb[:, n % 2, w - P:w], tb[:, n % 2, w - P:w], cst("mask"), ALU.add))
                    own(nc.vector.reduce_max(mx[:, c:c + 1], tb[:, n % 2, 0:w], AX.X))
                    g = cumn[:, i * H + hd:i * H + hd + 1]
                    own(tt(mf[:, c:c + 1], mx[:, c:c + 1], g, ALU.add))
                    tt(shift[:, c:c + 1], g, mf[:, c:c + 1], ALU.subtract).then_inc(sem("shift_ready"), 1)
                if 1 <= n < NSTEP + 1:
                    scale_probs(n - 1)
                if n >= 4 and (n - 4) % NT == NT - 1:
                    head_out((n - 4) // NT)

            for a in range(2):
                s = drained("hist", a)
                cp(es[0][:, a, :, 0:HIST], ps[:, 2 * s, 0:NB * HIST].rearrange("p (b t) -> p b t", b=NB))\
                    .then_inc(out_of["vector"], 1)
            wait_emptied(dve, FIRST["hist"] + 2)
            for a in range(2):
                own(cp(es[0][:, a, :, HIST:HIST + NS], big[:, a, SEQ:T].rearrange("p (b s) -> p b s", b=NB)))
                cp(hcopy[:, a, :].rearrange("p (b t) -> p b t", b=NB), es[0][:, a, :, NS:NS + HIST])\
                    .then_inc(sem("ext_s_ready"), 1)
            dve.wait_ge(sem("ext_s_ready"), 2)
            dve.sem_inc(sem("hist_copied"), 1)
            dve.wait_ge(sem("pooled"), 1)
            for a in range(2):
                ts(xn[:, a, 0:SEQ], ps[:, 4 + a, :], param("pool_scale", a), None, ALU.mult)
                own(ts(xn[:, a, SEQ:T], ps[:, 6 + a, 0:TS], param("pool_scale", a), None, ALU.mult))
            dve.sem_inc(sem("pool_mixed"), 1)
            dve.wait_ge(sem("hist_turned"), 1)
            for a in range(2):
                cp(hout[:, a * P:(a + 1) * P], ps[0:NB * HIST, a, 0:P])
                own(cp(hout_p[:, a * P:(a + 1) * P], ps[0:HIST, a, P:2 * P]))
            dve.sem_inc(sem("hist_out_ready"), 1)

            def at(x, b, n=1):
                return x[:, b:b + n] if isinstance(b, int) else x[:, bass.ds(b, n)]

            def stage_queries(b):
                if not isinstance(b, int) or b >= 1:
                    dve.wait_ge(sem("new_scored"), b)
                q = qall[:, b] if isinstance(b, int) else qall[:, bass.ds(b, 1)].rearrange("p o f c -> p (o f) c")
                cp(qcur, q).then_inc(sem("queries_staged"), 1)

            def stage_suffix(b, g):
                if not isinstance(b, int) or b * GROUPS + g >= 2:
                    dve.wait_ge(sem("groups_scored"), b * GROUPS + g - 1)
                n = GROUP * H
                lo = b * (PAGES * H) + g * n
                src = sfx[:, lo:lo + n] if isinstance(b, int) else sfx[:, bass.ds(lo, n)]
                cp(sgate[:, g % 2, :].rearrange("p (n s) -> p n s", s=NS),
                   src.rearrange("p (n o) -> p n o", o=1).broadcast_to([P, n, NS])).then_inc(sem("suffix_staged"), 1)

            def copy_page(b, p):
                k = b * PAGES + p
                dve.wait_ge(sem("k_page_used"), k + 1)
                quad = b * GROUPS + p // GROUP
                if p % GROUP == 0 and (not isinstance(b, int) or quad >= 2):
                    dve.wait_ge(sem("groups_scored"), quad - 1)
                at = p % GROUP * PAGE
                cp(kT[:, p // GROUP % 2, 4:HB, at:at + PAGE],
                   ps[:, 2 * (p % 2) + 1, 0:2 * PAGE].rearrange("p (f n) -> p f n", f=2)).then_inc(sem("kT_high"), 1)

            def take_scores(b, g):
                dve.wait_ge(sem("groups_scored"), b * GROUPS + g + 1)
                if not isinstance(b, int) or b >= 1:
                    dve.wait_ge(sem("probs_turned_s"), (b - 1) * (GROUPS + 1) + g + 1)
                n = GROUP * PAGE
                cp(S[:, g * n:(g + 1) * n], ps[0:HQ, 4 + g % 2, :])
                nc.vector.reduce_max(smax[:, g:g + 1], ps[0:HQ, 4 + g % 2, :], AX.X).then_inc(sem("scores_in"), 1)

            def take_new(b):
                dve.wait_ge(sem("new_scored"), b + 1)
                if not isinstance(b, int) or b >= 1:
                    dve.wait_ge(sem("probs_turned_s"), b * (GROUPS + 1))
                new = S[:, PAGES * PAGE:PAGES * PAGE + TS]
                own(tt(new, ps[0:HQ, 4, 0:TS], key_bias, ALU.add))
                start = (NB - 1 - b) * NS if isinstance(b, int) else b * (-NS) + (NB - 1) * NS
                window = cst("mask_seq", start, start + TS) if isinstance(b, int) else \
                    cst("mask_seq")[:, bass.ds(start, TS)]
                own(tt(new, new, window, ALU.add))
                nc.vector.reduce_max(smax[:, GROUPS:GROUPS + 1], new, AX.X).then_inc(sem("scores_in"), 1)

            def softmax_shift(b):
                dve.wait_ge(sem("scores_in"), (b + 1) * (GROUPS + 1))
                own(nc.vector.reduce_max(gmax, smax, AX.X))
                g = qgate[:, b:b + 1] if isinstance(b, int) else qgate[:, bass.ds(b, 1)]
                own(tt(gfull, gmax, g, ALU.add))
                tt(sshift, g, gfull, ALU.subtract).then_inc(sem("softmax_shift"), 1)

            def take_probs(b, g):
                dve.wait_ge(sem("probs_turned_s"), b * (GROUPS + 1) + g + 1)
                if not isinstance(b, int) or b >= 1:
                    if g < GROUPS:
                        dve.wait_ge(sem("v_page_used"), (b - 1) * PAGES + (g + 1) * GROUP)
                    else:
                        dve.wait_ge(sem("fox_sample_out"), b)
                if g == GROUPS:
                    ins = cp(pTs[0:TS, PAGES, :], ps[0:TS, 6, 0:HQ])
                else:
                    ins = cp(pTs[:, g * GROUP:(g + 1) * GROUP, :],
                             ps[:, 6, 0:GROUP * HQ].rearrange("p (m c) -> p m c", m=GROUP))
                ins.then_inc(sem("probs_in"), 1)

            def denominators(b):
                dve.wait_ge(sem("exp_done"), (b + 1) * (EXPS + 1))
                own(nc.vector.reduce_sum(sden, ssum, AX.X))
                own(nc.vector.reciprocal(srec, sden))

            def scale_out(b):
                dve.wait_ge(sem("fox_sample_out"), b + 1)
                ts(ostage, ps[0:HQ, 7, 0:256], srec, None, ALU.mult).then_inc(sem("out_scaled"), 1)

            def place_out(b):
                dve.wait_ge(sem("out_turned"), b + 1)
                for a in range(2):
                    r = slice(64 * a, 64 * a + 64)
                    for c in range(2):
                        src = ps[r, 6, c * HQ:(c + 1) * HQ].rearrange("p (j s) -> p j s", j=JT)
                        src = src[:, :, 16 * c + 8 * a:16 * c + 8 * a + NS]
                        rows = xn[r, 2:KD, :].rearrange("p (j c) t -> p c j t", c=2)[:, c]
                        dst = rows[:, :, SEQ + b * NS:SEQ + (b + 1) * NS] if isinstance(b, int) else \
                            rows[:, :, bass.ds(b * NS + SEQ, NS)]
                        ins = cp(dst, src)
                ins.then_inc(sem("outputs_placed"), 1)

            def phase(c, k=True, ending=True, starting=True):
                if starting:
                    softmax_shift(c - 1)
                if k:
                    stage_queries(c)
                for p in range(PAGES):
                    if ending and p == LAG:
                        scale_out(c - 2)
                    if k:
                        copy_page(c, p)
                        if p % GROUP == 2:
                            stage_suffix(c, p // GROUP)
                        if p > GROUP and p % GROUP == 1:
                            take_scores(c, p // GROUP - 1)
                    if starting and 3 <= p < 3 + GROUPS + 1:
                        take_probs(c - 1, p - 3)
                    if starting and p == 13:
                        denominators(c - 1)
                    if ending and p == 14:
                        place_out(c - 2)
                if starting and not ending:
                    dve.sem_inc(sem("outputs_placed"), 1)
                if k:
                    take_scores(c, GROUPS - 1)
                    take_new(c)

            own(nc.vector.memset(pTs[:, PAGES, :], 0.0))
            phase(0, ending=False, starting=False)
            phase(1, ending=False)
            with dve.Fori(2, NB) as c:
                own.loop(c - 2, 6)
                phase(c)
            own.end(NB - 2)
            phase(NB, k=False)
            scale_out(NB - 1)
            place_out(NB - 1)

            residual("out0")
            norm(1, PROW["norm_ffn"])
            squares("up0", 0)
            residual("down0")

            norm(2, PROW["norm_mix"] + KD)
            s = drained("wst", 0)
            low = cst("upto", 0, P).rearrange("p (o t) -> p o t", o=1).broadcast_to([P, 4, P])
            tt(wT, bankA(s).rearrange("p (g t) -> p g t", g=4), low, ALU.mult).then_inc(out_of["vector"], 1)
            s = drained("w8", 0)
            corner = ps[0:TS, 2 * s, 0:4 * NS].rearrange("p (g t) -> p g t", g=4)
            for g in range(4):
                last = tt(w8[:, g, :].rearrange("p (b t) -> p b t", b=NB),
                          corner[:, g:g + 1, :].broadcast_to([TS, NB, NS]),
                          cst1("same_s").rearrange("p (b t) -> p b t", b=NB), ALU.mult)
            last.then_inc(out_of["vector"], 1)
            wait_emptied(dve, FIRST["mu"] + 1)
            for f in range(4):
                g = big[:, OD_GV + f, :]
                tt(g, g, rstd[:, :], ALU.subtract).then_inc(sem("centred"), 1)
            wait_emptied(dve, FIRST["var"] + 1)
            own(nc.vector.reciprocal(rstd[:, :], rstd[:, :]))
            for f in range(4):
                g = big[:, OD_GV + f, :]
                own(stt(g, g, param("gmlp_ln_g", f), rstd[:, :], ALU.mult, ALU.mult))
                ts(g, g, param("gmlp_ln_b", f), None, ALU.add).then_inc(sem("ln_ready"), 1)
            for t in range(NT + 1):
                s = drained("vnat1", t)
                r = P if t < NT else TS
                cp(vnn[0:r, t, :], bankA(s, rows=r)).then_inc(out_of["vector"], 1)
            for g in range(4):
                s = drained("z", g)
                tt(xn[:, g, 0:SEQ], bankA(s), big[:, OD_U + g, 0:SEQ], ALU.mult)
                tt(xn[:, g, SEQ:T], bankB(s), big[:, OD_U + g, SEQ:T], ALU.mult).then_inc(out_of["vector"], 1)
            for n in range(2 * R):
                sc = 1.0 if n < R else DR ** -0.5
                x = big[:, OD_RQ + n, :]
                s = drained("rot", n)
                if n:
                    dve.wait_ge(sem("rotated"), n)
                stt(tmp[:, 0:TH], bankA(s, TH), sc, cst1("sin", 0, TH), ALU.mult, ALU.mult)
                stt(tmp[:, TH:T], bankB(s, TH), sc, cst1("sin", TH, T), ALU.mult, ALU.mult).then_inc(out_of["vector"], 1)
                own(stt(x, x, sc, cst1("cos"), ALU.mult, ALU.mult))
                tt(x, x, tmp, ALU.add).then_inc(sem("rotated"), 1)
            for t in range(NT + 1):
                s = drained("kn", t)
                r = P if t < NT else TS
                dk = cst1("dec_k" if t < NT else "dec_ks").rearrange("p (h o) -> p h o", o=1).broadcast_to([r, R, P])
                tt(kn[0:r, t, :].rearrange("p (h d) -> p h d", h=R),
                   bankA(s, rows=r).rearrange("p (h d) -> p h d", h=R), dk, ALU.mult).then_inc(out_of["vector"], 1)
            wait_emptied(dve, FIRST["vn"] + NT + 1)
            dve.wait_ge(sem("gv_stored"), 16)
            for n in range(R):
                base = 4 * n
                cols = slice(n * P, (n + 1) * P)
                if n:
                    dve.wait_ge(block_in, FIRST["ret"] + base - 1)
                vv = v2[0:TS, NT, cols].rearrange("p (o e) -> p o e", o=1).broadcast_to([TS, NB, P])
                mb = cst1("of_seq").rearrange("p (b o) -> p b o", o=1).broadcast_to([TS, NB, P])
                tt(vmask, vv, mb, ALU.mult).then_inc(sem("v_spread"), 1)
                s = drained("ret", base)
                if n:
                    wait_emptied(dve, FIRST["ret"] + base)
                dd = cst1("dec", n * P, (n + 1) * P).rearrange("p (o l) -> p o l", o=1).broadcast_to([P, NT, P])
                tt(sct[:, 0:SEQ].rearrange("p (t l) -> p t l", t=NT), bankA(s).rearrange("p (t l) -> p t l", t=NT),
                   dd, ALU.mult)
                tt(sct[0:TS, SEQ:T], bankB(s, rows=TS), cst1("dec_s", n * TS, (n + 1) * TS), ALU.mult)\
                    .then_inc(out_of["vector"], 1)
                q = big[:, OD_RQ + n, :]
                dq = cst1("dec_q", n * P, (n + 1) * P).rearrange("p (o l) -> p o l", o=1)
                qp = q[:, 0:SEQ].rearrange("p (t l) -> p t l", t=NT)
                tt(qp, qp, dq.broadcast_to([P, NT, P]), ALU.mult)
                qs = q[:, SEQ:T].rearrange("p (b l) -> p b l", b=NB)
                tt(qs, qs, dq[:, :, 0:NS].broadcast_to([P, NB, NS]), ALU.mult).then_inc(sem("q_decayed"), 1)
                s = drained("ret", base + 1)
                if n:
                    dve.wait_ge(sem("ret_stored"), 32 * n)
                own(cp(st[:, 0, :], ps[:, 2 * s, 0:P]))
                for t in range(1, NT):
                    ins = stt(st[:, t, :], st[:, t - 1, :], decay_step[0][n], ps[:, 2 * s, t * P:(t + 1) * P],
                              ALU.mult, ALU.add)
                    if t < NT - 1:
                        own(ins)
                ins.then_inc(out_of["vector"], 1)
                wait_emptied(dve, FIRST["ret"] + base + 2)
                dve.sem_inc(sem("states_ready"), 1)
                s = drained("ret", base + 2)
                for a in range(2):
                    ins = stt(s_out[:, 4 * a:4 * a + 4, :].rearrange("p b e -> p (b e)"),
                              s0[:, n, 4 * a:4 * a + 4, :].rearrange("p b e -> p (b e)"), decay_step[1][n],
                              ps[:, 2 * s + a, :], ALU.mult, ALU.add)
                ins.then_inc(out_of["vector"], 1)
                wait_emptied(dve, FIRST["ret"] + base + 3)
                dve.sem_inc(sem("ret_state_ready"), 1)
            for n in range(R):
                o, mu = big[:, OD_RQ + n, :], big[:, OD_RV + n, :]
                wait_emptied(dve, FIRST["hmu"] + n + 1)
                tt(o, o, mu, ALU.subtract).then_inc(sem("hcentred"), 1)
            dve.wait_ge(sem("gate_exp"), 1)
            ex = big[:, OD_RK:OD_RK + R, :]
            own(ts(ex, ex, 1.0, None, ALU.add))
            own(nc.vector.reciprocal(ex, ex))
            own(tt(ex, ex, big[:, OD_RG:OD_RG + R, :], ALU.mult))
            dve.wait_ge(sem("hcentred"), R)
            for n in range(R):
                o, rs = big[:, OD_RQ + n, :], big[:, OD_RV + n, :]
                wait_emptied(dve, FIRST["hvar"] + n + 1)
                own(nc.vector.reciprocal(rs, rs))
                own(stt(rs, rs, param("ret_gn_g", n), o, ALU.mult, ALU.mult))
                own(tt(xn[:, 4 + n, :], rs, big[:, OD_RK + n, :], ALU.mult))
            dve.sem_inc(sem("mixed1"), 1)
            residual("out1")
            norm(3, PROW["norm_ffn"] + KD)
            squares("up1", 32)
            residual("down1")
            norm(4, PROW["norm_final"])
            for t in range(NT + 1):
                s = drained("y", t)
                r = P if t < NT else TS
                if t >= 2:
                    dve.wait_ge(sem(f"y_stored_{t % 2}"), 16 * (t // 2))
                cp(ystage[0:r, t % 2, 0:512], bankA(s, rows=r))
                cp(ystage[0:r, t % 2, 512:DM], bankB(s, 512, r)).then_inc(out_of["vector"], 1)


_INS = ['x_prompt', 'x_sample', 'state_pool', 'cache_k', 'cache_v', 'cache_logf', 'page_table', 'state_ret', 'norm_mix',
        'w_in_even', 'b_forget', 'pool_w', 'pool_scale', 'w_out_even', 'w_in_odd', 'gmlp_ln_g', 'gmlp_ln_b', 'gmlp_ws',
        'gmlp_bs', 'ret_gn_g', 'w_out_odd', 'norm_ffn', 'w_up', 'w_down', 'norm_final']
_OUTS = [("y_prompt", (1, 512, 1024)), ("y_sample", (8, 8, 1024)), ("pool_prompt", (1, 1, 15, 256)),
         ("k_prompt", (1, 1, 512, 12, 64)), ("v_prompt", (1, 1, 512, 12, 64)), ("logf_prompt", (1, 1, 512, 12)),
         ("ret_prompt", (1, 1, 4, 128, 128)), ("pool_sample", (1, 8, 15, 256)), ("k_sample", (1, 8, 8, 12, 64)),
         ("v_sample", (1, 8, 8, 12, 64)), ("logf_sample", (1, 8, 8, 12)), ("gmlp_v_sample", (1, 8, 8, 512)),
         ("ret_sample", (1, 8, 4, 128, 128))]


def kernel(**inputs):
    import numpy as _np
    import concourse.bacc as _bacc
    from concourse import mybir as _mybir
    from concourse.bass_utils import run_bass_kernel_spmd as _run

    nc = _bacc.Bacc("TRN2", target_bir_lowering=False, num_devices=1)
    (tab0, where0), (tab1, where1), step = tables()
    arrays, ins, outs = {}, {}, {}
    for name in _INS:
        arrays[f"in_{name}"] = _np.ascontiguousarray(inputs[name])
    arrays["in_tab0"], arrays["in_tab1"] = tab0, tab1
    for name, a in arrays.items():
        ins[name[3:]] = nc.dram_tensor(name, a.shape, _mybir.dt.from_np(a.dtype), kind="ExternalInput").ap()
    for name, shape in _OUTS:
        outs[name] = nc.dram_tensor(f"out_{name}", shape, _mybir.dt.float32, kind="ExternalOutput").ap()
    hybrid_step(nc, ins, outs, where0, where1, step)
    r = _run(nc, [arrays], core_ids=[0])
    return tuple(r.results[0][f"out_{name}"] for name, _ in _OUTS)
```

```python
import math
from contextlib import ExitStack

import concourse.bass as bass
import numpy as np
from concourse import mybir

F32 = mybir.dt.float32
I32 = mybir.dt.int32
ALU = mybir.AluOpType
ACT = mybir.ActivationFunctionType
AX = mybir.AxisListType

P = 128
DM, SEQ, NB, NS = 1024, 512, 8, 8
TS = NB * NS
T = SEQ + TS
TH = T // 2
PAGES, PAGE, NPHYS = 32, 128, 320
FF = 4096
EPS = 1e-6
NEG = -1e30
KD = DM // P
NT = SEQ // P
H, D = 12, 64
HQ = H * NS
FOX = H * D
HB = FOX // P
R, DR = 4, 128
HIST = 15
EXT = HIST + SEQ
UNIT = KD * 512
RING = 4
GROUP = 4
GROUPS = PAGES // GROUP
LAG = 8
EXPS = GROUPS // 2
JT = HQ // 32
EV = 2572

EV_Q, EV_K, EV_V = 2, 8, 14
OD_U, OD_GV, OD_RQ, OD_RK, OD_RV, OD_RG = 0, 4, 8, 12, 16, 20

PARAMS = [("norm_mix", 16), ("norm_ffn", 16), ("norm_final", 8), ("pool_scale", 2), ("gmlp_ln_g", 4),
          ("gmlp_ln_b", 4), ("ret_gn_g", 4)]
PROW = {}
for _n, _k in PARAMS:
    PROW[_n] = sum(k for _, k in PARAMS[:len(PROW)])
NPARAM = sum(k for _, k in PARAMS)

STAGES = [("x", KD), ("norm0", 1), ("in0", 20), ("logf", 1), ("sfxT", 12), ("logfT", 1), ("sfx", 6),
          ("cum", 1), ("knat", 5), ("cumT", 1), ("vnat", 5), ("hist", 2), ("g96", 1),
          ("out0", 8), ("norm1", 1), ("up0", 32), ("down0", 8),
          ("norm2", 1), ("in1", 8), ("rq", 4), ("wst", 1), ("w8", 1), ("mu", 1), ("rk_a", 2), ("rot_q", 4),
          ("rk_b", 2), ("var", 1), ("rv_a", 2), ("rot_k", 4), ("rv_b", 2), ("vnat1", 5), ("vn", 5), ("z", 4), ("kn", 5)]
for _n in range(R):
    STAGES += [(f"ret_{_n}", 3)] + [(f"hmu_{_n - 1}", 1)] * (_n > 0) + [(f"u_{_n}", 1), (f"ret_out_{_n}", 1)]
    STAGES += [(f"hvar_{_n - 1}", 1)] * (_n > 0)
STAGES += [(f"hmu_{R - 1}", 1), (f"hvar_{R - 1}", 1),
           ("out1", 8), ("norm3", 1), ("up1", 32), ("down1", 2 * KD)]
FIRST = {}
_at = 0
for _n, _k in STAGES:
    FIRST[_n] = _at
    _at += _k

BY_SCALAR = {"norm0", "in0", "cum", "cumT", "sfxT", "sfx", "norm1", "up0", "norm2", "in1", "rq", "mu", "rk_a", "rk_b",
             "var", "rv_a", "rv_b", "vn", "norm3", "up1"}
BY_SCALAR |= {f"{_n}_{_j}" for _n in ("ret_out", "hmu", "hvar") for _j in range(R)}
OWNER = []
for _n, _k in STAGES:
    OWNER += ["scalar" if _n in BY_SCALAR else "vector"] * _k


def down_block(f):
    return FIRST["down1"] + max(0, 2 * f - 1)


def rows_block(f):
    return FIRST["down1"] + min(2 * f + 2, 2 * KD - 1)


def emptied_by(owner, n):
    return sum(o == owner for o in OWNER[:n])


WEIGHTS = [("in0", 5, 4), ("out0", 2, 4), ("up0", 8, 4), ("down0", 8, 1),
           ("in1", 6, 4), ("out1", 2, 4), ("up1", 8, 4), ("down1", 8, 1)]
IN1 = (OD_RG, OD_GV, OD_RQ, OD_RK, OD_RV, OD_U)
IN1_USED = (FIRST["in1"] + 4, FIRST["in1"] + 8, FIRST["rq"] + 4, FIRST["rk_b"] + 2, FIRST["rv_b"] + 2, FIRST["u_3"] + 1)
UFIRST = {}
_at = 0
for _n, _k, _b in WEIGHTS:
    UFIRST[_n] = _at
    _at += _k


def tables():
    p, f = np.arange(P)[:, None], np.arange(P)[None, :]
    q, g = np.arange(TS)[:, None], np.arange(TS)[None, :]
    same = q // NS == g // NS
    one = lambda m: m.astype(np.float32)
    w = np.array([[2, 8], [4, 16]])[(np.arange(P) >= 64).astype(int)]
    cnt = np.minimum(np.arange(16)[None, None, :] + 1, w[:, :, None])
    even = {
        "ident": one(p == f),
        "ones": np.ones((P, P), np.float32),
        "upto": np.concatenate([one(p <= f), np.ones((P, SEQ - P), np.float32)], 1),
        "mask": np.where(f <= p, 0.0, NEG).astype(np.float32),
        "later": one(p > f),
        "later_page": one((p // PAGES == f // PAGES) & (p > f)),
        "upto_s": one(same & (q <= g)),
        "head_of": one(np.arange(H)[:, None] == np.arange(HQ)[None, :] // NS),
        "mask_new": np.where(g % NS <= np.arange(HQ)[:, None] % NS, 0.0, NEG).astype(np.float32),
        "own_query": one(g % NS == np.arange(HQ)[:, None] % NS),
        "mask_seq": np.where(np.arange(2 * TS - NS)[None, :] // NS == NB - 1, 0.0, NEG).repeat(HQ, 0)
        .astype(np.float32),
        "inv_cnt": (1.0 / cnt).astype(np.float32).reshape(P, 32),
        "inv_w": (1.0 / w).astype(np.float32),
    }
    half = DR // 2
    inv = (np.float32(10000.0) ** (-np.arange(half, dtype=np.float32) / np.float32(half))).astype(np.float32)
    pos = np.concatenate([np.arange(SEQ), np.tile(PAGES * PAGE + np.arange(NS), NB)]).astype(np.float32)
    ang = (pos[None, :] * np.concatenate([inv, inv])[:, None]).astype(np.float32)
    lg = np.log1p(-np.exp2(-5.0 - np.arange(R))).astype(np.float32).astype(np.float64)
    dec = lambda n, gap, keep: np.where(keep, np.exp(np.where(keep, gap, 0) * lg[n]), 0.0)
    odd = {
        "cos": np.cos(ang.astype(np.float64)).astype(np.float32),
        "sin": np.sin(ang.astype(np.float64)).astype(np.float32),
        "swap": one(f == p + half) - one(p == f + half),
        "dec": np.concatenate([dec(n, f - p, f >= p) for n in range(R)], 1).astype(np.float32),
        "dec_s": np.concatenate([dec(n, g - q, same & (g >= q)) for n in range(R)], 1).astype(np.float32),
        "dec_q": np.concatenate([np.exp((f + 1) * lg[n]) + 0 * p for n in range(R)], 1).astype(np.float32),
        "dec_k": np.stack([np.exp((P - 1 - np.arange(P)) * lg[n]) for n in range(R)], 1).astype(np.float32),
        "dec_ks": np.stack([np.exp((NS - 1 - np.arange(TS) % NS) * lg[n]) for n in range(R)], 1).astype(np.float32),
        "same_s": one(same),
        "rep": one(np.arange(NS)[:, None] == np.arange(TS)[None, :] % NS),
        "of_seq": one(np.arange(TS)[:, None] // NS == np.arange(NB)[None, :]),
    }
    step = [math.exp(P * float(x)) for x in lg], [math.exp(NS * float(x)) for x in lg]

    def pack(parts):
        width = sum(a.shape[1] for a in parts.values())
        out, at, where = np.zeros((P, width), np.float32), 0, {}
        for name, a in parts.items():
            out[:a.shape[0], at:at + a.shape[1]] = a
            where[name] = (a.shape[0], at, a.shape[1])
            at += a.shape[1]
        return out, where

    return pack(even), pack(odd), step


class Steps:

    def __init__(self, eng, sem):
        self.eng, self.sem, self.n, self.more = eng, sem, 0, 0

    def __call__(self, ins):
        ins.then_inc(self.sem, 1)
        self.n += 1
        self.eng.wait_ge(self.sem, self.n + self.more)

    def loop(self, i, per):
        self.more, self.per, self.start = i * per, per, self.n

    def end(self, times):
        assert self.n - self.start == self.per, (self.n - self.start, self.per)
        self.n, self.more = self.start + self.per * times, 0


def hybrid_step(nc, I, O, where0, where1, decay_step):
    ctx = ExitStack()
    with ctx:
        def sb(name, shape, dt=F32):
            return ctx.enter_context(nc.sbuf_tensor(name, shape, dt))

        sems = {}

        def sem(name):
            if name not in sems:
                sems[name] = ctx.enter_context(nc.semaphore(name))
            return sems[name]

        h = sb("h", [P, KD, T])
        xn = sb("xn", [P, KD, T])
        big = sb("big", [P, 32, T])
        wring = sb("wring", [P, 2, UNIT])
        work = sb("work", [P, 2 * RING * FOX + 2 * 33 * HQ])
        c0 = sb("c0", [P, I["tab0"].shape[1]])
        prow = sb("prow", [NPARAM, P])
        pcol = sb("pcol", [P, NPARAM])
        rstd = sb("rstd", [P, T])
        cumT = sb("cumT", [H, T])
        cumn = sb("cumn", [P, (NT + 1) * H])
        lfn = sb("lfn", [P, (NT + 1) * H])
        ptab = sb("ptab", [1, NB * PAGES], I32)
        pidx = sb("pidx", [P, 2], I32)
        wf = sb("wf", [P, KD, H])
        bf = sb("bf", [H, 1])
        pwd = sb("pwd", [P, 2, P])
        stats = sb("stats", [HQ, 24])
        hstat = sb("hstat", [P, 6 * 4 + 8])
        ps = ctx.enter_context(nc.psum_tensor("ps", [P, 8, 512], F32))

        bigf = big[:, :, :].rearrange("p a t -> p (a t)")
        xnf = xn[:, :, :].rearrange("p a t -> p (a t)")

        def cst(name, lo=0, hi=None, rows=None):
            r, at, w = where0[name]
            return c0[0:rows or r, at + lo:at + (w if hi is None else hi)]

        ident = cst("ident")

        def param(name, j, rows=P):
            return pcol[0:rows, PROW[name] + j:PROW[name] + j + 1]

        def slot(name, j=0):
            return (FIRST[name] + j) % 4

        def bankA(s, n=512, rows=P):
            return ps[0:rows, 2 * s, 0:n]

        def bankB(s, n=TS, rows=P):
            return ps[0:rows, 2 * s + 1, 0:n]

        xstage = bigf[:, 0:NT * DM].rearrange("p (t n) -> p t n", t=NT)
        xstage_s = bigf[0:TS, NT * DM:(NT + 1) * DM]
        at0 = 20 * T
        sfx = bigf[:, at0:at0 + NB * PAGES * H]
        vs = bigf[:, at0 + 3072:at0 + 3840]
        qall = bigf[:, at0 + 3840:at0 + 5376].rearrange("p (b f c) -> p b f c", b=NB, f=HB)
        knew = bigf[:, at0 + 5376:at0 + 5760].rearrange("p (f t) -> p f t", f=HB)
        qcur = bigf[:, at0 + 5760:at0 + 5952].rearrange("p (f c) -> p f c", f=HB)
        key_bias = bigf[0:HQ, at0 + 6336:at0 + 6400]
        qgate = bigf[0:HQ, at0 + 6400:at0 + 6408]
        ostage = bigf[0:HQ, at0 + 6408:at0 + 6664]
        kT = bigf[:, 2 * T:2 * T + 2 * HB * GROUP * PAGE]\
            .rearrange("p (s f n) -> p s f n", s=2, f=HB)
        ptf = 2 * T + 2 * HB * GROUP * PAGE
        pTs = bigf[:, ptf:ptf + (PAGES + 1) * HQ].rearrange("p (g c) -> p g c", c=HQ)
        at1 = EV_V * T
        es = [bigf[:, at1 + 1536 + 368 * n:at1 + 1536 + 368 * (n + 1)].rearrange("p (a b t) -> p a b t", a=2, b=NB)
              for n in range(2)]
        hstage = bigf[0:NB * HIST, at0 + 6408:at0 + 6664]
        hcopy = bigf[:, at1 + 2528:at1 + 2768].rearrange("p (a t) -> p a t", a=2)
        hout = bigf[0:NB * HIST, at1 + 2768:at1 + 3024]
        hout_p = bigf[0:HIST, at1 + 3024:at1 + 3280]
        W1 = 2 * RING * FOX
        k_ring = work[:, 0:RING * FOX].rearrange("p (s n) -> p s n", s=RING)
        v_ring = work[:, RING * FOX:W1].rearrange("p (s n) -> p s n", s=RING)
        W2 = W1 + 33 * HQ
        S = work[0:HQ, W1:W1 + PAGES * PAGE + TS]
        SG = W1 + PAGES * PAGE + TS
        sgate = work[:, SG:SG + 2 * GROUP * HQ].rearrange("p (s c) -> p s c", s=2)
        lg = work[:, 0:3072].rearrange("p (a s h) -> p a s h", a=2, h=H)
        kstage = work[:, 0:3840].rearrange("p (t n) -> p t n", t=NT + 1)
        lT = xnf[:, 0:3072].rearrange("p (a h g) -> p a h g", a=2, h=H)
        lcT = work[:, W1:W1 + 3072].rearrange("p (a h g) -> p a h g", a=2, h=H)
        z = [work[0:H, W2 + T * n:W2 + T * (n + 1)] for n in range(4)]
        vn0 = work[:, W2:W2 + NT * FOX].rearrange("p (t n) -> p t n", t=NT)
        qz = work[:, W1:W1 + 1024].rearrange("p (s n) -> p s n", s=2)
        ep = [work[:, W1 + 1024:W1 + 1024 + 2 * EXT].rearrange("p (a t) -> p a t", a=2),
              bigf[:, at1:at1 + 2 * EXT].rearrange("p (a t) -> p a t", a=2)]
        eb = work[:, 0:2048].rearrange("p (s n) -> p s n", s=4)
        pT = work[:, 2048:6144].rearrange("p (s j n) -> p s j n", s=2, j=NT)
        diag = work[:, W1 + 1024 + 2 * EXT:W1 + 1024 + 2 * EXT + 4 * P]\
            .rearrange("p (s n) -> p s n", s=4)
        ngate = rstd[0:H, 0:SEQ]
        KZ = W1 + 1024 + 2 * EXT + 4 * P
        kz = [xn[:, KD - 1, 0:SEQ], work[:, KZ:KZ + SEQ]]
        col = lambda n, w=1: stats[:, n:n + w]
        smax, gmax, gfull, sshift, ssum, sden, srec = col(0, 9), col(9), col(10), col(11), col(12, 5), col(17), col(18)
        c1 = work[:, 0:I["tab1"].shape[1]]
        O1 = I["tab1"].shape[1]

        def cst1(name, lo=0, hi=None, rows=None):
            r, at, w = where1[name]
            return c1[0:rows or r, at + lo:at + (w if hi is None else hi)]

        def take(n):
            nonlocal O1
            O1 += n
            assert O1 <= 2 * RING * FOX + 2 * 33 * HQ
            return work[:, O1 - n:O1]

        wsn = take(512).rearrange("p (g s) -> p g s", g=4)
        vnn = take(2560).rearrange("p (t n) -> p t n", t=NT + 1)
        vmask = vnn.rearrange("p t n -> p (t n)")[0:TS, 0:1024].rearrange("p (b e) -> p b e", b=NB)
        s_out = vnn.rearrange("p t n -> p (t n)")[:, 1024:2048].rearrange("p (b e) -> p b e", b=NB)
        kn = take(2560).rearrange("p (t n) -> p t n", t=NT + 1)
        v2 = take(2560).rearrange("p (t n) -> p t n", t=NT + 1)
        lnsq = kn.rearrange("p t n -> p (t n)")[:, 0:4 * T].rearrange("p (f t) -> p f t", f=4)
        swish = v2.rearrange("p t n -> p (t n)")[:, 0:4 * T].rearrange("p (f t) -> p f t", f=4)
        sct = take(T)
        st = bigf[:, 24 * T + 4096:24 * T + 4608].rearrange("p (n e) -> p n e", n=NT)
        s0 = bigf[:, 24 * T:24 * T + 4096].rearrange("p (h b e) -> p h b e", h=R, b=NB)
        wT = take(512).rearrange("p (g t) -> p g t", g=4)
        w8 = take(256)[0:TS, :].rearrange("p (g t) -> p g t", g=4)
        bsr = cumT[0:1, 0:512]
        tmp = sct
        yrow = work[:, 0:5 * DM].rearrange("p (t n) -> p t n", t=NT + 1)
        gain = work[:, 5 * DM:6 * DM]
        raw = work[:, 6 * DM:6 * DM + KD * 5 * P].rearrange("p (f t n) -> p f t n", f=KD, t=NT + 1)
        ssq = hstat[:, 0:NT + 1]
        sumsq = rstd[:, 0:5 * KD].rearrange("p (t f) -> p t f", t=NT + 1)
        hlast = xn[:, 1:3, :]

        block_in = sem("block_filled")
        out_of = {"scalar": sem("emptied_by_scalar"), "vector": sem("emptied_by_vector")}

        def wait_emptied(eng, n):
            eng.wait_ge(out_of[OWNER[n - 1]], emptied_by(OWNER[n - 1], n))

        w_in = [sem("weights_in_0"), sem("weights_in_1")]
        k_in = [sem(f"k_page_in_{n}") for n in range(RING)]
        v_in = [sem(f"v_page_in_{n}") for n in range(RING)]

        blk = ctx.enter_context(nc.Block())

        @blk.sync
        def _(sp):
            sp.dma_start(xstage, I["x_prompt"][0].rearrange("(t p) n -> p t n", p=P)).then_inc(sem("x_in"), 16)
            sp.dma_start(xstage_s, I["x_sample"].rearrange("b s n -> (b s) n")).then_inc(sem("x_in"), 16)
            sp.dma_start(ptab[:, :], I["page_table"].rearrange("b g -> (b g)").rearrange("(o n) -> o n", o=1))\
                .then_inc(sem("ptab_in"), 16)

            def unit(stage, j):
                u = UFIRST[stage] + j
                if u >= 2:
                    for name, n, per in WEIGHTS:
                        m = u - 2 - UFIRST[name]
                        if 0 <= m < n:
                            sp.wait_ge(block_in, IN1_USED[m] if name == "in1" else down_block(m) + 1
                                       if name == "down1" else FIRST[name] + (m + 1) * per)
                layer = int(stage[-1])
                if stage[:-1] == "down":
                    src = I["w_down"][layer, :, j * P:(j + 1) * P].rearrange("(k p) n -> p k n", p=P)
                    dst = wring[:, u % 2, :].rearrange("p (k n) -> p k n", n=P)
                else:
                    w = {"in0": I["w_in_even"][0], "out0": I["w_out_even"][0], "in1": I["w_in_odd"][0],
                         "out1": I["w_out_odd"][0], "up0": I["w_up"][0], "up1": I["w_up"][1]}[stage]
                    at = IN1[j] * P if stage == "in1" else j * 512
                    src = w[:, at:at + 512].rearrange("(k p) n -> p k n", p=P)
                    dst = wring[:, u % 2, :].rearrange("p (k n) -> p k n", n=512)
                sp.dma_start(dst, src).then_inc(w_in[u % 2], 16)

            for j in range(5):
                unit("in0", j)
            unit("out0", 0)
            unit("out0", 1)

            sp.wait_ge(sem("ptab_in"), 16)
            sp.wait_ge(sem("ngate_ready"), 1)
            sp.wait_ge(sem("qz_zeroed"), 1)
            sp.wait_ge(sem("kz_zeroed"), 1)
            for hd in range(H):
                if hd >= 2:
                    sp.wait_ge(sem("scores_made"), NT * (hd - 1))
                r = 64 * (1 - hd % 2)
                sp.dma_start(kz[hd % 2][r:r + 1, :], ngate[hd:hd + 1, :]).then_inc(sem(f"gates_in_{hd % 2}"), 16)
            sp.wait_ge(sem("fox_prompt_done"), H)

            def page_ids(b, p):
                _, ids = nc.values_load_multi_w_load_instructions(
                    ptab[0:1, bass.ds(b * PAGES + p, RING)], engines=[mybir.EngineType.SP], min_val=0,
                    max_val=NPHYS - 1)
                return ids

            def page(cache, b, p, ids):
                ring, arrived, used = (k_ring, k_in, sem("k_page_used")) if cache == "cache_k" else \
                    (v_ring, v_in, sem("v_page_used"))
                if not isinstance(b, int) or b * PAGES + p >= RING:
                    sp.wait_ge(used, b * PAGES + p - RING + 1)
                sp.dma_start(ring[:, p % RING, :],
                             I[cache][0, bass.ds(ids[p % RING], 1)].rearrange("o p h d -> (o p) (h d)"))\
                    .then_inc(arrived[p % RING], 16)

            def phase(c, k=True, ending=True, starting=True):
                for p in range(0, PAGES, RING):
                    if k:
                        k_ids = page_ids(c, p)
                    v, q = (c - 2, PAGES - LAG + p) if p < LAG else (c - 1, p - LAG)
                    with_v = ending if p < LAG else starting
                    if with_v:
                        v_ids = page_ids(v, q)
                    for m in range(RING):
                        if k:
                            page("cache_k", c, p + m, k_ids)
                        if with_v:
                            page("cache_v", v, q + m, v_ids)

            phase(0, ending=False, starting=False)
            phase(1, ending=False)
            with sp.Fori(2, NB) as c:
                phase(c)
            phase(NB, k=False)
            for q in range(PAGES - LAG, PAGES, RING):
                ids = page_ids(NB - 1, q)
                for m in range(RING):
                    page("cache_v", NB - 1, q + m, ids)

            for name, n, _ in WEIGHTS[2:]:
                for j in range(n):
                    unit(name, j)

            yp = O["y_prompt"][0].rearrange("(t p) n -> t p n", p=P)
            for t in range(NT + 1):
                by = "scalar" if t % 2 else "vector"
                sp.wait_ge(sem(f"rows_scaled_by_{by}"), t // 2 + 1)
                dst = yp[t] if t < NT else O["y_sample"].rearrange("b s n -> (b s) n")
                sp.dma_start(dst, yrow[0:P if t < NT else TS, t, :]).then_inc(sem("y_stored"), 16)
            sp.wait_ge(sem("y_stored"), 16 * (NT + 1))

        @blk.gpsimd
        def _(pool):
            own = Steps(pool, sem("pool_steps"))
            pool.dma_start(c0[:, 2 * P:], I["tab0"][:, 2 * P:]).then_inc(sem("tab0_in"), 16)
            pool.dma_start(wf[:, :, :], I["w_in_even"][0, :, EV - H:EV].rearrange("(k p) n -> p k n", p=P))\
                .then_inc(sem("wf_in"), 16)
            pool.dma_start(bf[:, :], I["b_forget"].rearrange("o h -> h o")).then_inc(sem("wf_in"), 16)
            for a in range(2):
                rows = I["page_table"][4 * a:4 * a + 4, :].rearrange("b g -> (b g)").rearrange("(n o) -> n o", o=1)
                pool.dma_start(pidx[:, a:a + 1], rows).then_inc(sem("pidx_in"), 16)
            pool.dma_start(hstage, I["state_pool"][0].rearrange("b t c -> (b t) c")).then_inc(sem("hist_in"), 16)
            own(pool.memset(pwd[:, :, :], 0.0))
            for g in range(4):
                r = slice(64 * (g % 2), 64 * (g % 2) + 64)
                pool.dma_start(pwd[r, g // 2, r], I["pool_w"][0, g]).then_inc(sem("pwd_in"), 16)
            pool.wait_ge(sem("pidx_in"), 32)
            flat = I["cache_logf"][0].rearrange("n s h -> n (s h)")
            for a in range(2):
                pool.indirect_dma_start(lg[:, a].rearrange("p s h -> p (s h)"), None, flat,
                                        bass.IndirectOffsetOnAxis(ap=pidx[:, a:a + 1], axis=0))\
                    .then_inc(sem("lg_in"), 16)

            pool.wait_ge(sem("lfn_ready"), 1)
            pool.dma_start(O["logf_prompt"][0, 0].rearrange("(t p) h -> p t h", p=P),
                           lfn[:, 0:NT * H].rearrange("p (t h) -> p t h", h=H)).then_inc(sem("stored"), 16)
            pool.dma_start(O["logf_sample"][0].rearrange("b s h -> (b s) h"), lfn[0:TS, NT * H:(NT + 1) * H])\
                .then_inc(sem("stored"), 16)
            wait_emptied(pool, FIRST["sfx"] + 6)
            own(pool.memset(qz, 0.0))
            own(pool.memset(kz[1], 0.0))
            own(pool.memset(qz[64:65, 0, :], 1.0))
            pool.memset(qz[0:1, 1, :], 1.0).then_inc(sem("qz_zeroed"), 1)

            kp = O["k_prompt"][0, 0].rearrange("(t p) h d -> t p (h d)", p=P)
            for t in range(NT + 1):
                wait_emptied(pool, FIRST["knat"] + t + 1)
                dst = kp[t] if t < NT else O["k_sample"][0].rearrange("b s h d -> (b s) (h d)")
                pool.dma_start(dst, kstage[0:P if t < NT else TS, t, :]).then_inc(sem("k_stored"), 16)
            wait_emptied(pool, FIRST["vnat"] + NT)
            pool.dma_start(O["v_prompt"][0, 0].rearrange("(t p) h d -> p t (h d)", p=P), vn0)\
                .then_inc(sem("v_stored"), 16)
            wait_emptied(pool, FIRST["vnat"] + NT + 1)
            pool.dma_start(O["v_sample"][0].rearrange("b s h d -> (b s) (h d)"), vs[0:TS, :])\
                .then_inc(sem("v_stored"), 16)
            own(pool.memset(ep[0][:, :, 0:HIST], 0.0))
            own(pool.tensor_copy(ep[0][:, :, HIST:EXT], big[:, 0:2, 0:SEQ]))
            add = lambda o, a, b: own(pool.tensor_tensor(o, a, b, ALU.add))

            def group(src, rows, a):
                inv = cst("inv_w", a, a + 1)[rows, :]
                dst = xn[rows, a, 0:SEQ]
                own(pool.tensor_scalar(dst, src[rows, a, HIST:EXT], inv, None, ALU.mult))
                own(pool.tensor_tensor(xn[rows, a, 0:16], src[rows, a, HIST:HIST + 16],
                                       cst("inv_cnt", 16 * a, 16 * a + 16)[rows, :], ALU.mult))
                own(pool.tensor_tensor(dst, dst, big[rows, a, 0:SEQ], ALU.subtract))

            def group_s(src, rows, a):
                inv = cst("inv_w", a, a + 1)[rows, :]
                dst = xn[rows, a, SEQ:T].rearrange("p (b s) -> p b s", b=NB)
                own(pool.tensor_scalar(dst, src[rows, a, :, HIST:HIST + NS], inv, None, ALU.mult))
                own(pool.tensor_tensor(dst, dst, big[rows, a, SEQ:T].rearrange("p (b s) -> p b s", b=NB),
                                       ALU.subtract))

            lo, hi = slice(0, 64), slice(64, 128)
            e, f = ep
            add(f[:, :, 1:EXT], e[:, :, 1:EXT], e[:, :, 0:EXT - 1])
            group(f, lo, 0)
            add(e[:, :, 3:EXT], f[:, :, 3:EXT], f[:, :, 1:EXT - 2])
            group(e, hi, 0)
            add(f[:, 1, 7:EXT], e[:, 1, 7:EXT], e[:, 1, 3:EXT - 4])
            group(f, lo, 1)
            add(e[:, 1, 15:EXT], f[:, 1, 15:EXT], f[:, 1, 7:EXT - 8])
            group(e, hi, 1)
            pool.wait_ge(sem("ext_s_ready"), 2)
            e, f = es
            N = HIST + NS
            add(f[:, :, :, 1:N], e[:, :, :, 1:N], e[:, :, :, 0:N - 1])
            group_s(f, lo, 0)
            add(e[:, :, :, 3:N], f[:, :, :, 3:N], f[:, :, :, 1:N - 2])
            group_s(e, hi, 0)
            add(f[:, 1, :, 7:N], e[:, 1, :, 7:N], e[:, 1, :, 3:N - 4])
            group_s(f, lo, 1)
            add(e[:, 1, :, 15:N], f[:, 1, :, 15:N], f[:, 1, :, 7:N - 8])
            group_s(e, hi, 1)
            own(pool.memset(hstat[0:1, 24:25], 0.0))
            pool.memset(hstat[0:1, 25:26], 0.0).then_inc(sem("pool_d_ready"), 1)
            pool.wait_ge(sem("hist_out_ready"), 1)
            pool.dma_start(O["pool_sample"][0].rearrange("b t c -> (b t) c"), hout).then_inc(sem("stored"), 16)
            pool.dma_start(O["pool_prompt"][0, 0], hout_p).then_inc(sem("stored"), 16)

            pool.wait_ge(sem("outputs_placed"), NB + 1)
            pool.wait_ge(sem("v_stored"), 32)
            pool.dma_start(c1, I["tab1"]).then_inc(sem("tab1_in"), 16)
            pool.dma_start(bsr, I["gmlp_bs"].rearrange("o g t -> o (g t)")).then_inc(sem("bs_in"), 16)
            pool.dma_start(wsn, I["gmlp_ws"][0].rearrange("g t s -> t g s")).then_inc(sem("ws_in"), 16)
            pool.wait_ge(block_in, FIRST["down0"] + 8)
            for n in range(R):
                pool.dma_start(s0[:, n], I["state_ret"][0, :, n].rearrange("b d e -> d b e")).then_inc(sem("s0_in"), 16)
            wait_emptied(pool, FIRST["vnat1"] + NT + 1)
            pool.dma_start(O["gmlp_v_sample"][0].rearrange("b s c -> (b s) c"), vnn[0:TS, NT, :])\
                .then_inc(sem("gv_stored"), 16)
            for n in range(R):
                pool.wait_ge(sem("ret_state_ready"), n + 1)
                pool.dma_start(O["ret_prompt"][0, 0, n], st[:, NT - 1, :]).then_inc(sem("ret_stored"), 16)
                pool.dma_start(O["ret_sample"][0, :, n].rearrange("b d e -> d b e"), s_out)\
                    .then_inc(sem("ret_stored"), 16)
            pool.wait_ge(sem("ret_stored"), 32 * R)
            pool.wait_ge(block_in, FIRST[f"hvar_{R - 1}"] + 1)
            pool.dma_start(gain, I["norm_final"].rearrange("(o n) -> o n", o=1).broadcast_to([P, DM]))\
                .then_inc(sem("gain_in"), 16)
            pool.wait_ge(sem("stored"), 64)
            pool.wait_ge(sem("k_stored"), 80)
            pool.wait_ge(sem("gv_stored"), 16)
            pool.wait_ge(sem("ret_stored"), 32 * R)

        @blk.tensor
        def _(pe):
            mm = nc.tensor.matmul
            tr = nc.tensor.transpose

            def open_block(n):
                if n >= 4:
                    wait_emptied(pe, n - 3)

            def tiles(x, n=KD):
                return [x[:, k, :] for k in range(n)]

            def gemm(stage, rhs, ready=None, units=None):
                _, all_units, per = next(w for w in WEIGHTS if w[0] == stage)
                units = units or all_units
                ks = UNIT // (512 if per == 4 else P)
                body = 2 if per == 4 else 4

                def unit(j, i, first=False):
                    u = UFIRST[stage] + j
                    pe.wait_ge(w_in[u % 2], 16 * (u // 2 + 1) + i * (16 * body // 2))
                    for m in range(per):
                        n = j * per + m
                        s = slot(stage, n)
                        if isinstance(i, int):
                            open_block(FIRST[stage] + n)
                        else:
                            who = OWNER[FIRST[stage]]
                            pe.wait_ge(out_of[who], i * (body * per) + emptied_by(who, FIRST[stage]) + n - 3)
                        for k in range(ks):
                            if first and m == 0 and ready and ready[1] + k + 1 > 0:
                                pe.wait_ge(sem(ready[0]), ready[1] + k + 1)
                            at = k * (512 if per == 4 else P) + m * P
                            w = wring[:, u % 2, at:at + P]
                            mm(bankA(s, TH), w, rhs[k][:, 0:TH], start=(k == 0), stop=(k == ks - 1))
                            last = mm(bankB(s, TH), w, rhs[k][:, TH:T], start=(k == 0), stop=(k == ks - 1))
                        last.then_inc(block_in, 1)

                j = 0
                if ready:
                    for j in range(body):
                        unit(j, 0, first=(j == 0))
                    j = body
                loops = (units - j) // body
                if loops > 1:
                    for n in range(4 if j == 0 else 0):
                        open_block(FIRST[stage] + n)
                    with pe.Fori(0, loops) as i:
                        for m in range(body):
                            unit(j + m, i)
                elif loops == 1:
                    for m in range(body):
                        unit(j + m, 0)
                for m in range(j + loops * body, units):
                    unit(m, 0)

            def ones_sum(stage, j, ready, base, src, ks):
                s = slot(stage, j)
                open_block(FIRST[stage] + j)
                for k in range(ks):
                    pe.wait_ge(sem(ready), base + k + 1)
                    mm(bankA(s, TH), cst("ones"), src[:, k, 0:TH], start=(k == 0), stop=(k == ks - 1))
                    last = mm(bankB(s, TH), cst("ones"), src[:, k, TH:T], start=(k == 0), stop=(k == ks - 1))
                last.then_inc(block_in, 1)

            pe.wait_ge(sem("ident_in"), 16)
            pe.wait_ge(sem("x_in"), 32)
            for f in range(KD):
                s = slot("x", f)
                open_block(f)
                for t in range(NT):
                    tr(ps[:, 2 * s, t * P:(t + 1) * P], xstage[:, t, f * P:(f + 1) * P], ident)
                tr(bankB(s), xstage_s[:, f * P:(f + 1) * P], ident[0:TS, 0:TS]).then_inc(block_in, 1)
            ones_sum("norm0", 0, "sq_ready", 0, xn, KD)
            pe.wait_ge(sem("tab0_in"), 16)
            pe.wait_ge(sem("params_in"), 16 * len(PARAMS))
            wait_emptied(pe, KD)
            tr(ps[:, 7, 0:NPARAM], prow[:, :], ident[0:NPARAM, 0:NPARAM]).then_inc(sem("params_turned"), 1)
            pe.wait_ge(sem("params_ready"), 1)
            gemm("in0", tiles(xn), ("xn_ready", 0))

            s = slot("logf")
            open_block(FIRST["logf"])
            pe.wait_ge(sem("wf_in"), 32)
            for k in range(KD):
                mm(bankA(s, TH, H), wf[:, k, :], xn[:, k, 0:TH], start=(k == 0), stop=(k == KD - 1))
                last = mm(bankB(s, TH, H), wf[:, k, :], xn[:, k, TH:T], start=(k == 0), stop=(k == KD - 1))
            last.then_inc(block_in, 1)

            pe.wait_ge(sem("lg_in"), 32)
            for n in range(H):
                s = slot("sfxT", n)
                open_block(FIRST["sfxT"] + n)
                for a in range(2):
                    page = lg[:, a, :, n]
                    mm(ps[:, 2 * s, a * P:(a + 1) * P], page, ident, start=True, stop=True)
                    last = mm(ps[:, 2 * s + 1, a * P:(a + 1) * P], page, cst("later_page"), start=True, stop=True)
                last.then_inc(block_in, 1)

            def heads_to_tokens(stage, src):
                s = slot(stage)
                open_block(FIRST[stage])
                for t in range(NT):
                    tr(ps[:, 2 * s, t * H:(t + 1) * H], src[0:H, t * P:(t + 1) * P], ident[0:H, 0:H])
                tr(bankB(s, H, TS), src[0:H, SEQ:T], ident[0:H, 0:H]).then_inc(block_in, 1)

            pe.wait_ge(sem("logf_ready"), 1)
            heads_to_tokens("logfT", z[3])
            lf = lT.rearrange("p a h g -> p (a h g)")
            lcf = lcT.rearrange("p a h g -> p (a h g)")
            wait_emptied(pe, FIRST["sfxT"] + H)
            for n in range(6):
                s = slot("sfx", n)
                open_block(FIRST["sfx"] + n)
                mm(bankA(s), cst("later"), lf[:, n * 512:(n + 1) * 512], start=True, stop=False)
                mm(bankA(s), cst("ones"), lcf[:, n * 512:(n + 1) * 512], start=False, stop=True).then_inc(block_in, 1)

            pe.wait_ge(sem("lfn_ready"), 1)
            s = slot("cum")
            open_block(FIRST["cum"])
            for t in range(NT):
                mm(ps[0:H, 2 * s, t * P:SEQ], lfn[:, t * H:(t + 1) * H], cst("upto", 0, SEQ - t * P),
                   start=(t == 0), stop=(t == NT - 1))
            mm(bankB(s, rows=H), lfn[0:TS, NT * H:(NT + 1) * H], cst("upto_s"), start=True, stop=True)\
                .then_inc(block_in, 1)
            for stage, first in (("knat", EV_K), ("vnat", EV_V)):
                if stage == "vnat":
                    wait_emptied(pe, FIRST["cum"] + 1)
                    heads_to_tokens("cumT", cumT)
                for t in range(NT + 1):
                    s = slot(stage, t)
                    open_block(FIRST[stage] + t)
                    rows, cols = (P, slice(t * P, (t + 1) * P)) if t < NT else (TS, slice(SEQ, T))
                    for f in range(HB):
                        at = f * P
                        last = tr(ps[0:rows, 2 * s + at // 512, at % 512:at % 512 + P], big[:, first + f, cols], ident)
                    last.then_inc(block_in, 1)

            pe.wait_ge(sem("hist_in"), 16)
            for a in range(2):
                s = slot("hist", a)
                open_block(FIRST["hist"] + a)
                tr(ps[:, 2 * s, 0:NB * HIST], hstage[:, a * P:(a + 1) * P], ident[0:NB * HIST, 0:NB * HIST])\
                    .then_inc(block_in, 1)

            s = slot("g96")
            open_block(FIRST["g96"])
            mm(ps[0:HQ, 2 * s, 0:TS], cst("head_of"), cumT[0:H, SEQ:T], start=True, stop=True).then_inc(block_in, 1)

            wait_emptied(pe, FIRST["g96"] + 1)
            NSTEP = H * NT

            def score(n):
                hd, i = n // NT, n % NT
                if i == 0:
                    pe.wait_ge(sem("keys_in"), hd + 1)
                    pe.wait_ge(sem(f"gates_in_{hd % 2}"), 16 * (hd // 2 + 1))
                if n >= 4:
                    pe.wait_ge(sem("probs_made"), n - 3)
                w = (i + 1) * P
                bank = ps[:, (0, 1, 2, 7)[n % 4], :]
                mm(bank[:, 0:w], qz[:, hd % 2, i * P:w], kz[hd % 2][:, 0:w], start=True, stop=False)
                mm(bank[:, i * P:w], ident, cst("mask"), start=False, stop=True).then_inc(sem("scores_made"), 1)

            def turn(n):
                hd, i = n // NT, n % NT
                pe.wait_ge(sem("probs_made"), n + 1)
                pe.wait_ge(sem("diag_ready"), n + 1)
                if n >= 3:
                    pe.wait_ge(sem("probs_turned_copied"), n - 2)
                for j in range(i + 1):
                    last = mm(ps[:, 3 + n % 3, j * P:(j + 1) * P], eb[:, n % 4, j * P:(j + 1) * P], diag[:, n % 4, :],
                              start=True, stop=True)
                last.then_inc(sem("probs_turned"), 1)

            def weigh(hd):
                pe.wait_ge(sem("probs_turned_copied"), NT * (hd + 1))
                if hd >= 1:
                    pe.wait_ge(sem("fox_prompt_done"), hd)
                f = hd // 2
                for j in range(NT):
                    last = mm(ps[:, 6, j * P:SEQ], vn0[:, j, f * P:(f + 1) * P], pT[:, hd % 2, j, j * P:SEQ],
                              start=(j == 0), stop=(j == NT - 1))
                last.then_inc(sem("fox_prompt_out"), 1)

            for n in range(NSTEP + 5):
                if n < NSTEP:
                    score(n)
                if 3 <= n < NSTEP + 3:
                    turn(n - 3)
                if n >= 5 and (n - 5) % NT == NT - 1:
                    weigh((n - 5) // NT)

            pe.wait_ge(sem("hist_copied"), 1)
            for a in range(2):
                tr(ps[0:NB * HIST, a, 0:P], hcopy[:, a, :], ident)
                last = tr(ps[0:HIST, a, P:2 * P], big[:, a, SEQ - HIST:SEQ], ident)
            last.then_inc(sem("hist_turned"), 1)
            pe.wait_ge(sem("pwd_in"), 64)
            pe.wait_ge(sem("pool_d_ready"), 1)
            pe.wait_ge(sem("fox_prompt_done"), H)
            for a in range(2):
                mm(ps[:, 4 + a, :], pwd[:, a, :], xn[:, a, 0:SEQ], start=True, stop=True)
                last = mm(ps[:, 6 + a, 0:TS], pwd[:, a, :], xn[:, a, SEQ:T], start=True, stop=True)
            last.then_inc(sem("pooled"), 1)

            pe.wait_ge(sem("hist_out_ready"), 1)
            pe.wait_ge(sem("pool_mixed"), 1)
            pe.wait_ge(sem("queries_placed"), 2)
            pe.wait_ge(sem("v_stored"), 32)

            def turn_page(b, p):
                k = b * PAGES + p
                pe.wait_ge(k_in[p % RING], 16 * (b * (PAGES // RING) + p // RING + 1))
                static = isinstance(b, int)
                if not static or k >= 2:
                    pe.wait_ge(sem("kT_low"), k - 1)
                    pe.wait_ge(sem("kT_high"), k - 1)
                for f in range(HB):
                    at = f * P
                    last = tr(ps[:, 2 * (p % 2) + at // 512, at % 512:at % 512 + P],
                              k_ring[:, p % RING, at:at + P], ident)
                last.then_inc(sem("k_page_used"), 1)

            def score_group(b, g):
                first = isinstance(b, int) and b == 0
                pe.wait_ge(sem("kT_low"), b * PAGES + (g + 1) * GROUP)
                pe.wait_ge(sem("kT_high"), b * PAGES + (g + 1) * GROUP)
                if g == 0:
                    pe.wait_ge(sem("queries_staged"), b + 1)
                pe.wait_ge(sem("suffix_staged"), b * GROUPS + g + 1)
                if g >= 2:
                    pe.wait_ge(sem("scores_in"), b * (GROUPS + 1) + g - 1)
                elif not first:
                    pe.wait_ge(sem("scores_in"), b * (GROUPS + 1))
                bank = 4 + g % 2
                for half in range(2):
                    for j in range(JT):
                        mm(ps[32 * j:32 * j + 32, bank, :], qcur[:, 2 * j + half, :], kT[:, g % 2, 2 * j + half, :],
                           start=(half == 0), stop=False)
                for m in range(GROUP):
                    for j in range(JT):
                        at = m * HQ + 32 * j
                        last = mm(ps[32 * j:32 * j + 32, bank, m * PAGE:(m + 1) * PAGE],
                                  sgate[:, g % 2, at:at + 32], ident, start=False, stop=(m == GROUP - 1))
                last.then_inc(sem("groups_scored"), 1)

            def score_new(b):
                pe.wait_ge(sem("scores_in"), b * (GROUPS + 1) + GROUPS - 1)
                for half in range(2):
                    for j in range(JT):
                        last = mm(ps[32 * j:32 * j + 32, 4, 0:TS], qcur[:, 2 * j + half, :], knew[:, 2 * j + half, :],
                                  start=(half == 0), stop=(half == 1))
                last.then_inc(sem("new_scored"), 1)

            def turn_probs(b, g):
                pe.wait_ge(sem("exp_done"), b * (EXPS + 1) + g // 2 + 1)
                if g:
                    pe.wait_ge(sem("probs_in"), b * (GROUPS + 1) + g)
                elif not (isinstance(b, int) and b == 0):
                    pe.wait_ge(sem("outputs_placed"), b)
                if g == GROUPS:
                    last = mm(ps[0:TS, 6, 0:HQ], S[:, PAGES * PAGE:PAGES * PAGE + TS], ident[0:HQ, 0:HQ],
                              start=True, stop=True)
                else:
                    for m in range(GROUP):
                        at = (g * GROUP + m) * PAGE
                        last = tr(ps[:, 6, m * HQ:(m + 1) * HQ], S[:, at:at + PAGE], ident[0:HQ, 0:HQ])
                last.then_inc(sem("probs_turned_s"), 1)

            def turn_out(b):
                pe.wait_ge(sem("out_scaled"), b + 1)
                if not isinstance(b, int) or b < NB - 1:
                    pe.wait_ge(sem("probs_in"), (b + 2) * (GROUPS + 1))
                else:
                    pe.wait_ge(sem("outputs_placed"), NB)
                for c in range(2):
                    last = tr(ps[:, 6, c * HQ:(c + 1) * HQ], ostage[:, c * P:(c + 1) * P], ident[0:HQ, 0:HQ])
                last.then_inc(sem("out_turned"), 1)

            def weigh_page(b, p):
                if p == 0 and not (isinstance(b, int) and b == 0):
                    pe.wait_ge(sem("out_scaled"), b)
                if p < PAGES:
                    pe.wait_ge(v_in[p % RING], 16 * (b * (PAGES // RING) + p // RING + 1))
                if p % GROUP == 0:
                    pe.wait_ge(sem("probs_in"), b * (GROUPS + 1) + p // GROUP + 1)
                for j in range(JT):
                    v = v_ring[:, p % RING, 256 * j:256 * j + 256] if p < PAGES else vs[:, 256 * j:256 * j + 256]
                    last = mm(ps[32 * j:32 * j + 32, 7, 0:256], pTs[:, p, 32 * j:32 * j + 32], v,
                              start=(p == 0), stop=(p == PAGES))
                last.then_inc(sem("v_page_used") if p < PAGES else sem("fox_sample_out"), 1)

            def phase(c, k=True, ending=True, starting=True):
                for p in range(PAGES):
                    if k:
                        turn_page(c, p)
                        if p >= GROUP and p % GROUP == 0:
                            score_group(c, p // GROUP - 1)
                    if p < LAG and ending:
                        weigh_page(c - 2, PAGES - LAG + p)
                        if p == LAG - 1:
                            weigh_page(c - 2, PAGES)
                    if p >= LAG and starting:
                        weigh_page(c - 1, p - LAG)
                    if starting and 3 <= p < 3 + GROUPS + 1:
                        turn_probs(c - 1, p - 3)
                    if ending and p == 14:
                        turn_out(c - 2)
                if k:
                    score_group(c, GROUPS - 1)
                    score_new(c)

            phase(0, ending=False, starting=False)
            phase(1, ending=False)
            with pe.Fori(2, NB) as c:
                phase(c)
            phase(NB, k=False)
            for q in range(PAGES - LAG, PAGES + 1):
                weigh_page(NB - 1, q)
            turn_out(NB - 1)

            pe.wait_ge(sem("outputs_placed"), NB + 1)
            gemm("out0", tiles(xn))
            ones_sum("norm1", 0, "sq_ready", KD, big, KD)
            gemm("up0", tiles(xn), ("xn_ready", KD))
            gemm("down0", tiles(big, 32), ("u_ready", 0))

            ones_sum("norm2", 0, "sq_ready", 2 * KD, xn, KD)
            gemm("in1", tiles(xn), ("xn_ready", 2 * KD), units=2)

            def block(j, m, n):
                u = UFIRST["in1"] + j
                s = n % 4
                pe.wait_ge(w_in[u % 2], 16 * (u // 2 + 1))
                open_block(n)
                for k in range(KD):
                    w = wring[:, u % 2, k * 512 + m * P:k * 512 + (m + 1) * P]
                    mm(bankA(s, TH), w, xn[:, k, 0:TH], start=(k == 0), stop=(k == KD - 1))
                    last = mm(bankB(s, TH), w, xn[:, k, TH:T], start=(k == 0), stop=(k == KD - 1))
                last.then_inc(block_in, 1)

            def swap_halves(stage, first):
                for n in range(R):
                    s = slot(stage, n)
                    open_block(FIRST[stage] + n)
                    mm(bankA(s, TH), cst1("swap"), big[:, first + n, 0:TH], start=True, stop=True)
                    mm(bankB(s, TH), cst1("swap"), big[:, first + n, TH:T], start=True, stop=True)\
                        .then_inc(block_in, 1)

            def to_rows(stage, first):
                for t in range(NT + 1):
                    s = slot(stage, t)
                    open_block(FIRST[stage] + t)
                    rows, cols = (P, slice(t * P, (t + 1) * P)) if t < NT else (TS, slice(SEQ, T))
                    for f in range(4):
                        last = tr(ps[0:rows, 2 * s, f * P:(f + 1) * P], big[:, first + f, cols], ident)
                    last.then_inc(block_in, 1)

            for m in range(4):
                block(2, m, FIRST["rq"] + m)
            s = slot("wst")
            open_block(FIRST["wst"])
            pe.wait_ge(sem("ws_in"), 16)
            for g in range(4):
                last = tr(ps[:, 2 * s, g * P:(g + 1) * P], wsn[:, g, :], ident)
            last.then_inc(block_in, 1)
            s = slot("w8")
            open_block(FIRST["w8"])
            wait_emptied(pe, FIRST["wst"] + 1)
            pe.wait_ge(sem("tab1_in"), 16)
            mm(ps[0:TS, 2 * s, 0:4 * NS], cst1("rep"), wT[0:NS, :, 0:NS], start=True, stop=True).then_inc(block_in, 1)
            ones_sum("mu", 0, "emptied_by_scalar", emptied_by("scalar", FIRST["in1"] + 4), big[:, OD_GV:OD_GV + 4, :], 4)
            for m in range(2):
                block(3, m, FIRST["rk_a"] + m)
            wait_emptied(pe, FIRST["rq"] + 4)
            swap_halves("rot_q", OD_RQ)
            for m in range(2):
                block(3, 2 + m, FIRST["rk_b"] + m)
            ones_sum("var", 0, "lnsq_ready", 0, lnsq, 4)
            for m in range(2):
                block(4, m, FIRST["rv_a"] + m)
            wait_emptied(pe, FIRST["rk_b"] + 2)
            swap_halves("rot_k", OD_RK)
            for m in range(2):
                block(4, 2 + m, FIRST["rv_b"] + m)
            pe.wait_ge(sem("ln_ready"), 4)
            to_rows("vnat1", OD_GV)
            wait_emptied(pe, FIRST["rv_b"] + 2)
            to_rows("vn", OD_RV)
            pe.wait_ge(sem("bs_in"), 16)
            wait_emptied(pe, FIRST["vnat1"] + NT + 1)
            for g in range(4):
                s = slot("z", g)
                open_block(FIRST["z"] + g)
                bias = bsr[0:1, g * P:(g + 1) * P].rearrange("p (o t) -> p o t", o=1)
                mm(bankA(s), cst("ones", rows=1), bias.broadcast_to([1, NT, P]), start=True, stop=False)
                for t in range(NT):
                    mm(ps[:, 2 * s, t * P:(t + 1) * P], vnn[:, t, g * P:(g + 1) * P], wT[:, g, :],
                       start=False, stop=(t == NT - 1))
                mm(bankB(s), cst("ones", rows=1), bias[:, :, 0:NS].broadcast_to([1, NB, NS]), start=True, stop=False)
                mm(bankB(s), vnn[0:TS, NT, g * P:(g + 1) * P], w8[:, g, :], start=False, stop=True)\
                    .then_inc(block_in, 1)
            pe.wait_ge(sem("rotated"), 2 * R)
            to_rows("kn", OD_RK)
            wait_emptied(pe, FIRST["vn"] + NT + 1)
            wait_emptied(pe, FIRST["kn"] + NT + 1)
            pe.wait_ge(sem("s0_in"), 16 * R)

            def head_mean(n):
                at = emptied_by("scalar", FIRST[f"ret_out_{n}"])
                ones_sum(f"hmu_{n}", 0, "emptied_by_scalar", at, big[:, OD_RQ + n:OD_RQ + n + 1, :], 1)

            def head_variance(n):
                ones_sum(f"hvar_{n}", 0, "hsq_ready", n, big[:, OD_RK + n:OD_RK + n + 1, :], 1)

            for n in range(R):
                base = FIRST[f"ret_{n}"]
                q, k = big[:, OD_RQ + n, :], big[:, OD_RK + n, :]
                cols = slice(n * P, (n + 1) * P)
                s = base % 4
                open_block(base)
                for t in range(NT):
                    mm(ps[:, 2 * s, t * P:(t + 1) * P], k[:, t * P:(t + 1) * P], q[:, t * P:(t + 1) * P],
                       start=True, stop=True)
                mm(bankB(s, rows=TS), k[:, SEQ:T], q[:, SEQ:T], start=True, stop=True).then_inc(block_in, 1)
                s = (base + 1) % 4
                open_block(base + 1)
                for t in range(NT):
                    last = mm(ps[:, 2 * s, t * P:(t + 1) * P], kn[:, t, cols], v2[:, t, cols], start=True, stop=True)
                last.then_inc(block_in, 1)
                s = (base + 2) % 4
                open_block(base + 2)
                pe.wait_ge(sem("v_spread"), n + 1)
                for a in range(2):
                    last = mm(ps[:, 2 * s + a, :], kn[0:TS, NT, cols], vmask[:, 4 * a:4 * a + 4, :],
                              start=True, stop=True)
                last.then_inc(block_in, 1)
                if n:
                    head_mean(n - 1)
                block(5, n, FIRST[f"u_{n}"])
                out = FIRST[f"ret_out_{n}"]
                s = out % 4
                open_block(out)
                pe.wait_ge(sem("q_decayed"), n + 1)
                pe.wait_ge(sem("states_ready"), n + 1)
                for t in range(NT):
                    o = ps[:, 2 * s, t * P:(t + 1) * P]
                    mm(o, v2[:, t, cols], sct[:, t * P:(t + 1) * P], start=True, stop=(t == 0))
                    if t:
                        mm(o, st[:, t - 1, :], q[:, t * P:(t + 1) * P], start=False, stop=True)
                mm(bankB(s), v2[0:TS, NT, cols], sct[0:TS, SEQ:T], start=True, stop=False)
                for b in range(NB):
                    last = mm(ps[:, 2 * s + 1, b * NS:(b + 1) * NS], s0[:, n, b, :],
                              q[:, SEQ + b * NS:SEQ + (b + 1) * NS], start=False, stop=(b == NB - 1))
                last.then_inc(block_in, 1)
                if n:
                    head_variance(n - 1)
            head_mean(R - 1)
            head_variance(R - 1)
            wait_emptied(pe, FIRST["u_3"] + 1)
            gemm("out1", tiles(big[:, OD_U:OD_U + 4, :], 4) + tiles(big[:, OD_RQ:OD_RQ + R, :], R), ("head_mixed", -4))
            ones_sum("norm3", 0, "sq_ready", 3 * KD, xn, KD)
            gemm("up1", tiles(xn), ("xn_ready", 3 * KD))

            before = emptied_by("vector", FIRST["down1"])

            def down(f, i, first=False):
                u = UFIRST["down1"] + f
                n = down_block(f)
                pe.wait_ge(w_in[u % 2], 16 * (u // 2 + 1) + i * 16)
                if not first:
                    pe.wait_ge(out_of["vector"], i * 4 + before + n - FIRST["down1"] - 3)
                s = n % 4
                for k in range(FF // P):
                    if first:
                        pe.wait_ge(sem("u_ready"), FF // P + k + 1)
                    w = wring[:, u % 2, k * P:(k + 1) * P]
                    mm(bankA(s, TH), w, big[:, k, 0:TH], start=(k == 0), stop=(k == FF // P - 1))
                    last = mm(bankB(s, TH), w, big[:, k, TH:T], start=(k == 0), stop=(k == FF // P - 1))
                last.then_inc(block_in, 1)

            def to_final_rows(f, i):
                n = rows_block(f)
                free, ready = n - FIRST["down1"] - 3, down_block(f) - FIRST["down1"] + 1
                pe.wait_ge(out_of["vector"], i * 4 + before + max(free, ready))
                s = n % 4
                for t in range(NT):
                    tr(ps[:, 2 * s, t * P:(t + 1) * P], hlast[:, f % 2, t * P:(t + 1) * P], ident)
                tr(bankB(s, P, TS), hlast[:, f % 2, SEQ:T], ident).then_inc(block_in, 1)

            wait_emptied(pe, FIRST["down1"])
            down(0, 0, first=True)
            with pe.Fori(0, 3) as i:
                for f in (1, 2):
                    down(f, i)
                    to_final_rows(f - 1, i)
            down(KD - 1, 0)
            to_final_rows(KD - 2, 0)
            to_final_rows(KD - 1, 0)

        @blk.scalar
        def _(act):
            own = Steps(act, sem("act_steps"))
            act.dma_start(c0[:, 0:2 * P], I["tab0"][:, 0:2 * P]).then_inc(sem("ident_in"), 16)
            for name, n in PARAMS:
                src = I[name]
                while len(src.shape) > 1:
                    src = src.rearrange("a b -> (a b)")
                act.dma_start(prow[PROW[name]:PROW[name] + n, :], src.rearrange("(r c) -> r c", c=P))\
                    .then_inc(sem("params_in"), 16)
            act_f = nc.scalar.activation

            def evacuate(stage, count, dst, func=ACT.Copy, dyn=4):
                def one(n, i, m):
                    s = slot(stage, n)
                    act.wait_ge(block_in, FIRST[stage] + n + 1 + m)
                    d = dst(n, i)
                    act_f(d[:, 0:TH] if len(d.shape) == 2 else d[:, :, 0:TH], bankA(s, TH), func)
                    act_f(d[:, TH:T] if len(d.shape) == 2 else d[:, :, TH:T], bankB(s, TH), func)\
                        .then_inc(out_of["scalar"], 1)
                loops = count // 4
                if loops > 1:
                    with act.Fori(0, loops) as i:
                        for n in range(4):
                            one(n, i, i * 4)
                else:
                    for n in range(count):
                        one(n, None, 0)

            def norm(k):
                for f in range(KD):
                    wait_emptied(act, FIRST[("x", "out0", "down0", "out1", "down1")[k]] + f + 1)
                    act_f((big if k == 1 else xn)[:, f, :], h[:, f, :], ACT.Square).then_inc(sem("sq_ready"), 1)
                root(f"norm{k}", 0, DM, rstd[:, :], "rms_ready")

            def root(stage, j, width, dst, signal):
                s = slot(stage, j)
                act.wait_ge(block_in, FIRST[stage] + j + 1)
                act_f(dst[:, 0:TH], bankA(s, TH), ACT.Sqrt, bias=EPS, scale=1.0 / width).then_inc(sem(signal), 1)
                act_f(dst[:, TH:T], bankB(s, TH), ACT.Sqrt, bias=EPS, scale=1.0 / width).then_inc(out_of["scalar"], 1)

            norm(0)
            evacuate("in0", 20, lambda n, i: big[:, n, :] if i is None else big[:, bass.ds(i * 4 + n, 1), :])

            act.wait_ge(sem("negabs_ready"), 1)
            own(act_f(z[2], z[1], ACT.Exp))
            act_f(z[1], z[2], ACT.Ln, bias=1.0).then_inc(sem("log1p_ready"), 1)
            for n in range(H):
                s = slot("sfxT", n)
                act.wait_ge(block_in, FIRST["sfxT"] + n + 1)
                act_f(lT[:, :, n, :], bankA(s, 2 * P).rearrange("p (a g) -> p a g", a=2), ACT.Copy)
                act_f(lcT[:, :, n, :], bankB(s, 2 * P).rearrange("p (a g) -> p a g", a=2), ACT.Copy)\
                    .then_inc(out_of["scalar"], 1)
            to = sfx.rearrange("p (a g h) -> p a h g", a=2, h=H)
            for n in range(6):
                s = slot("sfx", n)
                act.wait_ge(block_in, FIRST["sfx"] + n + 1)
                act_f(to[:, n // 3, n % 3 * 4:n % 3 * 4 + 4, :], bankA(s).rearrange("p (h g) -> p h g", h=4), ACT.Copy)\
                    .then_inc(out_of["scalar"], 1)

            s = slot("cum")
            act.wait_ge(block_in, FIRST["cum"] + 1)
            act_f(cumT[:, 0:SEQ], bankA(s, rows=H), ACT.Copy)
            act_f(cumT[:, SEQ:T], bankB(s, rows=H), ACT.Copy)
            act.wait_ge(sem("xn_ready"), KD)
            act_f(ngate, bankA(s, rows=H), ACT.Copy, scale=-1.0).then_inc(out_of["scalar"], 1)
            wait_emptied(act, FIRST["cum"] + 1)
            act.sem_inc(sem("ngate_ready"), 1)
            s = slot("cumT")
            act.wait_ge(block_in, FIRST["cumT"] + 1)
            act_f(cumn[:, 0:NT * H], bankA(s, NT * H), ACT.Copy)
            act_f(cumn[0:TS, NT * H:(NT + 1) * H], bankB(s, H, TS), ACT.Copy).then_inc(out_of["scalar"], 1)
            def queries(hd):
                if hd >= 2:
                    act.wait_ge(sem("scores_made"), NT * (hd - 1))
                r = slice(64 * (hd % 2), 64 * (hd % 2) + 64)
                act_f(qz[r, hd % 2, :], big[r, EV_Q + hd // 2, 0:SEQ], ACT.Copy, scale=D ** -0.5)
                act_f(kz[hd % 2][r, :], big[r, EV_K + hd // 2, 0:SEQ], ACT.Copy).then_inc(sem("keys_in"), 1)

            NSTEP = H * NT
            act.wait_ge(sem("qz_zeroed"), 1)
            act.wait_ge(sem("kz_zeroed"), 1)
            queries(0)
            act.wait_ge(sem("k_stored"), 80)
            for n in range(NSTEP + 4):
                if n < NSTEP:
                    hd, i = n // NT, n % NT
                    if i == 1 and hd + 1 < H:
                        queries(hd + 1)
                    act.wait_ge(sem("shift_ready"), n + 1)
                    if n >= 4:
                        act.wait_ge(sem("probs_turned"), n - 3)
                    w = (i + 1) * P
                    act_f(eb[:, n % 4, 0:w], ps[:, (0, 1, 2, 7)[n % 4], 0:w], ACT.Exp,
                          bias=hstat[:, 8 + n % 4:9 + n % 4], accum_out=hstat[:, 12 + n % 4:13 + n % 4])\
                        .then_inc(sem("probs_made"), 1)
                if n >= 4:
                    m = n - 4
                    hd, i = m // NT, m % NT
                    act.wait_ge(sem("probs_turned"), m + 1)
                    if hd >= 2:
                        act.wait_ge(sem("fox_prompt_out"), hd - 1)
                    act_f(pT[:, hd % 2, 0:i + 1, i * P:(i + 1) * P],
                          ps[:, 3 + m % 3, 0:(i + 1) * P].rearrange("p (j q) -> p j q", j=i + 1), ACT.Copy)\
                        .then_inc(sem("probs_turned_copied"), 1)

            def copy_page(b, p):
                k = b * PAGES + p
                act.wait_ge(sem("k_page_used"), k + 1)
                quad = b * GROUPS + p // GROUP
                if p % GROUP == 0 and (not isinstance(b, int) or quad >= 2):
                    act.wait_ge(sem("groups_scored"), quad - 1)
                at = p % GROUP * PAGE
                act_f(kT[:, p // GROUP % 2, 0:4, at:at + PAGE],
                      ps[:, 2 * (p % 2), :].rearrange("p (f n) -> p f n", f=4), ACT.Copy).then_inc(sem("kT_low"), 1)

            def exps(b, c):
                act.wait_ge(sem("softmax_shift"), b + 1)
                n = 2 * GROUP * PAGE
                part = S[:, c * n:(c + 1) * n] if c < EXPS else S[:, c * n:c * n + TS]
                act_f(part, part, ACT.Exp, bias=sshift, accum_out=ssum[:, c:c + 1]).then_inc(sem("exp_done"), 1)

            def k_pages(b, soft):
                for p in range(PAGES):
                    copy_page(b, p)
                    if soft is not None and 1 <= p <= EXPS:
                        exps(soft, p - 1)
                        if p == EXPS:
                            exps(soft, EXPS)

            k_pages(0, None)
            k_pages(1, 0)
            with act.Fori(2, NB) as c:
                k_pages(c, c - 1)
            for c in range(EXPS + 1):
                exps(NB - 1, c)

            norm(1)
            def mlp(stage):
                with act.Fori(0, 8) as i:
                    for n in range(4):
                        s = slot(stage, n)
                        act.wait_ge(block_in, FIRST[stage] + n + 1 + i * 4)
                        act_f(big[:, bass.ds(i * 4 + n, 1), 0:TH], bankA(s, TH), ACT.Relu)
                        act_f(big[:, bass.ds(i * 4 + n, 1), TH:T], bankB(s, TH), ACT.Relu).then_inc(out_of["scalar"], 1)
            act.wait_ge(sem("stored"), 64)
            mlp("up0")
            norm(2)

            def take_block(n, dst, scale=1.0):
                s = n % 4
                act.wait_ge(block_in, n + 1)
                act_f(dst[:, 0:TH], bankA(s, TH), ACT.Copy, scale=scale)
                act_f(dst[:, TH:T], bankB(s, TH), ACT.Copy, scale=scale).then_inc(out_of["scalar"], 1)

            for m in range(4):
                take_block(FIRST["in1"] + m, big[:, OD_RG + m, :])
            wait_emptied(act, FIRST["in1"] + 4)
            for m in range(R):
                act_f(swish[:, m, :], big[:, OD_RG + m, :], ACT.Exp, scale=-1.0).then_inc(sem("gate_exp"), 1)
            for m in range(4):
                take_block(FIRST["in1"] + 4 + m, big[:, OD_GV + m, :])
            for m in range(4):
                take_block(FIRST["rq"] + m, big[:, OD_RQ + m, :])
            take_block(FIRST["mu"], rstd, 1.0 / 512)
            for f in range(4):
                act.wait_ge(sem("centred"), f + 1)
                act_f(lnsq[:, f, :], big[:, OD_GV + f, :], ACT.Square).then_inc(sem("lnsq_ready"), 1)
            for m in range(4):
                take_block(FIRST["rk_a"] + m if m < 2 else FIRST["rk_b"] + m - 2, big[:, OD_RK + m, :])
            root("var", 0, 512, rstd[:, :], "ln_root")
            for m in range(4):
                take_block(FIRST["rv_a"] + m if m < 2 else FIRST["rv_b"] + m - 2, big[:, OD_RV + m, :])
            act.wait_ge(sem("swish_ready"), R)
            for t in range(NT + 1):
                s = slot("vn", t)
                rows = P if t < NT else TS
                act.wait_ge(block_in, FIRST["vn"] + t + 1)
                act_f(v2[0:rows, t, :], bankA(s, rows=rows), ACT.Copy).then_inc(out_of["scalar"], 1)

            def head_mean(n):
                take_block(FIRST[f"hmu_{n}"], big[:, OD_RV + n, :], 1.0 / DR)
                act.wait_ge(sem("hcentred"), n + 1)
                act_f(big[:, OD_RK + n, :], big[:, OD_RQ + n, :], ACT.Square).then_inc(sem("hsq_ready"), 1)

            for n in range(R):
                if n:
                    head_mean(n - 1)
                out = FIRST[f"ret_out_{n}"]
                act.wait_ge(block_in, out + 1)
                act_f(big[:, OD_RQ + n, 0:SEQ], bankA(out % 4), ACT.Copy)
                act_f(big[:, OD_RQ + n, SEQ:T], bankB(out % 4), ACT.Copy).then_inc(out_of["scalar"], 1)
                if n:
                    root(f"hvar_{n - 1}", 0, DR, big[:, OD_RV + n - 1, :], "hroot_a")
            head_mean(R - 1)
            root(f"hvar_{R - 1}", 0, DR, big[:, OD_RV + R - 1, :], "hroot_a")
            norm(3)
            act.wait_ge(sem("ret_stored"), 32 * R)
            mlp("up1")
            for f in range(KD):
                act.wait_ge(sem("raw_rows"), f + 1)
                for t in range(NT + 1):
                    r = P if t < NT else TS
                    last = act_f(raw[0:r, f, t, :], raw[0:r, f, t, :], ACT.Square, accum_out=sumsq[0:r, t, f:f + 1])
                last.then_inc(sem("row_squares"), 1)
            act.wait_ge(sem("row_sums"), 1)
            act_f(ssq, ssq, ACT.Sqrt, bias=EPS, scale=1.0 / DM).then_inc(sem("row_roots"), 1)
            act.wait_ge(sem("row_scales"), 1)
            for t in range(1, NT + 1, 2):
                act_f(yrow[:, t, :], yrow[:, t, :], ACT.Copy, scale=ssq[:, t:t + 1])\
                    .then_inc(sem("rows_scaled_by_scalar"), 1)

        @blk.vector
        def _(dve):
            own = Steps(dve, sem("dve_steps"))
            tt, stt, ts = nc.vector.tensor_tensor, nc.vector.scalar_tensor_tensor, nc.vector.tensor_scalar
            cp = nc.vector.tensor_copy

            def drained(stage, n):
                dve.wait_ge(block_in, FIRST[stage] + n + 1)
                return slot(stage, n)

            def norm(k, row):
                wait_emptied(dve, FIRST[f"norm{k}"] + 1)
                own(nc.vector.reciprocal(rstd[:, :], rstd[:, :]))
                for f in range(KD):
                    stt(xn[:, f, :], h[:, f, :], pcol[:, row + f:row + f + 1], rstd[:, :], ALU.mult, ALU.mult)\
                        .then_inc(sem("xn_ready"), 1)

            def residual(stage):
                for n in range(KD):
                    s = drained(stage, n)
                    tt(h[:, n, 0:TH], bankA(s, TH), h[:, n, 0:TH], ALU.add)
                    tt(h[:, n, TH:T], bankB(s, TH), h[:, n, TH:T], ALU.add).then_inc(out_of["vector"], 1)

            def squares(stage, base):
                with dve.Fori(0, 8) as i:
                    for n in range(4):
                        dve.wait_ge(out_of["scalar"], emptied_by("scalar", FIRST[stage]) + n + 1 + i * 4)
                        u = big[:, bass.ds(i * 4 + n, 1), :]
                        tt(u, u, u, ALU.mult).then_inc(sem("u_ready"), 1)

            for f in range(KD):
                s = drained("x", f)
                cp(h[:, f, 0:SEQ], bankA(s))
                cp(h[:, f, SEQ:T], bankB(s)).then_inc(out_of["vector"], 1)
            dve.wait_ge(sem("params_turned"), 1)
            cp(pcol[:, :], ps[:, 7, 0:NPARAM]).then_inc(sem("params_ready"), 1)
            dve.wait_ge(sem("params_ready"), 1)
            norm(0, PROW["norm_mix"])

            s = drained("logf", 0)
            dve.wait_ge(sem("wf_in"), 32)
            ts(z[0][:, 0:TH], bankA(s, TH, H), bf[:, 0:1], None, ALU.add)
            ts(z[0][:, TH:T], bankB(s, TH, H), bf[:, 0:1], None, ALU.add).then_inc(out_of["vector"], 1)
            wait_emptied(dve, FIRST["logf"] + 1)
            own(ts(z[2], z[0], -1.0, None, ALU.mult))
            tt(z[1], z[2], z[0], ALU.min).then_inc(sem("negabs_ready"), 1)
            own(ts(z[0], z[0], 0.0, None, ALU.min))
            dve.wait_ge(sem("log1p_ready"), 1)
            tt(z[3], z[0], z[1], ALU.subtract).then_inc(sem("logf_ready"), 1)
            s = drained("logfT", 0)
            cp(lfn[:, 0:NT * H], bankA(s, NT * H))
            cp(lfn[0:TS, NT * H:(NT + 1) * H], bankB(s, H, TS)).then_inc(out_of["vector"], 1)
            wait_emptied(dve, FIRST["logfT"] + 1)
            dve.sem_inc(sem("lfn_ready"), 1)

            nc.vector.memset(vs, 0.0)
            nc.vector.memset(kz[0], 0.0).then_inc(sem("kz_zeroed"), 1)
            own(nc.vector.memset(bigf[:, at0 + 3840:at0 + 5376], 0.0))
            cp(knew, big[:, EV_K:EV_K + HB, SEQ:T])
            for a in range(2):
                r = slice(64 * a, 64 * a + 64)
                for c in range(2):
                    at = 16 * c + 8 * a
                    dst = qall[r, :, :, at:at + NS].rearrange("p b (j c) s -> p c j b s", c=2)[:, c]
                    src = big[r, EV_Q:EV_Q + HB, SEQ:T].rearrange("p (j c) (b s) -> p c j b s", c=2, b=NB)[:, c]
                    ins = ts(dst, src, D ** -0.5, None, ALU.mult)
                ins.then_inc(sem("queries_placed"), 1)

            def rows(stage, dst, before=None):
                for t in range(NT + 1):
                    if before:
                        before(t)
                    s = drained(stage, t)
                    r = P if t < NT else TS
                    d = dst(t)
                    cp(d[0:r, 0:512], bankA(s, rows=r))
                    cp(d[0:r, 512:FOX], bankB(s, FOX - 512, r)).then_inc(out_of["vector"], 1)

            def stage_free(t):
                if t == 0:
                    wait_emptied(dve, FIRST["sfx"] + 6)

            rows("knat", lambda t: kstage[:, t, :], stage_free)
            rows("vnat", lambda t: vn0[:, t, :] if t < NT else vs)
            for a in range(2):
                s = drained("hist", a)
                cp(es[0][:, a, :, 0:HIST], ps[:, 2 * s, 0:NB * HIST].rearrange("p (b t) -> p b t", b=NB))\
                    .then_inc(out_of["vector"], 1)
            wait_emptied(dve, FIRST["hist"] + 2)
            for a in range(2):
                own(cp(es[0][:, a, :, HIST:HIST + NS], big[:, a, SEQ:T].rearrange("p (b s) -> p b s", b=NB)))
                cp(hcopy[:, a, :].rearrange("p (b t) -> p b t", b=NB), es[0][:, a, :, NS:NS + HIST])\
                    .then_inc(sem("ext_s_ready"), 1)
            dve.wait_ge(sem("ext_s_ready"), 2)
            dve.sem_inc(sem("hist_copied"), 1)
            s = drained("g96", 0)
            gates = ps[0:HQ, 2 * s, 0:TS]
            tt(key_bias, cst("mask_new"), gates, ALU.subtract)
            tt(ostage[:, 0:TS], gates, cst("own_query"), ALU.mult).then_inc(out_of["vector"], 1)
            wait_emptied(dve, FIRST["g96"] + 1)
            nc.vector.reduce_sum(qgate, ostage[:, 0:TS].rearrange("p (b s) -> p b s", b=NB), AX.X)
            nmax, shift, den, rec = (hstat[:, 4 * n:4 * n + 4] for n in (0, 2, 3, 4))

            def maximum(n):
                hd, i = n // NT, n % NT
                c, w = n % 4, (i + 1) * P
                dve.wait_ge(sem("scores_made"), n + 1)
                if n >= 4:
                    dve.wait_ge(sem("probs_made"), n - 3)
                own(nc.vector.reduce_max(nmax[:, c:c + 1], ps[:, (0, 1, 2, 7)[c], 0:w], AX.X, negate=True))
                g = cumn[:, i * H + hd:i * H + hd + 1]
                stt(shift[:, c:c + 1], nmax[:, c:c + 1], g, g, ALU.subtract, ALU.add).then_inc(sem("shift_ready"), 1)

            def divisors(n):
                c = n % 4
                dve.wait_ge(sem("probs_made"), n + 1)
                if n >= 4:
                    dve.wait_ge(sem("probs_turned"), n - 3)
                own(nc.vector.reciprocal(rec[:, c:c + 1], den[:, c:c + 1]))
                ts(diag[:, c, :], ident, rec[:, c:c + 1], None, ALU.mult).then_inc(sem("diag_ready"), 1)

            def head_out(hd):
                r = slice(64 * (hd % 2), 64 * (hd % 2) + 64)
                dve.wait_ge(sem("fox_prompt_out"), hd + 1)
                cp(xn[r, 2 + hd // 2, 0:SEQ], ps[r, 6, :]).then_inc(sem("fox_prompt_done"), 1)

            NSTEP = H * NT
            for n in range(NSTEP + 6):
                if n < NSTEP:
                    maximum(n)
                if 2 <= n < NSTEP + 2:
                    divisors(n - 2)
                if n >= 6 and (n - 6) % NT == NT - 1:
                    head_out((n - 6) // NT)

            dve.wait_ge(sem("hist_turned"), 1)
            for a in range(2):
                cp(hout[:, a * P:(a + 1) * P], ps[0:NB * HIST, a, 0:P])
                own(cp(hout_p[:, a * P:(a + 1) * P], ps[0:HIST, a, P:2 * P]))
            dve.sem_inc(sem("hist_out_ready"), 1)

            dve.wait_ge(sem("pooled"), 1)
            for a in range(2):
                ts(xn[:, a, 0:SEQ], ps[:, 4 + a, :], param("pool_scale", a), None, ALU.mult)
                own(ts(xn[:, a, SEQ:T], ps[:, 6 + a, 0:TS], param("pool_scale", a), None, ALU.mult))
            dve.sem_inc(sem("pool_mixed"), 1)

            def at(x, b, n=1):
                return x[:, b:b + n] if isinstance(b, int) else x[:, bass.ds(b, n)]

            def stage_queries(b):
                if not isinstance(b, int) or b >= 1:
                    dve.wait_ge(sem("new_scored"), b)
                q = qall[:, b] if isinstance(b, int) else qall[:, bass.ds(b, 1)].rearrange("p o f c -> p (o f) c")
                cp(qcur, q).then_inc(sem("queries_staged"), 1)

            def stage_suffix(b, g):
                if not isinstance(b, int) or b * GROUPS + g >= 2:
                    dve.wait_ge(sem("groups_scored"), b * GROUPS + g - 1)
                n = GROUP * H
                lo = b * (PAGES * H) + g * n
                src = sfx[:, lo:lo + n] if isinstance(b, int) else sfx[:, bass.ds(lo, n)]
                cp(sgate[:, g % 2, :].rearrange("p (n s) -> p n s", s=NS),
                   src.rearrange("p (n o) -> p n o", o=1).broadcast_to([P, n, NS])).then_inc(sem("suffix_staged"), 1)

            def copy_page(b, p):
                k = b * PAGES + p
                dve.wait_ge(sem("k_page_used"), k + 1)
                quad = b * GROUPS + p // GROUP
                if p % GROUP == 0 and (not isinstance(b, int) or quad >= 2):
                    dve.wait_ge(sem("groups_scored"), quad - 1)
                at = p % GROUP * PAGE
                cp(kT[:, p // GROUP % 2, 4:HB, at:at + PAGE],
                   ps[:, 2 * (p % 2) + 1, 0:2 * PAGE].rearrange("p (f n) -> p f n", f=2)).then_inc(sem("kT_high"), 1)

            def take_scores(b, g):
                dve.wait_ge(sem("groups_scored"), b * GROUPS + g + 1)
                if not isinstance(b, int) or b >= 1:
                    dve.wait_ge(sem("probs_turned_s"), (b - 1) * (GROUPS + 1) + g + 1)
                n = GROUP * PAGE
                cp(S[:, g * n:(g + 1) * n], ps[0:HQ, 4 + g % 2, :])
                nc.vector.reduce_max(smax[:, g:g + 1], ps[0:HQ, 4 + g % 2, :], AX.X).then_inc(sem("scores_in"), 1)

            def take_new(b):
                dve.wait_ge(sem("new_scored"), b + 1)
                if not isinstance(b, int) or b >= 1:
                    dve.wait_ge(sem("probs_turned_s"), b * (GROUPS + 1))
                new = S[:, PAGES * PAGE:PAGES * PAGE + TS]
                own(tt(new, ps[0:HQ, 4, 0:TS], key_bias, ALU.add))
                start = (NB - 1 - b) * NS if isinstance(b, int) else b * (-NS) + (NB - 1) * NS
                window = cst("mask_seq", start, start + TS) if isinstance(b, int) else \
                    cst("mask_seq")[:, bass.ds(start, TS)]
                own(tt(new, new, window, ALU.add))
                nc.vector.reduce_max(smax[:, GROUPS:GROUPS + 1], new, AX.X).then_inc(sem("scores_in"), 1)

            def softmax_shift(b):
                dve.wait_ge(sem("scores_in"), (b + 1) * (GROUPS + 1))
                own(nc.vector.reduce_max(gmax, smax, AX.X))
                g = qgate[:, b:b + 1] if isinstance(b, int) else qgate[:, bass.ds(b, 1)]
                own(tt(gfull, gmax, g, ALU.add))
                tt(sshift, g, gfull, ALU.subtract).then_inc(sem("softmax_shift"), 1)

            def take_probs(b, g):
                dve.wait_ge(sem("probs_turned_s"), b * (GROUPS + 1) + g + 1)
                if not isinstance(b, int) or b >= 1:
                    if g < GROUPS:
                        dve.wait_ge(sem("v_page_used"), (b - 1) * PAGES + (g + 1) * GROUP)
                    else:
                        dve.wait_ge(sem("fox_sample_out"), b)
                if g == GROUPS:
                    ins = cp(pTs[0:TS, PAGES, :], ps[0:TS, 6, 0:HQ])
                else:
                    ins = cp(pTs[:, g * GROUP:(g + 1) * GROUP, :],
                             ps[:, 6, 0:GROUP * HQ].rearrange("p (m c) -> p m c", m=GROUP))
                ins.then_inc(sem("probs_in"), 1)

            def denominators(b):
                dve.wait_ge(sem("exp_done"), (b + 1) * (EXPS + 1))
                own(nc.vector.reduce_sum(sden, ssum, AX.X))
                own(nc.vector.reciprocal(srec, sden))

            def scale_out(b):
                dve.wait_ge(sem("fox_sample_out"), b + 1)
                ts(ostage, ps[0:HQ, 7, 0:256], srec, None, ALU.mult).then_inc(sem("out_scaled"), 1)

            def place_out(b):
                dve.wait_ge(sem("out_turned"), b + 1)
                for a in range(2):
                    r = slice(64 * a, 64 * a + 64)
                    for c in range(2):
                        src = ps[r, 6, c * HQ:(c + 1) * HQ].rearrange("p (j s) -> p j s", j=JT)
                        src = src[:, :, 16 * c + 8 * a:16 * c + 8 * a + NS]
                        rows = xn[r, 2:KD, :].rearrange("p (j c) t -> p c j t", c=2)[:, c]
                        dst = rows[:, :, SEQ + b * NS:SEQ + (b + 1) * NS] if isinstance(b, int) else \
                            rows[:, :, bass.ds(b * NS + SEQ, NS)]
                        ins = cp(dst, src)
                ins.then_inc(sem("outputs_placed"), 1)

            def phase(c, k=True, ending=True, starting=True):
                if starting:
                    softmax_shift(c - 1)
                if k:
                    stage_queries(c)
                for p in range(PAGES):
                    if ending and p == LAG:
                        scale_out(c - 2)
                    if k:
                        copy_page(c, p)
                        if p % GROUP == 2:
                            stage_suffix(c, p // GROUP)
                        if p > GROUP and p % GROUP == 1:
                            take_scores(c, p // GROUP - 1)
                    if starting and 3 <= p < 3 + GROUPS + 1:
                        take_probs(c - 1, p - 3)
                    if starting and p == 13:
                        denominators(c - 1)
                    if ending and p == 14:
                        place_out(c - 2)
                if starting and not ending:
                    dve.sem_inc(sem("outputs_placed"), 1)
                if k:
                    take_scores(c, GROUPS - 1)
                    take_new(c)

            own(nc.vector.memset(pTs[:, PAGES, :], 0.0))
            phase(0, ending=False, starting=False)
            phase(1, ending=False)
            with dve.Fori(2, NB) as c:
                own.loop(c - 2, 6)
                phase(c)
            own.end(NB - 2)
            phase(NB, k=False)
            scale_out(NB - 1)
            place_out(NB - 1)

            residual("out0")
            norm(1, PROW["norm_ffn"])
            squares("up0", 0)
            residual("down0")

            norm(2, PROW["norm_mix"] + KD)
            for n in range(R):
                dve.wait_ge(sem("gate_exp"), n + 1)
                e, g = swish[:, n, :], big[:, OD_RG + n, :]
                own(ts(e, e, 1.0, None, ALU.add))
                own(nc.vector.reciprocal(e, e))
                tt(g, g, e, ALU.mult).then_inc(sem("swish_ready"), 1)
            s = drained("wst", 0)
            low = cst("upto", 0, P).rearrange("p (o t) -> p o t", o=1).broadcast_to([P, 4, P])
            tt(wT, bankA(s).rearrange("p (g t) -> p g t", g=4), low, ALU.mult).then_inc(out_of["vector"], 1)
            s = drained("w8", 0)
            corner = ps[0:TS, 2 * s, 0:4 * NS].rearrange("p (g t) -> p g t", g=4)
            for g in range(4):
                last = tt(w8[:, g, :].rearrange("p (b t) -> p b t", b=NB),
                          corner[:, g:g + 1, :].broadcast_to([TS, NB, NS]),
                          cst1("same_s").rearrange("p (b t) -> p b t", b=NB), ALU.mult)
            last.then_inc(out_of["vector"], 1)
            wait_emptied(dve, FIRST["mu"] + 1)
            for f in range(4):
                g = big[:, OD_GV + f, :]
                tt(g, g, rstd[:, :], ALU.subtract).then_inc(sem("centred"), 1)

            def rotate(stage, first, done, sc):
                for n in range(R):
                    x = big[:, first + n, :]
                    s = drained(stage, n)
                    if done + n:
                        dve.wait_ge(sem("rotated"), done + n)
                    stt(tmp[:, 0:TH], bankA(s, TH), sc, cst1("sin", 0, TH), ALU.mult, ALU.mult)
                    stt(tmp[:, TH:T], bankB(s, TH), sc, cst1("sin", TH, T), ALU.mult, ALU.mult)\
                        .then_inc(out_of["vector"], 1)
                    own(stt(x, x, sc, cst1("cos"), ALU.mult, ALU.mult))
                    tt(x, x, tmp, ALU.add).then_inc(sem("rotated"), 1)

            rotate("rot_q", OD_RQ, 0, 1.0)
            wait_emptied(dve, FIRST["var"] + 1)
            own(nc.vector.reciprocal(rstd[:, :], rstd[:, :]))
            for f in range(4):
                g = big[:, OD_GV + f, :]
                own(stt(g, g, param("gmlp_ln_g", f), rstd[:, :], ALU.mult, ALU.mult))
                ts(g, g, param("gmlp_ln_b", f), None, ALU.add).then_inc(sem("ln_ready"), 1)
            rotate("rot_k", OD_RK, R, DR ** -0.5)
            for t in range(NT + 1):
                s = drained("vnat1", t)
                r = P if t < NT else TS
                cp(vnn[0:r, t, :], bankA(s, rows=r)).then_inc(out_of["vector"], 1)
            for g in range(4):
                s = drained("z", g)
                cp(big[:, OD_GV + g, 0:SEQ], bankA(s))
                cp(big[:, OD_GV + g, SEQ:T], bankB(s)).then_inc(out_of["vector"], 1)
            for t in range(NT + 1):
                s = drained("kn", t)
                r = P if t < NT else TS
                dk = cst1("dec_k" if t < NT else "dec_ks").rearrange("p (h o) -> p h o", o=1).broadcast_to([r, R, P])
                tt(kn[0:r, t, :].rearrange("p (h d) -> p h d", h=R),
                   bankA(s, rows=r).rearrange("p (h d) -> p h d", h=R), dk, ALU.mult).then_inc(out_of["vector"], 1)
            wait_emptied(dve, FIRST["vn"] + NT + 1)
            dve.wait_ge(sem("gv_stored"), 16)

            def centre_head(n):
                o, mu = big[:, OD_RQ + n, :], big[:, OD_RV + n, :]
                wait_emptied(dve, FIRST[f"hmu_{n}"] + 1)
                tt(o, o, mu, ALU.subtract).then_inc(sem("hcentred"), 1)

            def finish_head(n):
                o, rs = big[:, OD_RQ + n, :], big[:, OD_RV + n, :]
                wait_emptied(dve, FIRST[f"hvar_{n}"] + 1)
                own(nc.vector.reciprocal(rs, rs))
                own(stt(rs, rs, param("ret_gn_g", n), o, ALU.mult, ALU.mult))
                tt(o, rs, big[:, OD_RG + n, :], ALU.mult).then_inc(sem("head_mixed"), 1)

            for n in range(R):
                base = FIRST[f"ret_{n}"]
                cols = slice(n * P, (n + 1) * P)
                if n:
                    dve.wait_ge(block_in, FIRST[f"ret_{n - 1}"] + 3)
                vv = v2[0:TS, NT, cols].rearrange("p (o e) -> p o e", o=1).broadcast_to([TS, NB, P])
                mb = cst1("of_seq").rearrange("p (b o) -> p b o", o=1).broadcast_to([TS, NB, P])
                tt(vmask, vv, mb, ALU.mult).then_inc(sem("v_spread"), 1)
                s = drained(f"ret_{n}", 0)
                if n:
                    dve.wait_ge(block_in, FIRST[f"ret_out_{n - 1}"] + 1)
                dd = cst1("dec", n * P, (n + 1) * P).rearrange("p (o l) -> p o l", o=1).broadcast_to([P, NT, P])
                tt(sct[:, 0:SEQ].rearrange("p (t l) -> p t l", t=NT), bankA(s).rearrange("p (t l) -> p t l", t=NT),
                   dd, ALU.mult)
                tt(sct[0:TS, SEQ:T], bankB(s, rows=TS), cst1("dec_s", n * TS, (n + 1) * TS), ALU.mult)\
                    .then_inc(out_of["vector"], 1)
                q = big[:, OD_RQ + n, :]
                dq = cst1("dec_q", n * P, (n + 1) * P).rearrange("p (o l) -> p o l", o=1)
                qp = q[:, 0:SEQ].rearrange("p (t l) -> p t l", t=NT)
                tt(qp, qp, dq.broadcast_to([P, NT, P]), ALU.mult)
                qs = q[:, SEQ:T].rearrange("p (b l) -> p b l", b=NB)
                tt(qs, qs, dq[:, :, 0:NS].broadcast_to([P, NB, NS]), ALU.mult).then_inc(sem("q_decayed"), 1)
                s = drained(f"ret_{n}", 1)
                if n:
                    dve.wait_ge(sem("ret_stored"), 32 * n)
                own(cp(st[:, 0, :], ps[:, 2 * s, 0:P]))
                for t in range(1, NT):
                    ins = stt(st[:, t, :], st[:, t - 1, :], decay_step[0][n], ps[:, 2 * s, t * P:(t + 1) * P],
                              ALU.mult, ALU.add)
                    if t < NT - 1:
                        own(ins)
                ins.then_inc(out_of["vector"], 1)
                wait_emptied(dve, base + 2)
                dve.sem_inc(sem("states_ready"), 1)
                s = drained(f"ret_{n}", 2)
                for a in range(2):
                    ins = stt(s_out[:, 4 * a:4 * a + 4, :].rearrange("p b e -> p (b e)"),
                              s0[:, n, 4 * a:4 * a + 4, :].rearrange("p b e -> p (b e)"), decay_step[1][n],
                              ps[:, 2 * s + a, :], ALU.mult, ALU.add)
                ins.then_inc(out_of["vector"], 1)
                wait_emptied(dve, base + 3)
                dve.sem_inc(sem("ret_state_ready"), 1)
                if n:
                    centre_head(n - 1)
                if n >= 2:
                    finish_head(n - 2)
                s = drained(f"u_{n}", 0)
                tt(big[:, OD_U + n, 0:TH], bankA(s, TH), big[:, OD_GV + n, 0:TH], ALU.mult)
                tt(big[:, OD_U + n, TH:T], bankB(s, TH), big[:, OD_GV + n, TH:T], ALU.mult)\
                    .then_inc(out_of["vector"], 1)
            finish_head(R - 2)
            centre_head(R - 1)
            finish_head(R - 1)
            residual("out1")
            norm(3, PROW["norm_ffn"] + KD)
            squares("up1", 32)
            def take_rows(f):
                dve.wait_ge(block_in, rows_block(f) + 1)
                s = rows_block(f) % 4
                g = gain[:, f * P:(f + 1) * P].rearrange("p (o n) -> p o n", o=1)
                a = bankA(s).rearrange("p (t n) -> p t n", t=NT)
                cp(raw[:, f, 0:NT, :], a)
                cp(raw[0:TS, f, NT, :], bankB(s, P, TS)).then_inc(sem("raw_rows"), 1)
                tt(yrow[:, 0:NT, f * P:(f + 1) * P], a, g.broadcast_to([P, NT, P]), ALU.mult)
                tt(yrow[0:TS, NT, f * P:(f + 1) * P], bankB(s, P, TS), g[0:TS, 0, :], ALU.mult)\
                    .then_inc(out_of["vector"], 1)

            dve.wait_ge(sem("gain_in"), 16)
            own(nc.vector.memset(sumsq, 0.0))
            for f in range(KD):
                dve.wait_ge(block_in, down_block(f) + 1)
                s = down_block(f) % 4
                tt(hlast[:, f % 2, 0:TH], bankA(s, TH), h[:, f, 0:TH], ALU.add)
                tt(hlast[:, f % 2, TH:T], bankB(s, TH), h[:, f, TH:T], ALU.add).then_inc(out_of["vector"], 1)
                if f:
                    take_rows(f - 1)
            take_rows(KD - 1)
            dve.wait_ge(sem("row_squares"), KD)
            nc.vector.reduce_sum(ssq, sumsq, AX.X).then_inc(sem("row_sums"), 1)
            dve.wait_ge(sem("row_roots"), 1)
            nc.vector.reciprocal(ssq, ssq).then_inc(sem("row_scales"), 1)
            dve.wait_ge(sem("row_scales"), 1)
            for t in range(0, NT + 1, 2):
                r = P if t < NT else TS
                ts(yrow[0:r, t, :], yrow[0:r, t, :], ssq[0:r, t:t + 1], None, ALU.mult)\
                    .then_inc(sem("rows_scaled_by_vector"), 1)


_INS = ['x_prompt', 'x_sample', 'state_pool', 'cache_k', 'cache_v', 'cache_logf', 'page_table', 'state_ret', 'norm_mix',
        'w_in_even', 'b_forget', 'pool_w', 'pool_scale', 'w_out_even', 'w_in_odd', 'gmlp_ln_g', 'gmlp_ln_b', 'gmlp_ws',
        'gmlp_bs', 'ret_gn_g', 'w_out_odd', 'norm_ffn', 'w_up', 'w_down', 'norm_final']
_OUTS = [("y_prompt", (1, 512, 1024)), ("y_sample", (8, 8, 1024)), ("pool_prompt", (1, 1, 15, 256)),
         ("k_prompt", (1, 1, 512, 12, 64)), ("v_prompt", (1, 1, 512, 12, 64)), ("logf_prompt", (1, 1, 512, 12)),
         ("ret_prompt", (1, 1, 4, 128, 128)), ("pool_sample", (1, 8, 15, 256)), ("k_sample", (1, 8, 8, 12, 64)),
         ("v_sample", (1, 8, 8, 12, 64)), ("logf_sample", (1, 8, 8, 12)), ("gmlp_v_sample", (1, 8, 8, 512)),
         ("ret_sample", (1, 8, 4, 128, 128))]


def kernel(**inputs):
    import numpy as _np
    import concourse.bacc as _bacc
    from concourse import mybir as _mybir
    from concourse.bass_utils import run_bass_kernel_spmd as _run

    nc = _bacc.Bacc("TRN2", target_bir_lowering=False, num_devices=1)
    (tab0, where0), (tab1, where1), step = tables()
    arrays, ins, outs = {}, {}, {}
    for name in _INS:
        arrays[f"in_{name}"] = _np.ascontiguousarray(inputs[name])
    arrays["in_tab0"], arrays["in_tab1"] = tab0, tab1
    for name, a in arrays.items():
        ins[name[3:]] = nc.dram_tensor(name, a.shape, _mybir.dt.from_np(a.dtype), kind="ExternalInput").ap()
    for name, shape in _OUTS:
        outs[name] = nc.dram_tensor(f"out_{name}", shape, _mybir.dt.float32, kind="ExternalOutput").ap()
    hybrid_step(nc, ins, outs, where0, where1, step)
    r = _run(nc, [arrays], core_ids=[0])
    return tuple(r.results[0][f"out_{name}"] for name, _ in _OUTS)
```
